# Optimizing a Trainium2 kernel written in Bass

```python
import jax, jax.numpy as jnp
from jax import lax
import numpy as np

D_MODEL = 1024
BATCH = 1
SEQ = 1024
DEPTH = 1

CTX_LEN = 256
GRID_W = 64
D_MIX = D_MODEL
GLA_WIDTH = D_MIX // 2
CONV_WIDTH = D_MIX // 4
POOL_WIDTH = D_MIX - GLA_WIDTH - CONV_WIDTH
GLA_HEADS = 4
GLA_DV = GLA_WIDTH // GLA_HEADS
GLA_DK = GLA_DV // 2
GLA_KEY_WIDTH = GLA_HEADS * GLA_DK
GATE_RANK = 16
GATE_TAU = 16.0
CHUNK = 64
CONV_K = 3
CONV_HEADS = 4
POOL_WINDOWS = (2, 4, 8, 16)
POOL_GROUP = POOL_WIDTH // len(POOL_WINDOWS)
D_FF = 4 * D_MODEL
N_MOD = 6
EPS = 1e-6

Q_OFF = 0
K_OFF = Q_OFF + GLA_KEY_WIDTH
V_OFF = K_OFF + GLA_KEY_WIDTH
G_OFF = V_OFF + GLA_WIDTH
R_OFF = G_OFF + 2 * GATE_RANK
CB_OFF = R_OFF + GLA_WIDTH
CC_OFF = CB_OFF + CONV_WIDTH
CH_OFF = CC_OFF + CONV_WIDTH
P_OFF = CH_OFF + CONV_WIDTH
IN_COLS = P_OFF + POOL_WIDTH

kernel_name = 'hybrid_gla_conv_pool_dit_trunk'

def rmsnorm(x, w):
    xf = x.astype(jnp.float32)
    y = xf * lax.rsqrt(jnp.mean(xf * xf, axis=-1, keepdims=True) + EPS)
    return (y * w.astype(jnp.float32)).astype(x.dtype)

def modulate(x, w, shift, scale):
    return rmsnorm(x, w) * (1 + scale) + shift

def adaln(cvec, w_mod, b_mod, n):
    m = jax.nn.silu(cvec) @ w_mod[:, : n * D_MODEL] + b_mod[: n * D_MODEL]
    return jnp.split(m, n, axis=-1)

def to_heads(t, h):
    b, n, w = t.shape
    return t.reshape(b, n, h, w // h).transpose(0, 2, 1, 3)

def rev(t):
    return jnp.flip(t, axis=2)

def gla_kvg(k_raw, v_raw, z_raw, gate_w, gate_b):
    k = to_heads(k_raw, GLA_HEADS).astype(jnp.float32)
    v = to_heads(v_raw, GLA_HEADS).astype(jnp.float32)
    gates = tuple(
        to_heads(jax.nn.log_sigmoid((z_raw[..., d * GATE_RANK:(d + 1) * GATE_RANK] @ gate_w[d]
                                     + gate_b[d]).astype(jnp.float32)) / GATE_TAU, GLA_HEADS)
        for d in range(2))
    return k, v, gates

def gla_chunked(q, k, v, g, s0):
    bsz, h, n, _ = q.shape
    nc = n // CHUNK
    ch = lambda t: t.reshape(bsz, h, nc, CHUNK, t.shape[-1])
    q, k, v, g = ch(q), ch(k), ch(v), ch(g)
    b = jnp.cumsum(g, axis=3)
    b_last = b[:, :, :, -1:, :]
    u = jnp.einsum('bhncd,bhnce->bhnde', k * jnp.exp(b_last - b), v)
    decay = jnp.exp(b_last[:, :, :, 0, :])

    def step(s, inp):
        u_n, a_n = inp
        return a_n[..., None] * s + u_n, s

    s_final, s_before = lax.scan(step, s0, (jnp.moveaxis(u, 2, 0), jnp.moveaxis(decay, 2, 0)))
    s_before = jnp.moveaxis(s_before, 0, 2)
    qe = q * jnp.exp(b)
    ki = k * jnp.exp(-b)
    tri = jnp.tril(jnp.ones((CHUNK, CHUNK), dtype=bool))
    a = jnp.where(tri, jnp.einsum('bhntd,bhnsd->bhnts', qe, ki), 0.0)
    o = jnp.einsum('bhnts,bhnse->bhnte', a, v) + jnp.einsum('bhntd,bhnde->bhnte', qe, s_before)
    return o.reshape(bsz, h, n, -1), s_final

def gla_final_state(k, v, g):
    gc = jnp.cumsum(g, axis=2)
    return jnp.einsum('bhnd,bhne->bhde', k * jnp.exp(gc[:, :, -1:, :] - gc), v)

def gla_bidir(q, k, v, gates, s_init):
    o_f, s_f = gla_chunked(q, k, v, gates[0], s_init[0])
    o_b, s_b = gla_chunked(rev(q), rev(k), rev(v), rev(gates[1]), s_init[1])
    return o_f + rev(o_b), (s_f, s_b)

def gla_out(o, r, norm_w):
    o = o * lax.rsqrt(jnp.mean(o * o, axis=-1, keepdims=True) + EPS) * norm_w.astype(jnp.float32)
    bsz, h, n, dv = o.shape
    o = o.transpose(0, 2, 1, 3).reshape(bsz, n, h * dv)
    return (o * jax.nn.silu(r.astype(jnp.float32))).astype(r.dtype)

def short_conv(bg, cg, hv, conv_w):
    z = cg * hv
    length = z.shape[-2]
    zp = jnp.pad(z, [(0, 0)] * (z.ndim - 2) + [(CONV_K // 2, CONV_K // 2), (0, 0)])
    y = sum(conv_w[j] * zp[..., j:j + length, :] for j in range(CONV_K))
    return bg * y

def multi_scale_pool(u, pool_w, pool_scale):
    length = u.shape[-2]
    uf = u.astype(jnp.float32)
    cs = jnp.concatenate([jnp.zeros_like(uf[..., :1, :]), jnp.cumsum(uf, axis=-2)], axis=-2)
    t = np.arange(length)
    outs = []
    for gi, w in enumerate(POOL_WINDOWS):
        lo = np.clip(t - w // 2, 0, length)
        hi = np.clip(t + w // 2, 0, length)
        sl = slice(gi * POOL_GROUP, (gi + 1) * POOL_GROUP)
        csg = cs[..., sl]
        mean = (jnp.take(csg, hi, axis=-2) - jnp.take(csg, lo, axis=-2)) / (hi - lo).astype(np.float32)[:, None]
        outs.append(mean - uf[..., sl])
    p = jnp.stack(outs, axis=-2)
    y = jnp.einsum('...lgc,gcd->...lgd', p, pool_w.astype(jnp.float32))
    y = y.reshape(y.shape[:-2] + (POOL_WIDTH,)) * pool_scale.astype(jnp.float32)
    return y.astype(u.dtype)

def mix_and_mlp(x, proj, o_gla, n_seg, g1, sh2, sc2, g2, norm2_w, gla_norm_w, conv_w, pool_w,
                pool_scale, w_out, w_mlp1, w_mlp2):
    bsz, n, _ = proj.shape
    seg = lambda t: t.reshape(bsz, n_seg, n // n_seg, t.shape[-1])
    y_gla = gla_out(o_gla, proj[..., R_OFF:CB_OFF], gla_norm_w)
    y_conv = short_conv(seg(proj[..., CB_OFF:CC_OFF]), seg(proj[..., CC_OFF:CH_OFF]),
                        seg(proj[..., CH_OFF:P_OFF]), conv_w).reshape(bsz, n, CONV_WIDTH)
    y_pool = multi_scale_pool(seg(proj[..., P_OFF:IN_COLS]), pool_w, pool_scale).reshape(bsz, n, POOL_WIDTH)
    mix = jnp.concatenate([y_gla, y_conv, y_pool], axis=-1) @ w_out
    x = x + g1 * mix
    h2 = modulate(x, norm2_w, sh2, sc2)
    return x + g2 * (jnp.square(jax.nn.relu(h2 @ w_mlp1)) @ w_mlp2)

def setup_inputs(seed: int = 0) -> dict:
    key = jax.random.key(seed)
    ks = jax.random.split(key, 20)
    f32 = jnp.float32
    nrm = lambda k, shape, s: jax.random.normal(k, shape, f32) * s
    return {
        'x': nrm(ks[0], (BATCH, SEQ, D_MODEL), 1.0),
        'c': nrm(ks[1], (BATCH, D_MODEL), 1.0),
        'ctx': nrm(ks[2], (BATCH, CTX_LEN, D_MODEL), 1.0),
        'c_ctx': nrm(ks[3], (D_MODEL,), 1.0),
        'w_mod': nrm(ks[4], (DEPTH, D_MODEL, N_MOD * D_MODEL), 0.5 * D_MODEL ** -0.5),
        'b_mod': nrm(ks[5], (DEPTH, N_MOD * D_MODEL), 0.02),
        'norm1_w': 1.0 + nrm(ks[6], (DEPTH, D_MODEL), 0.02),
        'norm2_w': 1.0 + nrm(ks[7], (DEPTH, D_MODEL), 0.02),
        'w_in': nrm(ks[8], (DEPTH, D_MODEL, IN_COLS), D_MODEL ** -0.5),
        'gla_gate_w': nrm(ks[9], (DEPTH, 2, GATE_RANK, GLA_KEY_WIDTH), GATE_RANK ** -0.5),
        'gla_gate_b': jax.random.uniform(ks[10], (DEPTH, 2, GLA_KEY_WIDTH), f32, 1.0, 5.0),
        'gla_norm_w': 1.0 + nrm(ks[11], (DEPTH, GLA_DV), 0.02),
        'conv_w': nrm(ks[12], (DEPTH, CONV_K, CONV_WIDTH), CONV_K ** -0.5),
        'pool_w': nrm(ks[13], (DEPTH, len(POOL_WINDOWS), POOL_GROUP, POOL_GROUP), POOL_GROUP ** -0.5),
        'pool_scale': 1.0 + nrm(ks[14], (DEPTH, POOL_WIDTH), 0.02),
        'w_out': nrm(ks[15], (DEPTH, D_MIX, D_MODEL), D_MIX ** -0.5),
        'w_mlp1': nrm(ks[16], (DEPTH, D_MODEL, D_FF), D_MODEL ** -0.5),
        'w_mlp2': nrm(ks[17], (DEPTH, D_FF, D_MODEL), D_FF ** -0.5),
        'final_norm_w': 1.0 + nrm(ks[18], (D_MODEL,), 0.02),
    }

def reference(x, c, ctx, c_ctx, w_mod, b_mod, norm1_w, norm2_w, w_in, gla_gate_w, gla_gate_b,
              gla_norm_w, conv_w, pool_w, pool_scale, w_out, w_mlp1, w_mlp2, final_norm_w):
    bsz, n, _ = x.shape
    rows = n // GRID_W
    xc = ctx
    for l in range(DEPTH):
        last = l == DEPTH - 1
        sh1, sc1, g1, sh2, sc2, g2 = [m[:, None, :] for m in adaln(c, w_mod[l], b_mod[l], N_MOD)]
        h = modulate(x, norm1_w[l], sh1, sc1)
        proj = h @ w_in[l]
        q = to_heads(proj[..., Q_OFF:K_OFF], GLA_HEADS).astype(jnp.float32) * GLA_DK ** -0.5
        k, v, gates = gla_kvg(proj[..., K_OFF:V_OFF], proj[..., V_OFF:G_OFF], proj[..., G_OFF:R_OFF],
                              gla_gate_w[l], gla_gate_b[l])
        if last:
            csh1, csc1 = adaln(c_ctx, w_mod[l], b_mod[l], 2)
            hc = modulate(xc, norm1_w[l], csh1, csc1)
            pc = hc @ w_in[l][:, K_OFF:R_OFF]
            kc, vc, gc = gla_kvg(pc[..., :V_OFF - K_OFF], pc[..., V_OFF - K_OFF:G_OFF - K_OFF],
                                 pc[..., G_OFF - K_OFF:], gla_gate_w[l], gla_gate_b[l])
            s_ctx = (gla_final_state(kc, vc, gc[0]), gla_final_state(rev(kc), rev(vc), rev(gc[1])))
        else:
            csh1, csc1, cg1, csh2, csc2, cg2 = adaln(c_ctx, w_mod[l], b_mod[l], N_MOD)
            hc = modulate(xc, norm1_w[l], csh1, csc1)
            pc = hc @ w_in[l]
            qc = to_heads(pc[..., Q_OFF:K_OFF], GLA_HEADS).astype(jnp.float32) * GLA_DK ** -0.5
            kc, vc, gc = gla_kvg(pc[..., K_OFF:V_OFF], pc[..., V_OFF:G_OFF], pc[..., G_OFF:R_OFF],
                                 gla_gate_w[l], gla_gate_b[l])
            s0 = jnp.zeros((bsz, GLA_HEADS, GLA_DK, GLA_DV), jnp.float32)
            oc, s_ctx = gla_bidir(qc, kc, vc, gc, (s0, s0))
            xc = mix_and_mlp(xc, pc, oc, 1, cg1, csh2, csc2, cg2, norm2_w[l], gla_norm_w[l], conv_w[l],
                             pool_w[l], pool_scale[l], w_out[l], w_mlp1[l], w_mlp2[l])
        o_lat, _ = gla_bidir(q, k, v, gates, s_ctx)
        x = mix_and_mlp(x, proj, o_lat, rows, g1, sh2, sc2, g2, norm2_w[l], gla_norm_w[l], conv_w[l],
                        pool_w[l], pool_scale[l], w_out[l], w_mlp1[l], w_mlp2[l])
    return rmsnorm(x, final_norm_w)


_drawn_inputs = setup_inputs


def setup_inputs(seed=0):
    import zlib

    import numpy as np

    out = dict(_drawn_inputs(seed))
    spreads = {}
    factors = {'norm1_w': 6.302,
     'norm2_w': 41.263,
     'gla_gate_w': 2.749,
     'gla_norm_w': 64.0,
     'pool_scale': 64.0,
     'final_norm_w': 8.427,
     'ctx': 5.58,
     'c_ctx': 8.0,
     'gla_gate_b': 3.481}
    for name, (base, spread) in spreads.items():
        noise = np.random.default_rng([zlib.crc32(name.encode()), seed]).standard_normal(out[name].shape)
        drawn = base * np.exp(spread * noise) if base else spread * noise
        out[name] = __import__('jax').numpy.asarray(drawn.astype(out[name].dtype))
    for name, factor in factors.items():
        out[name] = (out[name] * factor).astype(out[name].dtype)
    return out
```

```python
from contextlib import ExitStack

import concourse.bass as bass
from concourse import mybir

F32 = mybir.dt.float32
F32R = mybir.dt.float32r
U8 = mybir.dt.uint8
U32 = mybir.dt.uint32
ALU = mybir.AluOpType
ACT = mybir.ActivationFunctionType

P = 128
D = 1024
KT = D // P
N = 1024
NC = 256
NA = N + NC
HALF = 512
HEADS, DK, DV = 4, 64, 128
CH = 64
NCH = N // CH
TT = N // P
SEG = 64
NSEG = N // SEG
PADW = SEG + 16
WINDOWS = (2, 4, 8, 16)
RANK = 16
TAU = 16.0
EPS = 1e-6
NFC = 4
CK = D
KIB = 1024

PROJ = ["V0", "V1", "V2", "V3", "K0", "K1", "Q0", "Q1", "P0", "P1", "CC0", "CH0", "CB0",
        "R0", "R1", "CC1", "CH1", "R2", "R3", "CB1"]
NPROJ = len(PROJ)
MAIN = ["G", "V0", "g0", "V1", "g1", "V2", "g2", "V3", "g3"] + PROJ[4:]
M_OF = {name: m for m, name in enumerate(MAIN)}
M_OUT = len(MAIN)
M_MLP = M_OUT + KT
T_OUT = NPROJ
T_MLP = T_OUT + KT
NSTREAM = T_MLP + 2 * NFC * KT
LO_H2 = KT
LO_HID = LO_H2 + 2 * KT

PLAN = {}


def put(tile, slot, *job):
    PLAN.setdefault((tile, slot), []).append(job)


for _h in range(HEADS):
    for _i, _s in enumerate((3, 5, 7)):
        put(_h + 1, _s, "vt", _h, _i)
for _s, _d, _i in ((4, 0, 0), (5, 0, 1), (6, 1, 0), (7, 1, 1)):
    put(5, _s, "kt", 0, _d, _i)
put(6, 0, "kc", 0)
put(6, 1, "cs", 0)
put(6, 4, "kc", 1)
put(6, 5, "cs", 1)
for _n, (_t, _s) in enumerate(((6, 2), (6, 3), (6, 6), (6, 7), (7, 0), (7, 2), (7, 4), (7, 6))):
    put(_t, _s, "u", 0, _n // 2 % 2, _n // 4, _n % 2)
for _s, _d, _i in ((1, 0, 0), (3, 0, 1), (5, 1, 0), (7, 1, 1)):
    put(8, _s, "kt", 1, _d, _i)
for _n, (_t, _s) in enumerate(((12, 1), (12, 3), (12, 5), (12, 7), (13, 0), (13, 2), (13, 4), (13, 6))):
    put(_t, _s, "u", 1, _n // 2 % 2, _n // 4, _n % 2)
for _h, _first in ((0, 9 * 8), (1, 10 * 8 + 4), (2, 14 * 8), (3, 15 * 8 + 4)):
    for _j in range(4):
        _q = _first + 2 * _j
        put(_q // 8, _q % 8, "A", _h, _j)
        _q += 2
        put(_q // 8, _q % 8, "O", _h, _j)
    for _i in range(2):
        _q = _first + 10 + _i
        put(_q // 8, _q % 8, "ns", _h, _i)
for _i in range(2):
    put(10, 5 + _i, "pl", 0, _i)
    put(11, 5 + 2 * _i, "pl", 1, _i)
for _g, (_t, _s) in enumerate(((3, 0), (5, 0), (6, 7), (9, 1))):
    put(_t, _s, "md", _g)
for _jobs in PLAN.values():
    _jobs.sort(key=lambda job: (job[0] != "O"))

MIX_ORDER = [0, 1, 6, 7, 4, 2, 3, 5]
MOD_AFTER = {0: (0,), 1: (1,), 2: (2,), 3: (3,), 4: (4, 5), 7: (6, 7)}
BANKED = ("vt", "kt", "kc", "cs", "u", "A", "ns", "pl", "md")
SMALL = [("mod1", _j) for _j in range(KT)]
for _t in range(NPROJ):
    for _s in range(KT):
        SMALL += [job for job in PLAN.get((_t, _s), ()) if job[0] in BANKED]
S_OF = {job: s for s, job in enumerate(SMALL)}

COLS = {}
_at = 0
for _name, _w in (("cc", 2 * KT), ("bmod", 6 * KT), ("n1", KT), ("n2", KT), ("fw", KT), ("gb", 4),
                  ("gnw", 1), ("cw", 6), ("ps", 2), ("eps", 1), ("one", 1), ("inv", 2 * SEG),
                  ("ident", P), ("ones", P), ("maskf", P), ("maskb", P), ("pw", 2 * P)):
    COLS[_name] = (_at, _at + _w)
    _at += _w
NSMALL = _at


def hybrid_trunk(nc, wstream, wg_in, wm1, wm2, xt, ct, small_in, gw_in, out):
    ctx = ExitStack()
    with ctx:
        cursor = [(nc.sbuf_base + 63) // 64 * 64]

        def at(name, shape, dt, offset):
            return nc.alloc_sbuf_tensor_at(name, shape, dt, offset=offset)

        def area(nbytes):
            start = cursor[0]
            cursor[0] += (nbytes + 31) // 32 * 32
            assert cursor[0] <= nc.sbuf_usable_end, cursor
            return start

        raw = at("raw", [P, 2, KT, P], F32, area(8 * KIB))
        w_hi = at("w_hi", [P, 2, KT, P], F32R, area(8 * KIB))
        w_lo = at("w_lo", [P, 2, KT, P], F32R, area(8 * KIB))
        HA = area(64 * KIB)
        a_hi = at("a_hi", [P, KT, N], F32R, HA)
        a_lo = at("a_lo", [P, KT, N], F32R, HA + 32 * KIB)
        wmod = at("wmod", [P, KT, 2, KT, P], F32, HA)
        small = at("small", [P, NSMALL], F32, area(NSMALL * 4))

        def col(name, rows=P):
            a, b = COLS[name]
            return small[0:rows, a:b]

        def one_col(name, i, rows=slice(0, P)):
            return small[rows, COLS[name][0] + i:COLS[name][0] + i + 1]

        ident, ones = col("ident"), col("ones")
        silu_c = at("silu_c", [P, 2 * KT], F32, area(64))
        csig = at("csig", [P, 2 * KT], F32, area(64))
        ab1 = at("ab1", [P, KT, 4], F32, area(KT * 16))
        mods = at("mods", [P, 4, KT], F32, area(KT * 16))
        gain2 = at("gain2", [P, KT], F32, area(KT * 4))
        decay = at("decay", [P, 4, NCH], F32, area(4 * NCH * 4))
        STATE = area(4 * P * 4)
        state = at("state", [P, 4, P], F32, STATE)
        wg_hi = at("wg_hi", [P, KT, 32], F32R, STATE)
        wg_lo = at("wg_lo", [P, KT, 32], F32R, STATE + KIB)
        PM = area(NSEG * PADW)
        pmask = at("pmask", [P, NSEG, PADW], U8, PM)
        wg = at("wg", [P, KT, 32], F32, PM)
        EARLY = area(4 * KIB)
        gw = at("gw", [32, 2, 2, P], F32, EARLY)
        gmask = at("gmask", [P, NA], U8, EARLY + 2 * KIB)
        a_f = at("a_f", [P, 2, P], F32, EARLY)
        a_b = at("a_b", [P, 2, P], F32, EARLY + KIB)
        a_sum = at("a_sum", [P, 2, 2, P], F32, EARLY + 2 * KIB)
        vct1 = at("vct1", [P, HEADS * DV], F32, area(2 * KIB))

        ZB = area(16 * KIB)
        ZC = area(16 * KIB)
        ZA = area(16 * KIB)
        ZD = area(8 * KIB)
        ZE = area(16 * KIB)
        ZT = area(16 * KIB)
        ZF = cursor[0]
        assert nc.sbuf_usable_end - ZF >= 18 * KIB, nc.sbuf_usable_end - ZF
        xs = at("xs", [P, KT, NA], F32, ZB)
        sq1 = at("sq1", [P, 2, NA], F32, ZA + 8 * KIB)
        acc1 = at("acc1", [P, NA], F32, ZA + 28 * KIB)
        rs1 = at("rs1", [P, NA], F32, ZF)
        c_hi = at("c_hi", [P, KT, NC], F32R, ZT)
        c_lo = at("c_lo", [P, KT, NC], F32R, ZT + 8 * KIB)
        qe = at("qe", [P, 4, N], F32, ZB)
        vtok = at("vtok", [P, TT, HEADS * DV], F32, ZC)
        ku = at("ku", [P, 4, N], F32, ZA)
        t1 = at("t1", [P, NA], F32, ZD)
        ktok = at("ktok", [P, 2, TT, P], F32, ZD)
        vtmp = at("vtmp", [P, NA], F32, ZE)
        mbuf = at("mbuf", [P, 2, N], F32, ZE + 5 * KIB)
        vct0 = at("vct0", [P, HEADS * DV], F32, ZE + 13 * KIB)
        ypool = at("ypool", [P, 2, N], F32, ZE)
        yconv = at("yconv", [P, 2, N], F32, ZE + 8 * KIB)
        tst = at("tst", [P, 2, NCH, DV], F32, ZT)
        zsb = at("zsb", [32, NA], F32, ZF)
        kctok = at("kctok", [P, 2, 2, 2, P], F32, ZF)
        kuc = at("kuc", [P, 4, NC], F32, ZF + 5 * KIB)
        macc = at("macc", [P, N], F32, ZF + 9 * KIB)
        t2 = at("t2", [P, NA], F32, ZF + 13 * KIB)
        upad = at("upad", [P, NSEG, PADW], F32, ZF)
        cpad = at("cpad", [P, NSEG, PADW], F32, ZF + 5 * KIB)
        zpad = at("zpad", [P, NSEG, SEG + 2], F32, ZF)
        rsig = at("rsig", [P, N], F32, ZF + 5 * KIB)
        sqo = at("sqo", [P, N], F32, ZF + 10 * KIB)
        rso = at("rso", [P, N], F32, ZF + 14 * KIB)
        X = at("X", [P, KT, N], F32, ZB)
        h_hi = at("h_hi", [P, KT, N], F32R, ZA)
        h_lo = at("h_lo", [P, KT, N], F32R, ZA + 32 * KIB)
        ZG = ZA + 64 * KIB
        assert nc.sbuf_usable_end - ZG >= 10 * KIB
        sq2 = at("sq2", [P, N], F32, ZG)
        acc2 = at("acc2", [P, N], F32, ZG + 4 * KIB)
        rs2 = at("rs2", [P, N], F32, ZG)
        ht2 = at("ht2", [P, 2, HALF], F32, ZG + 4 * KIB)
        relu = at("relu", [P, 2, N], F32, ZG)

        main = ctx.enter_context(nc.psum_tensor("main", [P, 2, N], F32))
        ob = ctx.enter_context(nc.psum_tensor("ob", [P, N], F32))
        sm = ctx.enter_context(nc.psum_tensor("sm", [P, 2, HALF], F32))

        def sem(name):
            return ctx.enter_context(nc.semaphore(name))

        small_in_done = sem("small_loaded")
        gw_loaded = sem("gw_loaded")
        wg_loaded = sem("wg_loaded")
        wmod_loaded = [sem(f"wmod_loaded{j}") for j in range(KT)]
        x_loaded = [sem(f"x_loaded{k}") for k in range(KT)]
        ctx_loaded = sem("ctx_loaded")
        raw_loaded = [sem("raw_loaded0"), sem("raw_loaded1")]
        mbuf_loaded = [sem("mbuf_loaded0"), sem("mbuf_loaded1")]
        x2_loaded = [sem("x2_loaded0"), sem("x2_loaded1")]
        out_stored = sem("out_stored")
        masks_made = sem("masks_made")
        pads_made = sem("pads_made")
        wg_split = sem("wg_split")
        hi_made = sem("hi_made")
        split_done = sem("split_done")
        tile_done = sem("tile_done")
        main_free = [sem("main_free0"), sem("main_free1")]
        ctx_free = [sem("ctx_free0"), sem("ctx_free1")]
        small_done = sem("small_done")
        small_free = [sem("small_free0"), sem("small_free1")]
        c_exp = sem("c_exp")
        c_ready = sem("c_ready")
        sq1_made = sem("sq1_made")
        acc1_made = sem("acc1_made")
        sums1_done = sem("sums1_done")
        rs1_made = sem("rs1_made")
        h1_made = sem("h1_made")
        h1_hi = sem("h1_hi")
        h1_lo = sem("h1_lo")
        gate_min = sem("gate_min")
        gate_log = sem("gate_log")
        gate_dif = sem("gate_dif")
        gate_exp = sem("gate_exp")
        pooled = sem("pooled")
        mod_taken = sem("mod_taken")
        a_ready = sem("a_ready")
        o_done = sem("o_done")
        sqo_made = sem("sqo_made")
        rso_made = sem("rso_made")
        y_normed = sem("y_normed")
        r_log = sem("r_log")
        r_min = sem("r_min")
        r_sig = sem("r_sig")
        y_gated = sem("y_gated")
        mix_hi = sem("mix_hi")
        sq2_made = sem("sq2_made")
        acc2_made = sem("acc2_made")
        sums2_done = sem("sums2_done")
        rs2_made = sem("rs2_made")
        h2_scaled = sem("h2_scaled")
        h2_made = sem("h2_made")
        hid_hi = sem("hid_hi")
        lo_made = sem("lo_made")
        hid_sq = sem("hid_sq")
        sq3_made = sem("sq3_made")
        acc3_made = sem("acc3_made")
        sums3_done = sem("sums3_done")
        rs3_made = sem("rs3_made")
        out_made = sem("out_made")
        dve_chain = sem("dve_chain")
        act_chain = sem("act_chain")
        pool_chain = sem("pool_chain")

        def chain(eng, s):
            count = [0]

            def link(ins):
                count[0] += 1
                ins.then_inc(s, 1)
                eng.wait_ge(s, count[0])
            return link

        def main_freed(m):
            return main_free[m % 2], m // 2 + 1

        def ctx_freed(m):
            return ctx_free[m % 2], m // 2 + 1

        def small_freed(s):
            return small_free[s % 2], s // 2 + 1

        def stream_free(t):
            return M_OF[PROJ[t]] + 1 if t < NPROJ else M_OUT + t - NPROJ + 1

        def by_tile(ap):
            return ap.rearrange("p (t e) -> p t e", e=DV)

        def y_gla(h):
            return vtok[:, :, h * DV:(h + 1) * DV]

        def mix_block(k):
            if k < 4:
                return y_gla(k), by_tile
            return (yconv[:, k - 4, :] if k < 6 else ypool[:, k - 6, :]), (lambda ap: ap)

        block = ctx.enter_context(nc.Block())

        @block.sync
        def _(sp):
            sp.dma_start(small[:, :], small_in).then_inc(small_in_done, 16)
            sp.dma_start(gw[:, :, :, :].rearrange("r d p c -> r (d p c)"), gw_in).then_inc(gw_loaded, 16)
            sp.dma_start(wg[:, :, :].rearrange("p k c -> p (k c)"), wg_in).then_inc(wg_loaded, 16)
            sp.dma_start(xs[:, :, N:NA], ct).then_inc(ctx_loaded, 16)
            for k in range(KT):
                sp.dma_start(xs[:, k, 0:N], xt[k]).then_inc(x_loaded[k], 16)
            for j in range(KT):
                sp.dma_start(wmod[:, j, :, :, :].rearrange("p a k c -> p (a k c)"), wm1[j]).then_inc(wmod_loaded[j], 16)

            def load_tile(t):
                if t >= 2:
                    sp.wait_ge(split_done, t - 1)
                sp.dma_start(raw[:, t % 2, :, :].rearrange("p k c -> p (k c)"), wstream[t]).then_inc(raw_loaded[t % 2], 16)

            def load_mod(n):
                if n >= 2:
                    sp.wait_ge(mod_taken, n - 1)
                sp.dma_start(mbuf[:, n % 2, :], wm2[n // KT, n % KT]).then_inc(mbuf_loaded[n % 2], 16)

            for t in range(4):
                load_tile(t)
            sp.wait_ge(h1_lo, KT)
            for t in range(NPROJ - 2):
                for part in MOD_AFTER.get(t, ()):
                    for n in range(4 * part, 4 * part + 4):
                        load_mod(n)
                load_tile(t + 4)
            sp.wait_ge(o_done, 4 * HEADS)
            sp.dma_start(X[:, 0:4, :], xt[0:4].rearrange("k p n -> p k n")).then_inc(x2_loaded[0], 16)
            sp.wait_ge(lo_made, KT)
            sp.dma_start(X[:, 4:8, :], xt[4:8].rearrange("k p n -> p k n")).then_inc(x2_loaded[1], 16)
            with sp.Fori(T_OUT // 2 + 1, NSTREAM // 2) as i:
                for b in range(2):
                    sp.wait_ge(split_done, i * 2 + (b - 1))
                    sp.dma_start(raw[:, b, :, :].rearrange("p k c -> p (k c)"),
                                 wstream[bass.ds(i * 2 + b, 1)].rearrange("a p c -> p (a c)")).then_inc(raw_loaded[b], 16)
            for k in range(KT):
                sp.wait_ge(out_made, k + 1)
                sp.dma_start(out[k], X[:, k, :]).then_inc(out_stored, 16)
            sp.wait_ge(out_stored, 16 * KT)

        @block.gpsimd
        def _(pool):
            link = chain(pool, pool_chain)
            pool.wait_ge(small_in_done, 16)
            link(pool.memset(gmask[:, :], 1))
            pool.memset(gmask[:, 0:N + 1:CH], 0).then_inc(masks_made, 1)
            pool.wait_ge(wg_loaded, 16)
            link(pool.tensor_scalar(wg_hi[:, :, :], wg[:, :, :], 1.0, None, ALU.mult))
            pool.tensor_tensor(wg_lo[:, :, :], wg[:, :, :], wg_hi[:, :, :].bitcast(F32), ALU.subtract).then_inc(wg_split, 1)

            def split(b, n, linked, looped=False):
                if looped:
                    ins = pool.tensor_tensor(w_hi[:, b, :, :], raw[:, b, :, :],
                                             ones.unsqueeze(1).broadcast_to([P, KT, P]), ALU.mult)
                else:
                    ins = pool.tensor_scalar(w_hi[:, b, :, :], raw[:, b, :, :], 1.0, None, ALU.mult)
                ins.then_inc(linked, 1)
                pool.wait_ge(linked, n)
                pool.tensor_tensor(w_lo[:, b, :, :], raw[:, b, :, :], w_hi[:, b, :, :].bitcast(F32),
                                   ALU.subtract).then_inc(split_done, 1)

            for t in range(NPROJ):
                pool.wait_ge(raw_loaded[t % 2], 16 * (t // 2 + 1))
                if t >= 2:
                    pool.wait_ge(tile_done, stream_free(t - 2))
                split(t % 2, t + 1, hi_made)
                if t == 0:
                    pool.wait_ge(wg_split, 1)
                    link(pool.memset(pmask[:, :, :], 1))
                    pool.memset(pmask[:, :, 0], 0).then_inc(masks_made, 1)
            for t in (T_OUT, T_OUT + 1):
                pool.wait_ge(raw_loaded[t % 2], 16 * (t // 2 + 1))
                pool.wait_ge(tile_done, stream_free(t - 2))
                split(t % 2, t + 1, hi_made)
            with pool.Fori(T_OUT // 2 + 1, NSTREAM // 2) as i:
                for b in range(2):
                    pool.wait_ge(raw_loaded[b], i * 16 + 16)
                    pool.wait_ge(tile_done, i * 2 + (b - 2 + M_OUT - T_OUT + 1))
                    split(b, i * 2 + (b + 1), hi_made, looped=True)

        @block.tensor
        def _(pe):
            def product(bank, slot, x_hi, x_lo, order=range(KT), ready=None, after=None):
                for n, k in enumerate(order):
                    if ready is not None:
                        ready(n, k)
                    first, last = n == 0, n == KT - 1
                    for w, x, begin, end in ((w_hi, x_hi, first, False), (w_hi, x_lo, False, False),
                                             (w_lo, x_hi, False, last)):
                        for half in range(2):
                            ins = pe.matmul(main[:, bank, half * HALF:(half + 1) * HALF], w[:, slot, k, :],
                                            x[:, k, half * HALF:(half + 1) * HALF], start=begin, stop=end)
                    if after is not None and not last:
                        after(k)
                ins.then_inc(tile_done, 1)

            def context_product(m, w_h, w_l, rows):
                for k in range(KT):
                    for w, x, begin, end in ((w_h, c_hi, k == 0, False), (w_h, c_lo, False, False),
                                             (w_l, c_hi, False, k == KT - 1)):
                        ins = pe.matmul(ob[0:rows, (m % 2) * HALF:(m % 2) * HALF + NC], w(k), x[:, k, :],
                                        start=begin, stop=end)
                return ins

            pe.wait_ge(c_ready, 1)
            pe.wait_ge(small_in_done, 16)
            pe.wait_ge(acc1_made, KT)
            for half in range(2):
                pe.matmul(main[:, 1, half * HALF:(half + 1) * HALF], ones, acc1[:, half * HALF:(half + 1) * HALF],
                          start=True, stop=True)
            pe.matmul(ob[:, HALF:HALF + NC], ones, acc1[:, N:NA], start=True, stop=True).then_inc(sums1_done, 1)
            for j in range(KT):
                pe.wait_ge(wmod_loaded[j], 16)
                if j >= 2:
                    pe.wait_ge(*small_freed(j - 2))
                for part in range(2):
                    for k in range(KT):
                        ins = pe.matmul(sm[:, j % 2, 2 * part:2 * part + 2], wmod[:, j, part, k, :],
                                        silu_c[:, 2 * k:2 * k + 2], start=(k == 0), stop=(k == KT - 1))
                ins.then_inc(small_done, 1)

            def begin_small(job):
                s = S_OF[job]
                pe.wait_ge(*small_freed(s - 2))
                return s % 2

            def v_to_tokens(h, i):
                b = begin_small(("vt", h, i))
                m = M_OF[f"V{h}"]
                pe.wait_ge(*main_freed(m))
                pe.wait_ge(*ctx_freed(m))
                for q in range(4 if i < 2 else 2):
                    ins = pe.transpose(sm[:, b, q * P:(q + 1) * P], vtmp[:, (4 * i + q) * P:(4 * i + q + 1) * P], ident)
                ins.then_inc(small_done, 1)

            def k_to_tokens(p, d, i):
                b = begin_small(("kt", p, d, i))
                pe.wait_ge(*main_freed(M_OF[f"K{p}"]))
                for q in range(4):
                    ins = pe.transpose(sm[:, b, q * P:(q + 1) * P], ku[:, 2 * d + p, (4 * i + q) * P:(4 * i + q + 1) * P], ident)
                ins.then_inc(small_done, 1)

            def kc_to_tokens(p):
                b = begin_small(("kc", p))
                pe.wait_ge(*ctx_freed(M_OF[f"K{p}"]))
                for d in range(2):
                    for q in range(2):
                        ins = pe.transpose(sm[:, b, (2 * d + q) * P:(2 * d + q + 1) * P],
                                           kuc[:, 2 * d + p, q * P:(q + 1) * P], ident)
                ins.then_inc(small_done, 1)

            def context_state(p):
                b = begin_small(("cs", p))
                pe.wait_ge(*small_freed(S_OF[("kc", p)]))
                pe.wait_ge(*small_freed(S_OF[("vt", 3, 2)]))
                for d in range(2):
                    for hh in range(2):
                        h = 2 * p + hh
                        for q, v in enumerate((vct0, vct1)):
                            ins = pe.matmul(sm[hh * DK:(hh + 1) * DK, b, d * DV:(d + 1) * DV],
                                            kctok[:, p, d, q, hh * DK:(hh + 1) * DK], v[:, h * DV:(h + 1) * DV],
                                            start=(q == 0), stop=(q == 1))
                ins.then_inc(small_done, 1)

            def chunk(d, g, q):
                return 8 * g + q if d == 0 else NCH - 1 - 8 * g - q

            def updates(p, d, g, odd):
                b = begin_small(("u", p, d, g, odd))
                for i in range(2):
                    pe.wait_ge(*small_freed(S_OF[("kt", p, d, i)]))
                    pe.wait_ge(*small_freed(S_OF[("vt", 3, i)]))
                for q in range(4):
                    n = chunk(d, g, 2 * q + odd)
                    rows = slice((n % 2) * CH, (n % 2 + 1) * CH)
                    for hh in range(2):
                        h = 2 * p + hh
                        ins = pe.matmul(sm[hh * DK:(hh + 1) * DK, b, q * DV:(q + 1) * DV],
                                        ktok[rows, d, n // 2, hh * DK:(hh + 1) * DK],
                                        vtok[rows, n // 2, h * DV:(h + 1) * DV], start=True, stop=True)
                ins.then_inc(small_done, 1)

            def scores(h, j):
                b = begin_small(("A", h, j))
                p, rows = h // 2, slice((h % 2) * DK, (h % 2 + 1) * DK)
                pe.wait_ge(*main_freed(M_OF[f"Q{p}"]))
                for d in range(2):
                    for tl in range(2):
                        t = slice((2 * j + tl) * P, (2 * j + tl + 1) * P)
                        ins = pe.matmul(sm[:, b, (2 * d + tl) * P:(2 * d + tl + 1) * P],
                                        ku[rows, 2 * d + p, t], qe[rows, 2 * d + p, t], start=True, stop=True)
                ins.then_inc(small_done, 1)

            def outputs(h, j):
                p, rows = h // 2, slice((h % 2) * DK, (h % 2 + 1) * DK)
                pe.wait_ge(a_ready, 4 * h + j + 1)
                if j == 0:
                    for d in range(2):
                        pe.wait_ge(*small_freed(S_OF[("u", p, d, 1, 1)]))
                    if h == 0:
                        pe.wait_ge(*ctx_freed(M_OF["K1"]))
                        pe.wait_ge(*ctx_freed(M_OF["K0"]))
                    else:
                        pe.wait_ge(y_normed, h)
                for tl in range(2):
                    t = 2 * j + tl
                    pe.matmul(ob[:, t * P:(t + 1) * P], vtok[:, t, h * DV:(h + 1) * DV], a_sum[:, j % 2, tl, :],
                              start=(t % 4 == 0), stop=False, skip_group_check=True)
                    for n in (2 * t, 2 * t + 1):
                        for d in range(2):
                            ins = pe.matmul(ob[:, n * CH:(n + 1) * CH], tst[rows, d, n, :],
                                            qe[rows, 2 * d + p, n * CH:(n + 1) * CH], start=False,
                                            stop=(t % 4 == 3 and n % 2 == 1 and d == 1), skip_group_check=True)
                ins.then_inc(o_done, 1)

            def head_sums(h, i):
                b = begin_small(("ns", h, i))
                pe.wait_ge(sqo_made, h + 1)
                pe.matmul(sm[:, b, :], ones, sqo[:, i * HALF:(i + 1) * HALF], start=True, stop=True).then_inc(small_done, 1)

            def pool_product(i, half):
                b = begin_small(("pl", i, half))
                pe.wait_ge(pooled, i + 1)
                a = COLS["pw"][0] + i * P
                pe.matmul(sm[:, b, :], small[:, a:a + P], ypool[:, i, half * HALF:(half + 1) * HALF],
                          start=True, stop=True).then_inc(small_done, 1)

            def mod_product(g):
                b = begin_small(("md", g))
                pe.wait_ge(mod_taken, KT * (g + 1))
                for j in range(KT):
                    ins = pe.matmul(sm[:, b, j:j + 1], macc[:, j * P:(j + 1) * P], ones[:, 0:1], start=True, stop=True)
                ins.then_inc(small_done, 1)

            jobs = {"vt": v_to_tokens, "kt": k_to_tokens, "kc": kc_to_tokens, "cs": context_state, "u": updates,
                    "A": scores, "O": outputs, "ns": head_sums, "pl": pool_product, "md": mod_product}

            def gate_products(j):
                d, p = j % 2, j // 2
                m = M_OF[f"g{j}"]
                pe.wait_ge(*main_freed(m - 2))
                pe.wait_ge(*ctx_freed(m - 2))
                if j == 0:
                    pe.wait_ge(*main_freed(M_OF["G"]))
                    pe.wait_ge(*ctx_freed(M_OF["G"]))
                    pe.wait_ge(gw_loaded, 16)
                pe.matmul(ob[:, (m % 2) * HALF:(m % 2) * HALF + NC], gw[:, d, p, :], zsb[:, N:NA], start=True, stop=True)
                for half in range(2):
                    ins = pe.matmul(main[:, m % 2, half * HALF:(half + 1) * HALF], gw[:, d, p, :],
                                    zsb[:, half * HALF:(half + 1) * HALF], start=True, stop=True)
                ins.then_inc(tile_done, 1)

            pe.wait_ge(wg_split, 1)
            for k in range(KT):
                pe.wait_ge(h1_lo, k + 1)
                for w, x, begin, end in ((wg_hi, a_hi, k == 0, False), (wg_hi, a_lo, False, False),
                                         (wg_lo, a_hi, False, k == KT - 1)):
                    for half in range(2):
                        pe.matmul(main[0:32, 0, half * HALF:(half + 1) * HALF], w[:, k, :],
                                  x[:, k, half * HALF:(half + 1) * HALF], start=begin, stop=end)
            context_product(0, lambda k: wg_hi[:, k, :], lambda k: wg_lo[:, k, :], 32).then_inc(tile_done, 1)
            for t, name in enumerate(PROJ):
                m = M_OF[name]
                pe.wait_ge(split_done, t + 1)
                if m >= 2:
                    pe.wait_ge(*main_freed(m - 2))
                if m <= M_OF["K1"]:
                    if m >= 2:
                        pe.wait_ge(*ctx_freed(m - 2))
                    context_product(m, lambda k: w_hi[:, t % 2, k, :], lambda k: w_lo[:, t % 2, k, :], P)

                def small_jobs(k, t=t):
                    for job in PLAN.get((t, k), ()):
                        jobs[job[0]](*job[1:])

                product(m % 2, t % 2, a_hi, a_lo, after=small_jobs)
                small_jobs(KT - 1)
                if name in ("V0", "V1", "V2", "V3"):
                    gate_products(int(name[1]))

            def out_pair(m_free, t_ready, first):
                for b in range(2):
                    pe.wait_ge(split_done, t_ready + b)
                    pe.wait_ge(main_free[1 - b], m_free + b)

                    def mixed(n, k):
                        pe.wait_ge(lo_made, n + 1)

                    product(1 - b, b, a_hi, a_lo, order=MIX_ORDER, ready=mixed if first and b == 0 else None)

            out_pair((M_OUT - 2) // 2 + 1, T_OUT + 1, True)
            with pe.Fori(1, KT // 2) as i:
                out_pair(i + ((M_OUT - 2) // 2 + 1), i * 2 + (T_OUT + 1), False)

            pe.wait_ge(acc2_made, KT + 1)
            for half in range(2):
                ins = pe.matmul(sm[:, half, :], ones, acc2[:, half * HALF:(half + 1) * HALF], start=True, stop=True)
            ins.then_inc(sums2_done, 1)

            def mlp_pair(x_hi, x_lo, m_free, t_ready, ready=None):
                for b in range(2):
                    pe.wait_ge(split_done, t_ready + b)
                    pe.wait_ge(main_free[1 - b], m_free + b)
                    product(1 - b, b, x_hi, x_lo, ready=ready if b == 0 else None)

            free0, ready0 = (M_MLP - 2) // 2 + 1, T_MLP + 1

            def normed(n, k):
                pe.wait_ge(lo_made, LO_H2 + 2 * n + 2)

            mlp_pair(h_hi, h_lo, free0, ready0, normed)
            with pe.Fori(1, KT // 2) as i:
                mlp_pair(h_hi, h_lo, i + free0, i * 2 + ready0)

            def second(base):
                def squared(n, k):
                    pe.wait_ge(lo_made, base + (LO_HID + n + 1 - KT // 2))

                mlp_pair(a_hi, a_lo, base + free0, base * 2 + ready0, squared)
                with pe.Fori(1, KT // 2) as i:
                    mlp_pair(a_hi, a_lo, i + base + free0, i * 2 + (base * 2 + ready0))

            second(KT // 2)
            with pe.Fori(1, NFC) as c:
                with pe.Fori(0, KT // 2) as i:
                    mlp_pair(h_hi, h_lo, i + c * KT + free0, i * 2 + (c * (2 * KT) + ready0))
                second(c * KT + KT // 2)

            pe.wait_ge(acc3_made, KT)
            for half in range(2):
                ins = pe.matmul(sm[:, half, :], ones, acc2[:, half * HALF:(half + 1) * HALF], start=True, stop=True)
            ins.then_inc(sums3_done, 1)

        @block.scalar
        def _(act):
            act.preload_act_table_set("natural_log_exp_and_others")
            link = chain(act, act_chain)

            def rsqrt(dst, src, width, s_out, free=None):
                ins = act.activation(dst, src, ACT.Ln, bias=col("eps"), scale=1.0 / width)
                if free is None:
                    link(ins)
                else:
                    ins.then_inc(free[0], 1)
                    act.wait_ge(*free)
                ins = act.activation(dst, dst, ACT.Exp, scale=-0.5)
                return ins if s_out is None else ins.then_inc(s_out, 1)

            act.wait_ge(small_in_done, 16)
            act.activation(csig[:, :], col("cc"), ACT.Exp, scale=-1.0).then_inc(c_exp, 1)
            act.wait_ge(ctx_loaded, 16)
            for k in range(KT):
                act.wait_ge(x_loaded[k], 16)
                if k >= 2:
                    act.wait_ge(acc1_made, k - 1)
                act.activation(sq1[:, k % 2, :], xs[:, k, :], ACT.Square).then_inc(sq1_made, 1)
            act.wait_ge(sums1_done, 1)
            rsqrt(rs1[:, 0:N], main[:, 1, :], D, None)
            rsqrt(rs1[:, N:NA], ob[:, HALF:HALF + NC], D, rs1_made)
            for k in range(KT):
                act.wait_ge(h1_made, k + 1)
                act.activation(a_hi[:, k, :], xs[:, k, 0:N], ACT.Copy)
                act.activation(c_hi[:, k, :], xs[:, k, N:NA], ACT.Copy).then_inc(h1_hi, 1)

            def v_to_tokens(h, i):
                s = S_OF[("vt", h, i)]
                act.wait_ge(small_done, s + 1)
                if i < 2:
                    act.activation(vtok[:, 4 * i:4 * i + 4, h * DV:(h + 1) * DV],
                                   sm[:, s % 2, :].rearrange("p (t e) -> p t e", t=4), ACT.Copy).then_inc(small_free[s % 2], 1)
                else:
                    act.activation(vct0[:, h * DV:(h + 1) * DV], sm[:, s % 2, 0:DV], ACT.Copy)
                    act.activation(vct1[:, h * DV:(h + 1) * DV], sm[:, s % 2, DV:2 * DV], ACT.Copy).then_inc(small_free[s % 2], 1)

            def k_to_tokens(p, d, i):
                s = S_OF[("kt", p, d, i)]
                act.wait_ge(small_done, s + 1)
                act.activation(ktok[:, d, 4 * i:4 * i + 4, :], sm[:, s % 2, :].rearrange("p (t e) -> p t e", t=4),
                               ACT.Copy).then_inc(small_free[s % 2], 1)

            def kc_to_tokens(p):
                s = S_OF[("kc", p)]
                act.wait_ge(small_done, s + 1)
                act.activation(kctok[:, p, :, :, :], sm[:, s % 2, :].rearrange("p (d q e) -> p d q e", d=2, q=2),
                               ACT.Copy).then_inc(small_free[s % 2], 1)

            def outputs(h, j):
                if j == 3:
                    act.wait_ge(o_done, 4 * (h + 1))
                    if h >= 1:
                        act.wait_ge(y_normed, h)
                    act.activation(sqo[:, :], ob[:, :], ACT.Square).then_inc(sqo_made, 1)

            def head_sums(h, i):
                s = S_OF[("ns", h, i)]
                act.wait_ge(small_done, s + 1)
                half = slice(i * HALF, (i + 1) * HALF)
                rsqrt(rso[:, half], sm[:, s % 2, :], DV, rso_made, small_freed(s))

            def pool_product(i, half):
                s = S_OF[("pl", i, half)]
                act.wait_ge(small_done, s + 1)
                act.activation(ypool[:, i, half * HALF:(half + 1) * HALF], sm[:, s % 2, :], ACT.Copy,
                               scale=one_col("ps", i)).then_inc(small_free[s % 2], 1)

            jobs = {"vt": v_to_tokens, "kt": k_to_tokens, "kc": kc_to_tokens, "O": outputs, "ns": head_sums,
                    "pl": pool_product}

            def after_g():
                act.wait_ge(tile_done, 1)
                act.activation(zsb[:, 0:N], main[0:32, 0, :], ACT.Copy).then_inc(main_free[0], 1)
                act.activation(zsb[:, N:NA], ob[0:32, 0:NC], ACT.Copy).then_inc(ctx_free[0], 1)

            def after_v(h, m):
                if h >= 1:
                    act.wait_ge(small_done, S_OF[("vt", h - 1, 2)] + 1)
                act.activation(vtmp[:, 0:N], main[:, m % 2, :], ACT.Copy).then_inc(main_free[m % 2], 1)
                act.activation(vtmp[:, N:NA], ob[:, (m % 2) * HALF:(m % 2) * HALF + NC], ACT.Copy).then_inc(ctx_free[m % 2], 1)

            def gates(j):
                dp, m = 2 * (j % 2) + j // 2, M_OF[f"g{j}"]
                sign = -1.0 / TAU if j % 2 == 0 else 1.0 / TAU
                act.wait_ge(gate_min, j + 1)
                act.activation(t2[:, 0:N], main[:, m % 2, :], ACT.Abs, bias=one_col("gb", dp)).then_inc(main_free[m % 2], 1)
                act.activation(t2[:, N:NA], ob[:, (m % 2) * HALF:(m % 2) * HALF + NC], ACT.Abs,
                               bias=one_col("gb", dp)).then_inc(ctx_free[m % 2], 1)
                act.wait_ge(*main_freed(m))
                act.wait_ge(*ctx_freed(m))
                link(act.activation(t2[:, :], t2[:, :], ACT.Exp, scale=-1.0))
                act.activation(t2[:, :], t2[:, :], ACT.Ln, bias=col("one")).then_inc(gate_log, 1)
                act.wait_ge(gate_dif, j + 1)
                act.activation(decay[:, dp, :], t2[:, CH - 1:N:CH], ACT.Exp, scale=1.0 / TAU)
                act.activation(ku[:, dp, :], t1[:, 0:N], ACT.Exp, scale=sign)
                act.activation(qe[:, dp, :], t1[:, 0:N], ACT.Exp, scale=-sign)
                act.activation(kuc[:, dp, :], t1[:, N:NA], ACT.Exp, scale=sign).then_inc(gate_exp, 1)

            def after_p(i, m):
                act.wait_ge(pads_made, 1)
                if i == 1:
                    act.wait_ge(pooled, 1)
                act.activation(upad[:, :, 9:9 + SEG], main[:, m % 2, :].rearrange("p (s t) -> p s t", t=SEG),
                               ACT.Copy).then_inc(main_free[m % 2], 1)

            def after_cc(i, m):
                act.wait_ge(pads_made, 2)
                if i == 1:
                    act.wait_ge(*main_freed(M_OF["CB0"]))
                act.activation(zpad[:, :, 1:1 + SEG], main[:, m % 2, :].rearrange("p (s t) -> p s t", t=SEG),
                               ACT.Copy).then_inc(main_free[m % 2], 1)

            def after_r(h, m):
                act.wait_ge(pads_made, 2)
                if h >= 1:
                    act.wait_ge(y_gated, h)
                link(act.activation(rsig[:, :], main[:, m % 2, :], ACT.Abs))
                link(act.activation(rsig[:, :], rsig[:, :], ACT.Exp, scale=-1.0))
                act.activation(rsig[:, :], rsig[:, :], ACT.Ln, bias=col("one")).then_inc(r_log, 1)
                act.wait_ge(r_min, h + 1)
                act.activation(rsig[:, :], rsig[:, :], ACT.Exp).then_inc(r_sig, 1)

            after_g()
            for t, name in enumerate(PROJ):
                for k in range(KT):
                    for job in PLAN.get((t, k), ()):
                        if job[0] in jobs:
                            jobs[job[0]](*job[1:])
                m, i = M_OF[name], int(name[-1])
                if name[:-1] in ("V", "P", "CC", "R"):
                    act.wait_ge(tile_done, m + 1)
                    {"V": after_v, "P": after_p, "CC": after_cc, "R": after_r}[name[:-1]](i, m)
                if name[:-1] == "V":
                    gates(i)

            act.wait_ge(tile_done, M_OUT)
            for k in MIX_ORDER:
                if k < 4:
                    act.wait_ge(y_gated, k + 1)
                elif k < 6:
                    act.wait_ge(*main_freed(M_OF[f"CB{k - 4}"]))
                src, shape = mix_block(k)
                act.activation(shape(a_hi[:, k, :]), src, ACT.Copy).then_inc(mix_hi, 1)

            with act.Fori(0, KT // 2) as i:
                for b in range(2):
                    act.wait_ge(main_free[1 - b], i + ((M_OUT + b) // 2 + 1))
                    act.wait_ge(acc2_made, i * 2 + (b + 1))
                    act.activation(sq2[:, :].unsqueeze(1), X[:, bass.ds(i * 2 + b, 1), :], ACT.Square).then_inc(sq2_made, 1)
            act.wait_ge(sums2_done, 1)
            for half in range(2):
                rsqrt(rs2[:, half * HALF:(half + 1) * HALF], sm[:, half, :], D, rs2_made)
            with act.Fori(0, KT) as k:
                for half in range(2):
                    act.wait_ge(h2_made, k * 2 + (half + 1))
                    act.activation(h_hi[:, bass.ds(k, 1), half * HALF:(half + 1) * HALF], ht2[:, half:half + 1, :],
                                   ACT.Copy).then_inc(hid_hi, 1)

            with act.Fori(0, NFC) as c:
                with act.Fori(0, KT // 2) as j:
                    for b in range(2):
                        act.wait_ge(tile_done, j * 2 + c * (2 * KT) + (M_MLP + b + 1))
                        act.wait_ge(lo_made, j * 2 + c * KT + (LO_HID + b - 1))
                        act.activation(relu[:, b:b + 1, :], main[:, 1 - b:2 - b, :], ACT.Relu).then_inc(main_free[1 - b], 1)
                        act.wait_ge(main_free[1 - b], j + c * KT + ((M_MLP + b) // 2 + 1))
                        act.activation(a_hi[:, bass.ds(j * 2 + b, 1), :], relu[:, b:b + 1, :], ACT.Square).then_inc(hid_hi, 1)

            for k in range(KT):
                if k == 0:
                    act.wait_ge(main_free[0], (M_MLP + 2 * NFC * KT - 1) // 2 + 1)
                    act.wait_ge(main_free[1], (M_MLP + 2 * NFC * KT - 2) // 2 + 1)
                    act.wait_ge(lo_made, LO_HID + NFC * KT)
                else:
                    act.wait_ge(acc3_made, k)
                act.activation(sq2[:, :], X[:, k, :], ACT.Square).then_inc(sq3_made, 1)
            act.wait_ge(sums3_done, 1)
            for half in range(2):
                rsqrt(rs2[:, half * HALF:(half + 1) * HALF], sm[:, half, :], D, rs3_made)

        @block.vector
        def _(dve):
            link = chain(dve, dve_chain)
            tt, ts, stt = dve.tensor_tensor, dve.tensor_scalar, dve.scalar_tensor_tensor

            dve.wait_ge(c_exp, 1)
            link(ts(csig[:, :], csig[:, :], 1.0, None, ALU.add))
            link(dve.reciprocal(csig[:, :], csig[:, :]))
            tt(silu_c[:, :], csig[:, :], col("cc"), ALU.mult).then_inc(c_ready, 1)

            for k in range(KT):
                dve.wait_ge(sq1_made, k + 1)
                if k == 0:
                    ins = dve.tensor_copy(acc1[:, :], sq1[:, 0, :])
                else:
                    ins = tt(acc1[:, :], acc1[:, :], sq1[:, k % 2, :], ALU.add)
                ins.then_inc(acc1_made, 1)
                dve.wait_ge(acc1_made, k + 1)
            dve.wait_ge(rs1_made, 1)
            for k in range(KT):
                last = tt(xs[:, k, :], xs[:, k, :], rs1[:, :], ALU.mult)
            link(last)

            def low1(k):
                dve.wait_ge(h1_hi, k + 1)
                dve.wait_ge(small_done, 5 + k // 2)
                tt(a_lo[:, k, :], xs[:, k, 0:N], a_hi[:, k, :].bitcast(F32), ALU.subtract)
                tt(c_lo[:, k, :], xs[:, k, N:NA], c_hi[:, k, :].bitcast(F32), ALU.subtract).then_inc(h1_lo, 1)

            for j in range(KT):
                s = S_OF[("mod1", j)]
                dve.wait_ge(small_done, s + 1)
                ts(ab1[:, j, 0:2], sm[:, s % 2, 0:2], one_col("bmod", j), None, ALU.add)
                ts(ab1[:, j, 2:4], sm[:, s % 2, 2:4], one_col("bmod", KT + j), 1.0, ALU.add, ALU.add).then_inc(small_free[s % 2], 1)
                dve.wait_ge(*small_freed(s))
                link(ts(ab1[:, j, 2:4], ab1[:, j, 2:4], one_col("n1", j), None, ALU.mult))
                ts(xs[:, j, N:NA], xs[:, j, N:NA], ab1[:, j, 3:4], ab1[:, j, 1:2], ALU.mult, ALU.add)
                ts(xs[:, j, 0:N], xs[:, j, 0:N], ab1[:, j, 2:3], ab1[:, j, 0:1], ALU.mult, ALU.add).then_inc(h1_made, 1)
                if 4 <= j < 7:
                    low1(2 * j - 8)
                    low1(2 * j - 7)
            low1(6)
            low1(7)

            def context_state(p):
                s = S_OF[("cs", p)]
                dve.wait_ge(small_done, s + 1)
                dve.tensor_copy(state[:, p:p + 3:2, :], sm[:, s % 2, 0:2 * DV].rearrange("p (d e) -> p d e", d=2)).then_inc(small_free[s % 2], 1)
                dve.wait_ge(*small_freed(s))

            def updates(p, d, g, odd):
                if not odd:
                    return
                s, dp = S_OF[("u", p, d, g, 1)], 2 * d + p
                assert S_OF[("u", p, d, g, 0)] == s - 1
                dve.wait_ge(small_done, s + 1)
                if p == 1:
                    dve.wait_ge(o_done, 8)
                for q in range(8):
                    n = 8 * g + q if d == 0 else NCH - 1 - 8 * g - q
                    bank = (s - 1 + q % 2) % 2
                    link(ts(tst[:, d, n, :], state[:, dp, :], decay[:, dp, n:n + 1], None, ALU.mult))
                    ins = tt(state[:, dp, :], tst[:, d, n, :], sm[:, bank, (q // 2) * DV:(q // 2 + 1) * DV], ALU.add)
                    if q < 6:
                        link(ins)
                    else:
                        ins.then_inc(small_free[bank], 1)
                        dve.wait_ge(*small_freed(s - 1 + q % 2))

            def scores(h, j):
                s = S_OF[("A", h, j)]
                dve.wait_ge(small_done, s + 1)
                for dst, mask, d in ((a_f, "maskf", 0), (a_b, "maskb", 1)):
                    ins = dve.copy_predicated(dst[:, :, :], col(mask).bitcast(U32).unsqueeze(1).broadcast_to([P, 2, P]),
                                              sm[:, s % 2, 2 * d * P:2 * (d + 1) * P].rearrange("p (t q) -> p t q", t=2))
                ins.then_inc(small_free[s % 2], 1)
                dve.wait_ge(*small_freed(s))
                if 4 * h + j >= 2:
                    dve.wait_ge(o_done, 4 * h + j - 1)
                tt(a_sum[:, j % 2, :, :], a_f[:, :, :], a_b[:, :, :], ALU.add).then_inc(a_ready, 1)
                dve.wait_ge(a_ready, 4 * h + j + 1)

            def head_sums(h, i):
                if i == 1:
                    dve.wait_ge(rso_made, 2 * (h + 1))
                    tt(y_gla(h), by_tile(ob[:, :]), by_tile(rso[:, :]), ALU.mult).then_inc(y_normed, 1)
                    dve.wait_ge(y_normed, h + 1)

            def mod_product(g):
                s = S_OF[("md", g)]
                dve.wait_ge(small_done, s + 1)
                a = COLS["bmod"][0] + (2 + g) * KT
                tt(mods[:, g, :], sm[:, s % 2, 0:KT], small[:, a:a + KT], ALU.add).then_inc(small_free[s % 2], 1)
                dve.wait_ge(*small_freed(s))
                if g == 2:
                    link(stt(out=gain2[:, :], in0=mods[:, 2, :], scalar=1.0, in1=col("n2"), op0=ALU.add, op1=ALU.mult))

            jobs = {"cs": context_state, "u": updates, "A": scores, "ns": head_sums, "md": mod_product}

            def gates(j):
                d, dp, m = j % 2, 2 * (j % 2) + j // 2, M_OF[f"g{j}"]
                dve.wait_ge(tile_done, m + 1)
                if j >= 1:
                    dve.wait_ge(gate_exp, j)
                ts(t1[:, 0:N], main[:, m % 2, :], one_col("gb", dp), 0.0, ALU.add, ALU.min)
                ts(t1[:, N:NA], ob[:, (m % 2) * HALF:(m % 2) * HALF + NC], one_col("gb", dp), 0.0, ALU.add,
                   ALU.min).then_inc(gate_min, 1)
                dve.wait_ge(gate_min, j + 1)
                dve.wait_ge(gate_log, j + 1)
                link(tt(t1[:, :], t1[:, :], t2[:, :], ALU.subtract))
                dve.wait_ge(masks_made, 1)
                link(dve.tensor_tensor_scan(out=t2[:, :], data0=gmask[:, :], data1=t1[:, :], initial=0.0,
                                            op0=ALU.mult, op1=ALU.add))
                if d == 0:
                    chunks = t2[:, 0:N].rearrange("p (n t) -> p n t", t=CH)
                    tt(t1[:, 0:N].rearrange("p (n t) -> p n t", t=CH), chunks,
                       chunks[:, :, CH - 1:CH].broadcast_to([P, NCH, CH]), ALU.subtract)
                    ts(t1[:, N:NA], t2[:, N:NA], t2[:, NA - 1:NA], None, ALU.subtract).then_inc(gate_dif, 1)
                else:
                    tt(t1[:, :], t2[:, :], t1[:, :], ALU.subtract).then_inc(gate_dif, 1)
                dve.wait_ge(gate_dif, j + 1)

            def add_modulations(part):
                for n in range(4 * part, 4 * part + 4):
                    g, k = n // KT, n % KT
                    dve.wait_ge(mbuf_loaded[n % 2], 16 * (n // 2 + 1))
                    if k == 0:
                        if g >= 1:
                            dve.wait_ge(small_done, S_OF[("md", g - 1)] + 1)
                        ins = ts(macc[:, :], mbuf[:, n % 2, :], silu_c[:, 2 * k:2 * k + 1], None, ALU.mult)
                    else:
                        ins = stt(out=macc[:, :], in0=mbuf[:, n % 2, :], scalar=silu_c[:, 2 * k:2 * k + 1],
                                  in1=macc[:, :], op0=ALU.mult, op1=ALU.add)
                    ins.then_inc(mod_taken, 1)
                    dve.wait_ge(mod_taken, n + 1)

            def after_k(p, m):
                dve.wait_ge(gate_exp, 2 * p + 2)
                for d in range(2):
                    ins = tt(ku[:, 2 * d + p, :], main[:, m % 2, :], ku[:, 2 * d + p, :], ALU.mult)
                ins.then_inc(main_free[m % 2], 1)
                for d in range(2):
                    ins = tt(kuc[:, 2 * d + p, :], ob[:, (m % 2) * HALF:(m % 2) * HALF + NC], kuc[:, 2 * d + p, :], ALU.mult)
                ins.then_inc(ctx_free[m % 2], 1)

            def after_q(p, m):
                for d in range(2):
                    ins = stt(out=qe[:, 2 * d + p, :], in0=main[:, m % 2, :], scalar=float(DK) ** -0.5,
                              in1=qe[:, 2 * d + p, :], op0=ALU.mult, op1=ALU.mult)
                ins.then_inc(main_free[m % 2], 1)

            def after_p(i, m):
                dve.wait_ge(*main_freed(m))
                dve.wait_ge(masks_made, 2)
                dve.wait_ge(small_done, S_OF[("md", 3)] + 1)
                link(dve.tensor_tensor_scan(out=cpad[:, :, :].rearrange("p s t -> p (s t)"),
                                            data0=pmask[:, :, :].rearrange("p s t -> p (s t)"),
                                            data1=upad[:, :, :].rearrange("p s t -> p (s t)"), initial=0.0,
                                            op0=ALU.mult, op1=ALU.add))
                y = ypool[:, i, :].rearrange("p (s t) -> p s t", t=SEG)
                for r in range(2):
                    rows, w = slice(64 * r, 64 * r + 64), WINDOWS[2 * i + r]
                    last = tt(y[rows], cpad[rows, :, 8 + w // 2:8 + w // 2 + SEG], cpad[rows, :, 8 - w // 2:8 - w // 2 + SEG],
                              ALU.subtract)
                link(last)
                a = COLS["inv"][0] + i * SEG
                link(tt(y, y, small[:, a:a + SEG].unsqueeze(1).broadcast_to([P, NSEG, SEG]), ALU.mult))
                tt(y, y, upad[:, :, 9:9 + SEG], ALU.subtract).then_inc(pooled, 1)

            def after_ch(i, m):
                dve.wait_ge(*main_freed(M_OF[f"CC{i}"]))
                z = zpad[:, :, 1:1 + SEG]
                tt(z, z, main[:, m % 2, :].rearrange("p (s t) -> p s t", t=SEG), ALU.mult).then_inc(main_free[m % 2], 1)
                dve.wait_ge(*main_freed(m))
                y = yconv[:, i, :].rearrange("p (s t) -> p s t", t=SEG)
                link(ts(y, zpad[:, :, 0:SEG], one_col("cw", 3 * i), None, ALU.mult))
                for j in (1, 2):
                    link(stt(out=y, in0=zpad[:, :, j:j + SEG], scalar=one_col("cw", 3 * i + j), in1=y,
                             op0=ALU.mult, op1=ALU.add))

            def after_cb(i, m):
                tt(yconv[:, i, :], main[:, m % 2, :], yconv[:, i, :], ALU.mult).then_inc(main_free[m % 2], 1)

            def after_r(h, m):
                dve.wait_ge(r_log, h + 1)
                stt(out=rsig[:, :], in0=main[:, m % 2, :], scalar=0.0, in1=rsig[:, :], op0=ALU.min,
                    op1=ALU.subtract).then_inc(r_min, 1)
                dve.wait_ge(r_sig, h + 1)
                tt(rsig[:, :], main[:, m % 2, :], rsig[:, :], ALU.mult).then_inc(main_free[m % 2], 1)
                dve.wait_ge(*main_freed(m))
                stt(out=y_gla(h), in0=y_gla(h), scalar=col("gnw"), in1=by_tile(rsig[:, :]), op0=ALU.mult,
                    op1=ALU.mult).then_inc(y_gated, 1)

            after = {"K": after_k, "Q": after_q, "P": after_p, "CH": after_ch, "CB": after_cb, "R": after_r}
            for t, name in enumerate(PROJ):
                for k in range(KT):
                    for job in PLAN.get((t, k), ()):
                        if job[0] in jobs:
                            jobs[job[0]](*job[1:])
                m, i = M_OF[name], int(name[-1])
                if name == "P0":
                    dve.memset(upad[:, :, :], 0.0).then_inc(pads_made, 1)
                    dve.memset(a_f[:, :, :], 0.0)
                    link(dve.memset(a_b[:, :, :], 0.0))
                if name[:-1] in after:
                    dve.wait_ge(tile_done, m + 1)
                    after[name[:-1]](i, m)
                if name == "P1":
                    dve.wait_ge(pooled, 2)
                    dve.memset(zpad[:, :, :], 0.0).then_inc(pads_made, 1)
                if name[:-1] == "V":
                    gates(i)
                for part in MOD_AFTER.get(t, ()):
                    add_modulations(part)

            for n, k in enumerate(MIX_ORDER):
                dve.wait_ge(mix_hi, n + 1)
                src, shape = mix_block(k)
                tt(shape(a_lo[:, k, :]), src, shape(a_hi[:, k, :].bitcast(F32)), ALU.subtract).then_inc(lo_made, 1)

            dve.memset(acc2[:, :], 0.0).then_inc(acc2_made, 1)
            dve.wait_ge(acc2_made, 1)
            dve.wait_ge(x2_loaded[0], 16)
            dve.wait_ge(x2_loaded[1], 16)
            with dve.Fori(0, KT // 2) as i:
                for b in range(2):
                    dve.wait_ge(tile_done, i * 2 + (M_OUT + b + 1))
                    xk = X[:, bass.ds(i * 2 + b, 1), :]
                    stt(out=xk, in0=main[:, 1 - b:2 - b, :], scalar=mods[:, 0, bass.ds(i * 2 + b, 1)], in1=xk,
                        op0=ALU.mult, op1=ALU.add).then_inc(main_free[1 - b], 1)
                    dve.wait_ge(sq2_made, i * 2 + (b + 1))
                    tt(acc2[:, :], acc2[:, :], sq2[:, :], ALU.add).then_inc(acc2_made, 1)
                    dve.wait_ge(acc2_made, i * 2 + (b + 2))

            dve.wait_ge(rs2_made, 2)
            with dve.Fori(0, KT) as k:
                dve.wait_ge(lo_made, k * 2 + LO_H2)
                for half in range(2):
                    cols = slice(half * HALF, (half + 1) * HALF)
                    tt(ht2[:, half:half + 1, :], X[:, bass.ds(k, 1), cols], rs2[:, cols].unsqueeze(1), ALU.mult).then_inc(h2_scaled, 1)
                for half in range(2):
                    dve.wait_ge(h2_scaled, k * 2 + (half + 1))
                    ts(ht2[:, half:half + 1, :], ht2[:, half:half + 1, :], gain2[:, bass.ds(k, 1)], mods[:, 1, bass.ds(k, 1)],
                       ALU.mult, ALU.add).then_inc(h2_made, 1)
                for half in range(2):
                    cols = slice(half * HALF, (half + 1) * HALF)
                    dve.wait_ge(hid_hi, k * 2 + (half + 1))
                    tt(h_lo[:, bass.ds(k, 1), cols], ht2[:, half:half + 1, :], h_hi[:, bass.ds(k, 1), cols].bitcast(F32),
                       ALU.subtract).then_inc(lo_made, 1)

            with dve.Fori(0, NFC) as c:
                with dve.Fori(0, KT // 2) as j:
                    for b in range(2):
                        dve.wait_ge(hid_hi, j * 2 + c * KT + (2 * KT + b + 1))
                        r = relu[:, b:b + 1, :]
                        tt(r, r, r, ALU.mult).then_inc(hid_sq, 1)
                        dve.wait_ge(hid_sq, j * 2 + c * KT + (b + 1))
                        tt(a_lo[:, bass.ds(j * 2 + b, 1), :], r, a_hi[:, bass.ds(j * 2 + b, 1), :].bitcast(F32),
                           ALU.subtract).then_inc(lo_made, 1)
                with dve.Fori(0, KT // 2) as j:
                    for b in range(2):
                        dve.wait_ge(tile_done, j * 2 + c * (2 * KT) + (M_MLP + KT + b + 1))
                        xk = X[:, bass.ds(j * 2 + b, 1), :]
                        stt(out=xk, in0=main[:, 1 - b:2 - b, :], scalar=mods[:, 3, bass.ds(j * 2 + b, 1)], in1=xk,
                            op0=ALU.mult, op1=ALU.add).then_inc(main_free[1 - b], 1)

            for k in range(KT):
                dve.wait_ge(sq3_made, k + 1)
                if k == 0:
                    ins = dve.tensor_copy(acc2[:, :], sq2[:, :])
                else:
                    ins = tt(acc2[:, :], acc2[:, :], sq2[:, :], ALU.add)
                ins.then_inc(acc3_made, 1)
                dve.wait_ge(acc3_made, k + 1)
            dve.wait_ge(rs3_made, 2)
            for k in range(KT):
                stt(out=X[:, k, :], in0=X[:, k, :], scalar=one_col("fw", k), in1=rs2[:, :], op0=ALU.mult,
                    op1=ALU.mult).then_inc(out_made, 1)


def kernel(**inputs):
    import numpy as np
    from concourse import bacc
    from concourse.bass_utils import run_bass_kernel_spmd

    a = {k: np.asarray(v) for k, v in inputs.items()}

    def tiles(w):
        return w.reshape(KT, P, -1, P).transpose(2, 1, 0, 3).reshape(-1, P, KT * P)

    def by_feature(v):
        return v.reshape(-1, P).T

    w_in = a["w_in"][0]
    at = {}
    g_off = 2 * HEADS * DK + HEADS * DV
    rest = g_off + 2 * RANK
    for name, start in (("Q", 0), ("K", HEADS * DK), ("V", 2 * HEADS * DK), ("R", rest), ("CB", rest + HEADS * DV),
                        ("CC", rest + HEADS * DV + 256), ("CH", rest + HEADS * DV + 512), ("P", rest + HEADS * DV + 768)):
        at[name] = start
    stream = [tiles(w_in[:, at[n[:-1]] + P * int(n[-1]):at[n[:-1]] + P * int(n[-1]) + P]) for n in PROJ]
    stream.append(tiles(a["w_out"][0]))
    for c in range(NFC):
        cols = slice(c * CK, (c + 1) * CK)
        stream.append(tiles(a["w_mlp1"][0][:, cols]))
        stream.append(tiles(a["w_mlp2"][0][cols, :]))

    w_mod = a["w_mod"][0]
    wm1 = w_mod[:, :2 * D].reshape(KT, P, 2, KT, P).transpose(3, 1, 2, 0, 4).reshape(KT, P, 2 * KT * P)
    wm2 = w_mod[:, 2 * D:].reshape(KT, P, 4, D).transpose(2, 0, 1, 3)

    token = np.arange(P)
    same = (token[:, None] // CH) == (token[None, :] // CH)
    t = np.arange(SEG)
    inv = np.zeros((P, 2, SEG), np.float32)
    for g, w in enumerate(WINDOWS):
        count = np.clip(t + w // 2, 0, SEG) - np.clip(t - w // 2, 0, SEG)
        inv[64 * (g % 2):64 * (g % 2) + 64, g // 2] = np.float32(1) / count.astype(np.float32)
    pw = np.zeros((P, 2, P), np.float32)
    for g in range(4):
        r = slice(64 * (g % 2), 64 * (g % 2) + 64)
        pw[r, g // 2, r] = a["pool_w"][0, g]
    parts = {
        "cc": np.stack([by_feature(a["c"][0]), by_feature(a["c_ctx"])], axis=2),
        "bmod": by_feature(a["b_mod"][0]), "n1": by_feature(a["norm1_w"][0]), "n2": by_feature(a["norm2_w"][0]),
        "fw": by_feature(a["final_norm_w"]), "gb": by_feature(a["gla_gate_b"][0].reshape(-1)),
        "gnw": by_feature(a["gla_norm_w"][0]),
        "cw": a["conv_w"][0].reshape(3, 2, P).transpose(2, 1, 0),
        "ps": by_feature(a["pool_scale"][0]),
        "eps": np.full((P, 1), EPS), "one": np.ones((P, 1)), "inv": inv,
        "ident": np.eye(P), "ones": np.ones((P, P)),
        "maskf": same & (token[:, None] <= token[None, :]), "maskb": same & (token[:, None] >= token[None, :]),
        "pw": pw,
    }
    small = np.zeros((P, NSMALL), np.float32)
    for name, (lo, hi) in COLS.items():
        small[:, lo:hi] = np.asarray(parts[name], np.float32).reshape(P, hi - lo)
    gw = np.zeros((2 * RANK, 2, 2 * P), np.float32)
    for d in range(2):
        gw[d * RANK:(d + 1) * RANK, d] = a["gla_gate_w"][0, d]

    arrays = {
        "wstream": np.concatenate(stream), "wg_in": w_in[:, g_off:rest].reshape(KT, P, 32).transpose(1, 0, 2).reshape(P, -1),
        "wm1": wm1, "wm2": wm2, "xt": a["x"][0].T.reshape(KT, P, N),
        "ct": a["ctx"][0].T.reshape(KT, P, NC).transpose(1, 0, 2), "small_in": small, "gw_in": gw.reshape(2 * RANK, -1),
    }
    arrays = {k: np.ascontiguousarray(v) for k, v in arrays.items()}
    nc = bacc.Bacc("TRN2", target_bir_lowering=False, num_devices=1)
    args = [nc.dram_tensor(k, v.shape, mybir.dt.from_np(v.dtype), kind="ExternalInput").ap() for k, v in arrays.items()]
    out = nc.dram_tensor("out", (KT, P, N), F32, kind="ExternalOutput").ap()
    hybrid_trunk(nc, *args, out)
    r = run_bass_kernel_spmd(nc, [arrays], core_ids=[0])
    return r.results[0]["out"].reshape(D, N).T.reshape(1, N, D)
```

```python
from contextlib import ExitStack

import concourse.bass as bass
from concourse import mybir

F32 = mybir.dt.float32
F32R = mybir.dt.float32r
U8 = mybir.dt.uint8
U32 = mybir.dt.uint32
ALU = mybir.AluOpType
ACT = mybir.ActivationFunctionType

P = 128
D = 1024
KT = D // P
N = 1024
NC = 256
NA = N + NC
HALF = 512
HEADS, DK, DV = 4, 64, 128
CH = 64
NCH = N // CH
TT = N // P
SEG = 64
NSEG = N // SEG
PADW = SEG + 16
WINDOWS = (2, 4, 8, 16)
RANK = 16
TAU = 16.0
EPS = 1e-6
NFC = 4
CK = D
KIB = 1024

PROJ = ["V0", "V1", "V2", "V3", "K0", "K1", "Q0", "Q1", "P0", "P1", "CC0", "CH0", "CB0",
        "R0", "R1", "CC1", "CH1", "R2", "R3", "CB1"]
NPROJ = len(PROJ)
MAIN = ["G", "V0", "g0", "V1", "g1", "V2", "g2", "V3", "g3"] + PROJ[4:]
M_OF = {name: m for m, name in enumerate(MAIN)}
M_OUT = len(MAIN)
M_MLP = M_OUT + KT
T_OUT = NPROJ
T_MLP = T_OUT + KT
NSTREAM = T_MLP + 2 * NFC * KT
LO_H2 = KT
LO_HID = LO_H2 + 2 * KT

PLAN = {}


def put(tile, slot, *job):
    PLAN.setdefault((tile, slot), []).append(job)


for _h in range(HEADS):
    for _i, _s in enumerate((3, 5, 7)):
        put(_h + 1, _s, "vt", _h, _i)
for _s, _d, _i in ((4, 0, 0), (5, 0, 1), (6, 1, 0), (7, 1, 1)):
    put(5, _s, "kt", 0, _d, _i)
put(6, 0, "kc", 0)
put(6, 1, "cs", 0)
put(6, 4, "kc", 1)
put(6, 5, "cs", 1)
for _n, (_t, _s) in enumerate(((6, 2), (6, 3), (6, 6), (6, 7), (7, 0), (7, 2), (7, 4), (7, 6))):
    put(_t, _s, "u", 0, _n // 2, _n % 2)
for _s, _d, _i in ((1, 0, 0), (3, 0, 1), (5, 1, 0), (7, 1, 1)):
    put(8, _s, "kt", 1, _d, _i)
for _n in range(8):
    _q = 12 * 8 + 5 + 2 * _n
    put(_q // 8, _q % 8, "u", 1, _n // 2, _n % 2)
for _h, _first in ((0, 9 * 8 + 4), (1, 11 * 8), (2, 14 * 8 + 7), (3, 16 * 8 + 3)):
    for _j in range(4):
        _q = _first + 2 * _j
        put(_q // 8, _q % 8, "A", _h, _j)
        _q += 2
        put(_q // 8, _q % 8, "O", _h, _j)
    for _i in range(2):
        _q = _first + 11 + _i
        put(_q // 8, _q % 8, "ns", _h, _i)
for _i in range(2):
    put(10, 5 + _i, "pl", 0, _i)
    put(11, 5 + 2 * _i, "pl", 1, _i)
IN_GATES = ((0, 1, 2), (3, 4, 5), (6, 7), (8, 9, 10))
MOD_SLOT = {41 + 5 * _i // 2: 11 + _i for _i in range(21)}
for _g, _q in enumerate((27, 53, 73, 93)):
    put(_q // 8, _q % 8, "md", _g)
for _jobs in PLAN.values():
    _jobs.sort(key=lambda job: (job[0] != "O"))

MIX_ORDER = [0, 1, 6, 7, 4, 2, 3, 5]
H2_POOL = (1, 3, 5, 6, 7)
H2_DVE = tuple(k for k in range(KT) if k not in H2_POOL)
OUT_DVE = 5
OUT_ORDER = (0, 1, 5, 2, 3, 6, 4, 7)
BANKED = ("vt", "kt", "kc", "cs", "u", "A", "ns", "pl", "md")
SMALL = [(_name, _j) for _j in range(KT // 2) for _name in ("rows", "turn")]
for _t in range(NPROJ):
    for _s in range(KT):
        SMALL += [job for job in PLAN.get((_t, _s), ()) if job[0] in BANKED]
S_OF = {job: s for s, job in enumerate(SMALL)}

COLS = {}
_at = 0
for _name, _w in (("cc", 2 * KT), ("bmod", 6 * KT), ("n1", KT), ("n2", KT), ("fw", KT), ("gb", 4),
                  ("gnw", 1), ("cw", 6), ("ps", 2), ("eps", 1), ("one", 1), ("inv", 2 * SEG),
                  ("ident", P), ("ones", P), ("maskf", P), ("maskb", P), ("pw", 2 * P)):
    COLS[_name] = (_at, _at + _w)
    _at += _w
NSMALL = _at


def hybrid_trunk(nc, wstream, wg_in, wm1, wm2, xt, ct, small_in, gw_in, out):
    ctx = ExitStack()
    with ctx:
        cursor = [(nc.sbuf_base + 63) // 64 * 64]

        def at(name, shape, dt, offset):
            return nc.alloc_sbuf_tensor_at(name, shape, dt, offset=offset)

        def area(nbytes):
            start = cursor[0]
            cursor[0] += (nbytes + 31) // 32 * 32
            assert cursor[0] <= nc.sbuf_usable_end, cursor
            return start

        raw = at("raw", [P, 2, KT, P], F32, area(8 * KIB))
        w_hi = at("w_hi", [P, 2, KT, P], F32R, area(8 * KIB))
        w_lo = at("w_lo", [P, 2, KT, P], F32R, area(8 * KIB))
        HA = area(64 * KIB)
        a_hi = at("a_hi", [P, KT, N], F32R, HA)
        a_lo = at("a_lo", [P, KT, N], F32R, HA + 32 * KIB)
        wmod = at("wmod", [P, KT // 2, KT, HALF], F32, HA)
        small = at("small", [P, NSMALL], F32, area(NSMALL * 4))

        def col(name, rows=P):
            a, b = COLS[name]
            return small[0:rows, a:b]

        def one_col(name, i, rows=slice(0, P)):
            return small[rows, COLS[name][0] + i:COLS[name][0] + i + 1]

        ident, ones = col("ident"), col("ones")
        silu_c = at("silu_c", [P, 2 * KT], F32, area(64))
        csig = at("csig", [P, 2 * KT], F32, area(64))
        ab1 = at("ab1", [P, KT, 4], F32, area(KT * 16))
        mods = at("mods", [P, 4, KT], F32, area(KT * 16))
        gain2 = at("gain2", [P, KT], F32, area(KT * 4))
        decay = at("decay", [P, 4, NCH], F32, area(4 * NCH * 4))
        STATE = area(4 * P * 4)
        state = at("state", [P, 4, P], F32, STATE)
        wg_hi = at("wg_hi", [P, KT, 32], F32R, STATE)
        wg_lo = at("wg_lo", [P, KT, 32], F32R, STATE + KIB)
        PM = area(NSEG * PADW)
        pmask = at("pmask", [P, NSEG, PADW], U8, PM)
        wg = at("wg", [P, KT, 32], F32, PM)
        EARLY = area(4 * KIB)
        gw = at("gw", [32, 2, 2, P], F32, EARLY)
        gmask = at("gmask", [P, NA], U8, EARLY + 2 * KIB)
        a_f = at("a_f", [P, 2, P], F32, EARLY)
        a_b = at("a_b", [P, 2, P], F32, EARLY + KIB)
        a_sum = at("a_sum", [P, 2, 2, P], F32, EARLY + 2 * KIB)
        vct1 = at("vct1", [P, HEADS * DV], F32, area(2 * KIB))

        ZB = area(16 * KIB)
        ZC = area(16 * KIB)
        ZA = area(16 * KIB)
        ZD = area(8 * KIB)
        ZE = area(16 * KIB)
        ZT = area(16 * KIB)
        ZF = cursor[0]
        assert nc.sbuf_usable_end - ZF >= 18 * KIB, nc.sbuf_usable_end - ZF
        xs = at("xs", [P, KT, NA], F32, ZB)
        sq1 = at("sq1", [P, 2, NA], F32, ZA + 8 * KIB)
        acc1 = at("acc1", [P, NA], F32, ZA + 28 * KIB)
        rs1 = at("rs1", [P, NA], F32, ZF)
        mrow = at("mrow", [2, 2, HALF], F32, ZF + 5 * KIB)
        c_hi = at("c_hi", [P, KT, NC], F32R, ZT)
        c_lo = at("c_lo", [P, KT, NC], F32R, ZT + 8 * KIB)
        qe = at("qe", [P, 4, N], F32, ZB)
        vtok = at("vtok", [P, TT, HEADS * DV], F32, ZC)
        ku = at("ku", [P, 4, N], F32, ZA)
        t1 = at("t1", [P, NA], F32, ZD)
        ktok = at("ktok", [P, 2, TT, P], F32, ZD)
        vtmp = at("vtmp", [P, NA], F32, ZE)
        mbuf = at("mbuf", [P, 2, N], F32, ZE + 8 * KIB)
        vct0 = at("vct0", [P, HEADS * DV], F32, ZE + 5 * KIB)
        ypool = at("ypool", [P, 2, N], F32, ZE)
        yconv = at("yconv", [P, 2, N], F32, ZE + 8 * KIB)
        tst = at("tst", [P, 2, NCH, DV], F32, ZT)
        zsb = at("zsb", [32, NA], F32, ZF)
        kctok = at("kctok", [P, 2, 2, 2, P], F32, ZF)
        kuc = at("kuc", [P, 4, NC], F32, ZF + 9 * KIB)
        macc = at("macc", [P, N], F32, ZF + 5 * KIB)
        t2 = at("t2", [P, NA], F32, ZF + 13 * KIB)
        upad = at("upad", [P, NSEG, PADW], F32, ZF)
        cpad = at("cpad", [P, NSEG, PADW], F32, ZF + 13 * KIB)
        zpad = at("zpad", [P, NSEG, SEG + 2], F32, ZF)
        rsig = at("rsig", [P, N], F32, ZF + 5 * KIB)
        sqo = at("sqo", [P, N], F32, ZF + 10 * KIB)
        rso = at("rso", [P, N], F32, ZF + 14 * KIB)
        early_hi = at("early_hi", [P, 2, N], F32R, ZA)
        early_lo = at("early_lo", [P, 2, N], F32R, ZA + 8 * KIB)
        X = at("X", [P, KT, N], F32, ZB)
        h_hi = at("h_hi", [P, KT, N], F32R, ZA)
        h_lo = at("h_lo", [P, KT, N], F32R, ZA + 32 * KIB)
        ZG = ZA + 64 * KIB
        assert nc.sbuf_usable_end - ZG >= 10 * KIB
        sq2 = at("sq2", [P, N], F32, ZG)
        acc2 = at("acc2", [P, N], F32, ZG + 4 * KIB)
        rs2 = at("rs2", [P, N], F32, ZG)
        xg = at("xg", [P, KT, N], F32, ZA + 32 * KIB)
        relu = at("relu", [P, 2, N], F32, ZG)

        main = ctx.enter_context(nc.psum_tensor("main", [P, 2, N], F32))
        ob = ctx.enter_context(nc.psum_tensor("ob", [P, N], F32))
        sm = ctx.enter_context(nc.psum_tensor("sm", [P, 2, HALF], F32))

        def sem(name):
            return ctx.enter_context(nc.semaphore(name))

        small_in_done = sem("small_loaded")
        gw_loaded = sem("gw_loaded")
        wg_loaded = sem("wg_loaded")
        wmod_loaded = [sem(f"wmod_loaded{j}") for j in range(KT // 2)]
        x_loaded = [sem(f"x_loaded{k}") for k in range(KT)]
        ctx_loaded = sem("ctx_loaded")
        raw_loaded = [sem("raw_loaded0"), sem("raw_loaded1")]
        mbuf_loaded = [sem("mbuf_loaded0"), sem("mbuf_loaded1")]
        x2_loaded = [sem("x2_loaded0"), sem("x2_loaded1")]
        out_stored = sem("out_stored")
        masks_made = sem("masks_made")
        pads_made = sem("pads_made")
        wg_split = sem("wg_split")
        hi_made = sem("hi_made")
        split_done = sem("split_done")
        tile_done = sem("tile_done")
        main_free = [sem("main_free0"), sem("main_free1")]
        ctx_free = [sem("ctx_free0"), sem("ctx_free1")]
        small_done = sem("small_done")
        small_free = [sem("small_free0"), sem("small_free1")]
        c_exp = sem("c_exp")
        c_ready = sem("c_ready")
        sq1_made = sem("sq1_made")
        acc1_made = sem("acc1_made")
        sums1_done = sem("sums1_done")
        rs1_made = sem("rs1_made")
        h1_made = sem("h1_made")
        h1_hi = sem("h1_hi")
        h1_lo = sem("h1_lo")
        gate_min = sem("gate_min")
        gate_log = sem("gate_log")
        gate_dif = sem("gate_dif")
        gate_exp = sem("gate_exp")
        summed = sem("summed")
        pooled = sem("pooled")
        mod_taken = sem("mod_taken")
        a_ready = sem("a_ready")
        o_done = sem("o_done")
        sqo_made = sem("sqo_made")
        rso_made = sem("rso_made")
        y_normed = sem("y_normed")
        r_log = sem("r_log")
        r_min = sem("r_min")
        r_sig = sem("r_sig")
        y_gated = sem("y_gated")
        mix_hi = sem("mix_hi")
        half_done = sem("half_done")
        res_half = sem("res_half")
        sq_last = sem("sq_last")
        states_made = sem("states_made")
        sq2_made = sem("sq2_made")
        acc2_made = sem("acc2_made")
        sums2_done = sem("sums2_done")
        rs2_made = sem("rs2_made")
        h2_scaled = sem("h2_scaled")
        h2_scaled_pool = sem("h2_scaled_pool")
        xg_made = sem("xg_made")
        hid_hi = sem("hid_hi")
        lo_made = sem("lo_made")
        hid_sq = sem("hid_sq")
        sq3_made = sem("sq3_made")
        acc3_made = sem("acc3_made")
        sums3_done = sem("sums3_done")
        rs3_made = sem("rs3_made")
        out_made = sem("out_made")
        out_scaled = sem("out_scaled")
        out_made_act = sem("out_made_act")
        dve_chain = sem("dve_chain")
        act_chain = sem("act_chain")
        pool_chain = sem("pool_chain")

        def chain(eng, s):
            count = [0]

            def mark(ins):
                count[0] += 1
                ins.then_inc(s, 1)
                return count[0]

            def link(ins):
                eng.wait_ge(s, mark(ins))

            link.mark = mark
            return link

        def main_freed(m):
            return main_free[m % 2], m // 2 + 1

        def ctx_freed(m):
            return ctx_free[m % 2], m // 2 + 1

        def small_freed(s):
            return small_free[s % 2], s // 2 + 1

        def stream_free(t):
            return M_OF[PROJ[t]] + 1 if t < NPROJ else M_OUT + t - NPROJ + 1

        def by_tile(ap):
            return ap.rearrange("p (t e) -> p t e", e=DV)

        def y_gla(h):
            return vtok[:, :, h * DV:(h + 1) * DV]

        def mix_block(k):
            if k < 4:
                return y_gla(k), by_tile
            return (yconv[:, k - 4, :] if k < 6 else ypool[:, k - 6, :]), (lambda ap: ap)

        def mix_parts(k):
            n = MIX_ORDER.index(k)
            return (early_hi[:, n, :], early_lo[:, n, :]) if n < 2 else (a_hi[:, k, :], a_lo[:, k, :])

        block = ctx.enter_context(nc.Block())

        @block.sync
        def _(sp):
            sp.dma_start(small[:, :], small_in).then_inc(small_in_done, 16)
            def load_wmod(j):
                sp.dma_start(wmod[:, j, :, :].rearrange("p k c -> p (k c)"), wm1[j]).then_inc(wmod_loaded[j], 16)

            def load_tile(t):
                if t >= 2:
                    sp.wait_ge(split_done, t - 1)
                sp.dma_start(raw[:, t % 2, :, :].rearrange("p k c -> p (k c)"), wstream[t]).then_inc(raw_loaded[t % 2], 16)

            def load_mod(n):
                if n >= 2:
                    sp.wait_ge(mod_taken, n - 1)
                sp.dma_start(mbuf[:, n % 2, :], wm2[n // KT, n % KT]).then_inc(mbuf_loaded[n % 2], 16)

            load_wmod(0)
            sp.dma_start(xs[:, :, N:NA], ct).then_inc(ctx_loaded, 16)
            for k in range(KT):
                sp.dma_start(xs[:, k, 0:N], xt[k]).then_inc(x_loaded[k], 16)
                if k == 1:
                    load_wmod(1)
            sp.dma_start(wg[:, :, :].rearrange("p k c -> p (k c)"), wg_in).then_inc(wg_loaded, 16)
            load_tile(0)
            load_wmod(2)
            load_wmod(3)
            sp.dma_start(gw[:, :, :, :].rearrange("r d p c -> r (d p c)"), gw_in).then_inc(gw_loaded, 16)
            for t in range(1, 4):
                load_tile(t)
            sp.wait_ge(h1_lo, KT)
            slot = {n: KT * (j + 1) + 1 for j, part in enumerate(IN_GATES) for n in part}
            slot.update({n: q for q, n in MOD_SLOT.items()})
            loads = [(slot[max(n - 2, 0)], 0, load_mod, n) for n in range(4 * KT)]
            loads += [(KT * (t - 3) + 3, 1, load_tile, t) for t in range(4, T_OUT + 2)]
            for _, _, load, n in sorted(loads, key=lambda x: (x[0], x[1], x[3])):
                load(n)
            sp.wait_ge(o_done, 4 * HEADS)
            sp.dma_start(X[:, 0:4, :], xt[0:4].rearrange("k p n -> p k n")).then_inc(x2_loaded[0], 16)
            sp.wait_ge(lo_made, KT)
            sp.dma_start(X[:, 4:8, :], xt[4:8].rearrange("k p n -> p k n")).then_inc(x2_loaded[1], 16)
            with sp.Fori(T_OUT // 2 + 1, NSTREAM // 2) as i:
                for b in range(2):
                    sp.wait_ge(split_done, i * 2 + (b - 1))
                    sp.dma_start(raw[:, b, :, :].rearrange("p k c -> p (k c)"),
                                 wstream[bass.ds(i * 2 + b, 1)].rearrange("a p c -> p (a c)")).then_inc(raw_loaded[b], 16)
            for half in range(2):
                cols = slice(half * HALF, (half + 1) * HALF)
                for k in OUT_ORDER:
                    if k < OUT_DVE:
                        sp.wait_ge(out_made, half * OUT_DVE + k + 1)
                    else:
                        sp.wait_ge(out_made_act, half * (KT - OUT_DVE) + k - OUT_DVE + 1)
                    sp.dma_start(out[k][:, cols], X[:, k, cols]).then_inc(out_stored, 16)
            sp.wait_ge(out_stored, 16 * 2 * KT)

        @block.gpsimd
        def _(pool):
            link = chain(pool, pool_chain)
            pool.wait_ge(small_in_done, 16)
            link(pool.memset(gmask[:, :], 1))
            pool.memset(gmask[:, 0:N + 1:CH], 0).then_inc(masks_made, 1)
            pool.wait_ge(wg_loaded, 16)
            link(pool.tensor_scalar(wg_hi[:, :, :], wg[:, :, :], 1.0, None, ALU.mult))
            pool.tensor_tensor(wg_lo[:, :, :], wg[:, :, :], wg_hi[:, :, :].bitcast(F32), ALU.subtract).then_inc(wg_split, 1)

            def split(b, n, linked):
                pool.tensor_tensor(w_hi[:, b, :, :], raw[:, b, :, :], ones.unsqueeze(1).broadcast_to([P, KT, P]),
                                   ALU.mult).then_inc(linked, 1)
                pool.wait_ge(linked, n)
                pool.tensor_tensor(w_lo[:, b, :, :], raw[:, b, :, :], w_hi[:, b, :, :].bitcast(F32),
                                   ALU.subtract).then_inc(split_done, 1)

            for t in range(NPROJ):
                pool.wait_ge(raw_loaded[t % 2], 16 * (t // 2 + 1))
                if t >= 2:
                    pool.wait_ge(tile_done, stream_free(t - 2))
                split(t % 2, t + 1, hi_made)
                if PROJ[t] == "P0":
                    pool.wait_ge(small_done, S_OF[("cs", 1)] + 1)
                    pool.wait_ge(gate_exp, HEADS)
                    pool.memset(a_f[:, :, :], 0.0)
                    pool.memset(a_b[:, :, :], 0.0)
                    pool.memset(upad[:, :, :], 0.0).then_inc(pads_made, 1)
                if t >= 2 and PROJ[t - 2] in ("P0", "P1"):
                    i = int(PROJ[t - 2][1])
                    pool.wait_ge(summed, i + 1)
                    y = ypool[:, i, :].rearrange("p (s t) -> p s t", t=SEG)
                    a = COLS["inv"][0] + i * SEG
                    link(pool.tensor_tensor(y, y, small[:, a:a + SEG].unsqueeze(1).broadcast_to([P, NSEG, SEG]), ALU.mult))
                    pool.tensor_tensor(y, y, upad[:, :, 9:9 + SEG], ALU.subtract).then_inc(pooled, 1)
                    if i == 1:
                        pool.wait_ge(pooled, 2)
                        pool.memset(zpad[:, :, :], 0.0).then_inc(pads_made, 1)
                if t == 0:
                    pool.wait_ge(wg_split, 1)
                    link(pool.memset(pmask[:, :, :], 1))
                    pool.memset(pmask[:, :, 0], 0).then_inc(masks_made, 1)
            for t in (T_OUT, T_OUT + 1):
                pool.wait_ge(raw_loaded[t % 2], 16 * (t // 2 + 1))
                pool.wait_ge(tile_done, stream_free(t - 2))
                split(t % 2, t + 1, hi_made)
            def split_pairs(first, last):
                with pool.Fori(first, last) as i:
                    for b in range(2):
                        pool.wait_ge(raw_loaded[b], i * 16 + 16)
                        pool.wait_ge(tile_done, i * 2 + (b - 2 + M_OUT - T_OUT + 1))
                        split(b, i * 2 + (b + 1), hi_made)

            split_pairs(T_OUT // 2 + 1, T_MLP // 2)
            t = T_MLP
            pool.wait_ge(raw_loaded[0], 16 * (t // 2 + 1))
            pool.wait_ge(tile_done, stream_free(t - 2))
            split(0, t + 1, hi_made)
            for half in range(2):
                cols = slice(half * HALF, (half + 1) * HALF)
                pool.wait_ge(rs2_made, half + 1)
                for k in H2_POOL:
                    pool.wait_ge(xg_made, min(k, KT - 1) + half * (k == KT - 1) + 1)
                    pool.tensor_tensor(xg[:, k, cols], xg[:, k, cols], rs2[:, cols], ALU.mult).then_inc(h2_scaled_pool, 1)
            pool.wait_ge(raw_loaded[1], 16 * (t // 2 + 1))
            pool.wait_ge(tile_done, stream_free(t - 1))
            split(1, t + 2, hi_made)
            split_pairs(T_MLP // 2 + 1, NSTREAM // 2)
            for half in range(2):
                cols = slice(half * HALF, (half + 1) * HALF)
                pool.wait_ge(rs3_made, half + 1)
                for k in range(OUT_DVE, KT):
                    pool.tensor_tensor(X[:, k, cols], X[:, k, cols], rs2[:, cols], ALU.mult).then_inc(out_scaled, 1)

        @block.tensor
        def _(pe):
            def of_a(k):
                return a_hi[:, k, :], a_lo[:, k, :]

            def of_h(k):
                return h_hi[:, k, :], h_lo[:, k, :]

            def product(bank, slot, parts, order=range(KT), ready=None, after=None):
                for n, k in enumerate(order):
                    if ready is not None:
                        ready(n, k)
                    first, last = n == 0, n == KT - 1
                    h, l = parts(k)
                    for w, x, begin, end in ((w_hi, h, first, False), (w_hi, l, False, False), (w_lo, h, False, last)):
                        for half in range(2):
                            ins = pe.matmul(main[:, bank, half * HALF:(half + 1) * HALF], w[:, slot, k, :],
                                            x[:, half * HALF:(half + 1) * HALF], start=begin, stop=end)
                    if after is not None and not last:
                        after(k)
                ins.then_inc(tile_done, 1)

            def product_by_halves(bank, slot, parts, order=range(KT), ready=None, within=None, counted=True):
                for half in range(2):
                    for n, k in enumerate(order):
                        if ready is not None:
                            ready(half, n)
                        if within is not None and half == 1 and n == 3:
                            within()
                        h, l = parts(k)
                        for w, x, begin, end in ((w_hi, h, n == 0, False), (w_hi, l, False, False),
                                                 (w_lo, h, False, n == KT - 1)):
                            ins = pe.matmul(main[:, bank, half * HALF:(half + 1) * HALF], w[:, slot, k, :],
                                            x[:, half * HALF:(half + 1) * HALF], start=begin, stop=end)
                    if counted or half:
                        ins.then_inc(tile_done if half else half_done, 1)

            def squares_summed(acc_made, nth, s_out, half):
                pe.wait_ge(acc_made, KT)
                pe.wait_ge(sq_last, 2 * nth + half + 1)
                cols = slice(half * HALF, (half + 1) * HALF)
                pe.matmul(sm[:, half, :], ones, acc2[:, cols], start=True, stop=False)
                pe.matmul(sm[:, half, :], ones, sq2[:, cols], start=False, stop=True).then_inc(s_out, 1)

            def context_product(m, w_h, w_l, rows):
                for k in range(KT):
                    for w, x, begin, end in ((w_h, c_hi, k == 0, False), (w_h, c_lo, False, False),
                                             (w_l, c_hi, False, k == KT - 1)):
                        ins = pe.matmul(ob[0:rows, (m % 2) * HALF:(m % 2) * HALF + NC], w(k), x[:, k, :],
                                        start=begin, stop=end)
                return ins

            def modulation_rows(j):
                s = S_OF[("rows", j)]
                if s >= 2:
                    pe.wait_ge(*small_freed(s - 2))
                pe.wait_ge(wmod_loaded[j], 16)
                for k in range(KT):
                    ins = pe.matmul(sm[0:2, s % 2, :], silu_c[:, 2 * k:2 * k + 2], wmod[:, j, k, :],
                                    start=(k == 0), stop=(k == KT - 1))
                ins.then_inc(small_done, 1)

            def modulation_turned(j):
                s = S_OF[("turn", j)]
                if s >= 2:
                    pe.wait_ge(*small_freed(s - 2))
                pe.wait_ge(*small_freed(S_OF[("rows", j)]))
                for q in range(4):
                    ins = pe.transpose(sm[:, s % 2, 2 * q:2 * q + 2], mrow[:, j % 2, q * P:(q + 1) * P], ident[0:2, 0:2])
                ins.then_inc(small_done, 1)

            pe.wait_ge(c_ready, 1)
            pe.wait_ge(small_in_done, 16)
            for j in range(2):
                modulation_rows(j)
                modulation_turned(j)
            for squares, ready, n in ((acc1, acc1_made, KT - 1), (sq1[:, (KT - 1) % 2, :], sq1_made, KT)):
                pe.wait_ge(ready, n)
                for half in range(2):
                    pe.matmul(main[:, 1, half * HALF:(half + 1) * HALF], ones, squares[:, half * HALF:(half + 1) * HALF],
                              start=(n < KT), stop=(n == KT))
                ins = pe.matmul(ob[:, HALF:HALF + NC], ones, squares[:, N:NA], start=(n < KT), stop=(n == KT))
            ins.then_inc(sums1_done, 1)

            def begin_small(job):
                s = S_OF[job]
                pe.wait_ge(*small_freed(s - 2))
                return s % 2

            def v_to_tokens(h, i):
                b = begin_small(("vt", h, i))
                m = M_OF[f"V{h}"]
                pe.wait_ge(*main_freed(m))
                pe.wait_ge(*ctx_freed(m))
                for q in range(4 if i < 2 else 2):
                    ins = pe.transpose(sm[:, b, q * P:(q + 1) * P], vtmp[:, (4 * i + q) * P:(4 * i + q + 1) * P], ident)
                ins.then_inc(small_done, 1)

            def k_to_tokens(p, d, i):
                b = begin_small(("kt", p, d, i))
                pe.wait_ge(*main_freed(M_OF[f"K{p}"]))
                for q in range(4):
                    ins = pe.transpose(sm[:, b, q * P:(q + 1) * P], ku[:, 2 * d + p, (4 * i + q) * P:(4 * i + q + 1) * P], ident)
                ins.then_inc(small_done, 1)

            def kc_to_tokens(p):
                b = begin_small(("kc", p))
                pe.wait_ge(*ctx_freed(M_OF[f"K{p}"]))
                for d in range(2):
                    for q in range(2):
                        ins = pe.transpose(sm[:, b, (2 * d + q) * P:(2 * d + q + 1) * P],
                                           kuc[:, 2 * d + p, q * P:(q + 1) * P], ident)
                ins.then_inc(small_done, 1)

            def context_state(p):
                b = begin_small(("cs", p))
                pe.wait_ge(*small_freed(S_OF[("kc", p)]))
                pe.wait_ge(*small_freed(S_OF[("vt", 3, 2)]))
                for d in range(2):
                    for hh in range(2):
                        h = 2 * p + hh
                        for q, v in enumerate((vct0, vct1)):
                            ins = pe.matmul(sm[hh * DK:(hh + 1) * DK, b, d * DV:(d + 1) * DV],
                                            kctok[:, p, d, q, hh * DK:(hh + 1) * DK], v[:, h * DV:(h + 1) * DV],
                                            start=(q == 0), stop=(q == 1))
                ins.then_inc(small_done, 1)

            def updates(p, g, side):
                b = begin_small(("u", p, g, side))
                for d in range(2):
                    for i in range(2):
                        pe.wait_ge(*small_freed(S_OF[("kt", p, d, i)]))
                for i in range(2):
                    pe.wait_ge(*small_freed(S_OF[("vt", 3, i)]))
                rows = slice(side * CH, (side + 1) * CH)
                for d in range(2):
                    for q in range(2):
                        n = 4 * g + 2 * q + side if d == 0 else NCH - 2 - 4 * g - 2 * q + side
                        for hh in range(2):
                            h = 2 * p + hh
                            ins = pe.matmul(sm[hh * DK:(hh + 1) * DK, b, (2 * d + q) * DV:(2 * d + q + 1) * DV],
                                            ktok[rows, d, n // 2, hh * DK:(hh + 1) * DK],
                                            vtok[rows, n // 2, h * DV:(h + 1) * DV], start=True, stop=True)
                ins.then_inc(small_done, 1)

            def scores(h, j):
                b = begin_small(("A", h, j))
                p, rows = h // 2, slice((h % 2) * DK, (h % 2 + 1) * DK)
                pe.wait_ge(*main_freed(M_OF[f"Q{p}"]))
                for d in range(2):
                    for tl in range(2):
                        t = slice((2 * j + tl) * P, (2 * j + tl + 1) * P)
                        ins = pe.matmul(sm[:, b, (2 * d + tl) * P:(2 * d + tl + 1) * P],
                                        ku[rows, 2 * d + p, t], qe[rows, 2 * d + p, t], start=True, stop=True)
                ins.then_inc(small_done, 1)

            def outputs(h, j):
                p, rows = h // 2, slice((h % 2) * DK, (h % 2 + 1) * DK)
                pe.wait_ge(a_ready, 4 * h + j + 1)
                if j == 0:
                    pe.wait_ge(states_made, 8 * (p + 1))
                    if h == 0:
                        pe.wait_ge(*ctx_freed(M_OF["K1"]))
                        pe.wait_ge(*ctx_freed(M_OF["K0"]))
                    else:
                        pe.wait_ge(y_normed, h)
                for tl in range(2):
                    t = 2 * j + tl
                    pe.matmul(ob[:, t * P:(t + 1) * P], vtok[:, t, h * DV:(h + 1) * DV], a_sum[:, j % 2, tl, :],
                              start=(t % 4 == 0), stop=False, skip_group_check=True)
                    for n in (2 * t, 2 * t + 1):
                        for d in range(2):
                            ins = pe.matmul(ob[:, n * CH:(n + 1) * CH], tst[rows, d, n, :],
                                            qe[rows, 2 * d + p, n * CH:(n + 1) * CH], start=False,
                                            stop=(t % 4 == 3 and n % 2 == 1 and d == 1), skip_group_check=True)
                ins.then_inc(o_done, 1)

            def head_sums(h, i):
                b = begin_small(("ns", h, i))
                pe.wait_ge(sqo_made, h + 1)
                pe.matmul(sm[:, b, :], ones, sqo[:, i * HALF:(i + 1) * HALF], start=True, stop=True).then_inc(small_done, 1)

            def pool_product(i, half):
                b = begin_small(("pl", i, half))
                pe.wait_ge(pooled, i + 1)
                a = COLS["pw"][0] + i * P
                pe.matmul(sm[:, b, :], small[:, a:a + P], ypool[:, i, half * HALF:(half + 1) * HALF],
                          start=True, stop=True).then_inc(small_done, 1)

            def mod_product(g):
                b = begin_small(("md", g))
                pe.wait_ge(mod_taken, KT * (g + 1))
                for j in range(KT):
                    ins = pe.matmul(sm[:, b, j:j + 1], macc[:, j * P:(j + 1) * P], ones[:, 0:1], start=True, stop=True)
                ins.then_inc(small_done, 1)

            jobs = {"vt": v_to_tokens, "kt": k_to_tokens, "kc": kc_to_tokens, "cs": context_state, "u": updates,
                    "A": scores, "O": outputs, "ns": head_sums, "pl": pool_product, "md": mod_product}

            def gate_products(j):
                d, p = j % 2, j // 2
                m = M_OF[f"g{j}"]
                pe.wait_ge(*main_freed(m - 2))
                pe.wait_ge(*ctx_freed(m - 2))
                if j == 0:
                    pe.wait_ge(*main_freed(M_OF["G"]))
                    pe.wait_ge(*ctx_freed(M_OF["G"]))
                    pe.wait_ge(gw_loaded, 16)
                pe.matmul(ob[:, (m % 2) * HALF:(m % 2) * HALF + NC], gw[:, d, p, :], zsb[:, N:NA], start=True, stop=True)
                for half in range(2):
                    ins = pe.matmul(main[:, m % 2, half * HALF:(half + 1) * HALF], gw[:, d, p, :],
                                    zsb[:, half * HALF:(half + 1) * HALF], start=True, stop=True)
                ins.then_inc(tile_done, 1)

            def first_products(k):
                pe.wait_ge(h1_lo, k + 1)
                begin, end = k == 0, k == KT - 1
                for m, rows, hi, lo in ((0, 32, wg_hi[:, k, :], wg_lo[:, k, :]), (1, P, w_hi[:, 0, k, :], w_lo[:, 0, k, :])):
                    for w, x, c, b, e in ((hi, a_hi, c_hi, begin, False), (hi, a_lo, c_lo, False, False),
                                          (lo, a_hi, c_hi, False, end)):
                        for half in range(2):
                            pe.matmul(main[0:rows, m, half * HALF:(half + 1) * HALF], w,
                                      x[:, k, half * HALF:(half + 1) * HALF], start=b, stop=e)
                        ins = pe.matmul(ob[0:rows, m * HALF:m * HALF + NC], w, c[:, k, :], start=b, stop=e)
                    if end:
                        ins.then_inc(tile_done, 1)

            pe.wait_ge(wg_split, 1)
            pe.wait_ge(split_done, 1)
            modulation_rows(2)
            first_products(0)
            modulation_turned(2)
            modulation_rows(3)
            first_products(1)
            modulation_turned(3)
            for k in range(2, KT):
                first_products(k)
            gate_products(0)

            for t, name in enumerate(PROJ[1:], 1):
                m = M_OF[name]
                pe.wait_ge(split_done, t + 1)
                pe.wait_ge(*main_freed(m - 2))
                if m <= M_OF["K1"]:
                    pe.wait_ge(*ctx_freed(m - 2))
                    context_product(m, lambda k: w_hi[:, t % 2, k, :], lambda k: w_lo[:, t % 2, k, :], P)

                def small_jobs(k, t=t):
                    for job in PLAN.get((t, k), ()):
                        jobs[job[0]](*job[1:])

                product(m % 2, t % 2, of_a, after=small_jobs)
                small_jobs(KT - 1)
                if name in ("V1", "V2", "V3"):
                    gate_products(int(name[1]))

            def out_pair(m_free, t_ready, first):
                for b in range(2):
                    pe.wait_ge(split_done, t_ready + b)
                    pe.wait_ge(main_free[1 - b], m_free + b)

                    def mixed(n, k):
                        pe.wait_ge(lo_made, n + 1)

                    product(1 - b, b, mix_parts, order=MIX_ORDER, ready=mixed if first and b == 0 else None)

            out_pair((M_OUT - 2) // 2 + 1, T_OUT + 1, True)
            with pe.Fori(1, KT // 2 - 1) as i:
                out_pair(i + ((M_OUT - 2) // 2 + 1), i * 2 + (T_OUT + 1), False)

            def last_pair(m_free, t_ready, acc_made, nth, s_out, parts, order=range(KT)):
                pe.wait_ge(split_done, t_ready)
                pe.wait_ge(main_free[1], m_free)
                product(1, 0, parts, order=order)
                pe.wait_ge(split_done, t_ready + 1)
                pe.wait_ge(main_free[0], m_free + 1)
                product_by_halves(0, 1, parts, order=order,
                                  within=lambda: squares_summed(acc_made, nth, s_out, 0))
                squares_summed(acc_made, nth, s_out, 1)

            last_pair(KT // 2 - 1 + (M_OUT - 2) // 2 + 1, T_OUT + KT - 1, acc2_made, 0, sums2_done, mix_parts, MIX_ORDER)

            def mlp_pair(parts, m_free, t_ready, ready=None):
                for b in range(2):
                    pe.wait_ge(split_done, t_ready + b)
                    pe.wait_ge(main_free[1 - b], m_free + b)
                    product(1 - b, b, parts, ready=ready if b == 0 else None)

            free0, ready0 = (M_MLP - 2) // 2 + 1, T_MLP + 1

            def normed(half, n):
                pe.wait_ge(lo_made, LO_H2 + half * KT + n + 1)

            pe.wait_ge(split_done, ready0)
            pe.wait_ge(main_free[1], free0)
            product_by_halves(1, 0, of_h, ready=normed, counted=False)
            pe.wait_ge(split_done, ready0 + 1)
            pe.wait_ge(main_free[0], free0 + 1)
            product(0, 1, of_h)
            with pe.Fori(1, KT // 2) as i:
                mlp_pair(of_h, i + free0, i * 2 + ready0)

            def second(base, pairs=KT // 2):
                def squared(n, k):
                    pe.wait_ge(lo_made, base + (LO_HID + n + 1 - KT // 2))

                mlp_pair(of_a, base + free0, base * 2 + ready0, squared)
                with pe.Fori(1, pairs) as i:
                    mlp_pair(of_a, i + base + free0, i * 2 + (base * 2 + ready0))

            second(KT // 2)
            with pe.Fori(1, NFC - 1) as c:
                with pe.Fori(0, KT // 2) as i:
                    mlp_pair(of_h, i + c * KT + free0, i * 2 + (c * (2 * KT) + ready0))
                second(c * KT + KT // 2)
            base = (NFC - 1) * KT
            with pe.Fori(0, KT // 2) as i:
                mlp_pair(of_h, i + (base + free0), i * 2 + (2 * base + ready0))
            second(base + KT // 2, KT // 2 - 1)
            last_pair(base + KT - 1 + free0, 2 * (base + KT - 1) + ready0, acc3_made, 1, sums3_done, of_a)

        @block.scalar
        def _(act):
            act.preload_act_table_set("natural_log_exp_and_others")
            link = chain(act, act_chain)

            def rsqrt(dst, src, width, s_out, free=None):
                ins = act.activation(dst, src, ACT.Ln, bias=col("eps"), scale=1.0 / width)
                if free is None:
                    link(ins)
                else:
                    ins.then_inc(free[0], 1)
                    act.wait_ge(*free)
                ins = act.activation(dst, dst, ACT.Exp, scale=-0.5)
                return ins if s_out is None else ins.then_inc(s_out, 1)

            act.wait_ge(small_in_done, 16)
            act.activation(csig[:, :], col("cc"), ACT.Exp, scale=-1.0).then_inc(c_exp, 1)
            act.wait_ge(ctx_loaded, 16)
            def copy_rows(j):
                s = S_OF[("rows", j)]
                act.wait_ge(small_done, s + 1)
                if j >= 2:
                    act.wait_ge(small_done, S_OF[("turn", j - 2)] + 1)
                act.activation(mrow[:, j % 2, :], sm[0:2, s % 2, :], ACT.Copy).then_inc(small_free[s % 2], 1)

            for k in range(KT):
                act.wait_ge(x_loaded[k], 16)
                if k >= 2:
                    act.wait_ge(acc1_made, k - 1)
                act.activation(sq1[:, k % 2, :], xs[:, k, :], ACT.Square).then_inc(sq1_made, 1)
                if k in (1, 5):
                    copy_rows(k // 4)
            act.wait_ge(sums1_done, 1)
            rsqrt(rs1[:, 0:N], main[:, 1, :], D, None)
            rsqrt(rs1[:, N:NA], ob[:, HALF:HALF + NC], D, rs1_made)
            for k in range(KT):
                act.wait_ge(h1_made, k + 1)
                act.activation(a_hi[:, k, :], xs[:, k, 0:N], ACT.Copy)
                act.activation(c_hi[:, k, :], xs[:, k, N:NA], ACT.Copy).then_inc(h1_hi, 1)
                if k in (0, 2):
                    copy_rows(2 + k // 2)

            def v_to_tokens(h, i):
                s = S_OF[("vt", h, i)]
                act.wait_ge(small_done, s + 1)
                if i < 2:
                    act.activation(vtok[:, 4 * i:4 * i + 4, h * DV:(h + 1) * DV],
                                   sm[:, s % 2, :].rearrange("p (t e) -> p t e", t=4), ACT.Copy).then_inc(small_free[s % 2], 1)
                else:
                    act.activation(vct0[:, h * DV:(h + 1) * DV], sm[:, s % 2, 0:DV], ACT.Copy)
                    act.activation(vct1[:, h * DV:(h + 1) * DV], sm[:, s % 2, DV:2 * DV], ACT.Copy).then_inc(small_free[s % 2], 1)

            def k_to_tokens(p, d, i):
                s = S_OF[("kt", p, d, i)]
                act.wait_ge(small_done, s + 1)
                act.activation(ktok[:, d, 4 * i:4 * i + 4, :], sm[:, s % 2, :].rearrange("p (t e) -> p t e", t=4),
                               ACT.Copy).then_inc(small_free[s % 2], 1)

            def kc_to_tokens(p):
                s = S_OF[("kc", p)]
                act.wait_ge(small_done, s + 1)
                act.activation(kctok[:, p, :, :, :], sm[:, s % 2, :].rearrange("p (d q e) -> p d q e", d=2, q=2),
                               ACT.Copy).then_inc(small_free[s % 2], 1)

            def outputs(h, j):
                if j == 3:
                    act.wait_ge(o_done, 4 * (h + 1))
                    act.wait_ge(summed, 2)
                    if h >= 1:
                        act.wait_ge(y_normed, h)
                    act.activation(sqo[:, :], ob[:, :], ACT.Square).then_inc(sqo_made, 1)

            def head_sums(h, i):
                s = S_OF[("ns", h, i)]
                act.wait_ge(small_done, s + 1)
                half = slice(i * HALF, (i + 1) * HALF)
                rsqrt(rso[:, half], sm[:, s % 2, :], DV, rso_made, small_freed(s))

            def pool_product(i, half):
                s = S_OF[("pl", i, half)]
                act.wait_ge(small_done, s + 1)
                act.activation(ypool[:, i, half * HALF:(half + 1) * HALF], sm[:, s % 2, :], ACT.Copy,
                               scale=one_col("ps", i)).then_inc(small_free[s % 2], 1)

            jobs = {"vt": v_to_tokens, "kt": k_to_tokens, "kc": kc_to_tokens, "O": outputs, "ns": head_sums,
                    "pl": pool_product}

            def after_g():
                act.wait_ge(tile_done, 1)
                act.activation(zsb[:, 0:N], main[0:32, 0, :], ACT.Copy).then_inc(main_free[0], 1)
                act.activation(zsb[:, N:NA], ob[0:32, 0:NC], ACT.Copy).then_inc(ctx_free[0], 1)

            def after_v(h, m):
                if h >= 1:
                    act.wait_ge(small_done, S_OF[("vt", h - 1, 2)] + 1)
                act.activation(vtmp[:, 0:N], main[:, m % 2, :], ACT.Copy).then_inc(main_free[m % 2], 1)
                act.activation(vtmp[:, N:NA], ob[:, (m % 2) * HALF:(m % 2) * HALF + NC], ACT.Copy).then_inc(ctx_free[m % 2], 1)

            def gates(j):
                dp, m = 2 * (j % 2) + j // 2, M_OF[f"g{j}"]
                sign = -1.0 / TAU if j % 2 == 0 else 1.0 / TAU
                act.wait_ge(gate_min, j + 1)
                act.activation(t2[:, 0:N], main[:, m % 2, :], ACT.Abs, bias=one_col("gb", dp)).then_inc(main_free[m % 2], 1)
                act.activation(t2[:, N:NA], ob[:, (m % 2) * HALF:(m % 2) * HALF + NC], ACT.Abs,
                               bias=one_col("gb", dp)).then_inc(ctx_free[m % 2], 1)
                act.wait_ge(*main_freed(m))
                act.wait_ge(*ctx_freed(m))
                link(act.activation(t2[:, :], t2[:, :], ACT.Exp, scale=-1.0))
                act.activation(t2[:, :], t2[:, :], ACT.Ln, bias=col("one")).then_inc(gate_log, 1)
                act.wait_ge(gate_dif, j + 1)
                act.activation(decay[:, dp, :], t2[:, CH - 1:N:CH], ACT.Exp, scale=1.0 / TAU)
                act.activation(ku[:, dp, :], t1[:, 0:N], ACT.Exp, scale=sign)
                act.activation(qe[:, dp, :], t1[:, 0:N], ACT.Exp, scale=-sign)
                act.activation(kuc[:, dp, :], t1[:, N:NA], ACT.Exp, scale=sign).then_inc(gate_exp, 1)

            def after_p(i, m):
                act.wait_ge(pads_made, 1)
                if i == 1:
                    act.wait_ge(pooled, 1)
                act.activation(upad[:, :, 9:9 + SEG], main[:, m % 2, :].rearrange("p (s t) -> p s t", t=SEG),
                               ACT.Copy).then_inc(main_free[m % 2], 1)

            def after_cc(i, m):
                act.wait_ge(pads_made, 2)
                if i == 1:
                    act.wait_ge(*main_freed(M_OF["CB0"]))
                act.activation(zpad[:, :, 1:1 + SEG], main[:, m % 2, :].rearrange("p (s t) -> p s t", t=SEG),
                               ACT.Copy).then_inc(main_free[m % 2], 1)

            def after_r(h, m):
                act.wait_ge(pads_made, 2)
                if h >= 1:
                    act.wait_ge(y_gated, h)
                link(act.activation(rsig[:, :], main[:, m % 2, :], ACT.Abs))
                link(act.activation(rsig[:, :], rsig[:, :], ACT.Exp, scale=-1.0))
                act.activation(rsig[:, :], rsig[:, :], ACT.Ln, bias=col("one")).then_inc(r_log, 1)
                act.wait_ge(r_min, h + 1)
                act.activation(rsig[:, :], rsig[:, :], ACT.Exp).then_inc(r_sig, 1)

            after_g()
            for t, name in enumerate(PROJ):
                for k in range(KT):
                    for job in PLAN.get((t, k), ()):
                        if job[0] in jobs:
                            jobs[job[0]](*job[1:])
                m, i = M_OF[name], int(name[-1])
                if name[:-1] in ("V", "P", "CC", "R"):
                    act.wait_ge(tile_done, m + 1)
                    {"V": after_v, "P": after_p, "CC": after_cc, "R": after_r}[name[:-1]](i, m)
                if name[:-1] == "V":
                    gates(i)

            for n, k in enumerate(MIX_ORDER):
                if n == 0:
                    act.wait_ge(o_done, 4 * HEADS)
                if n == 2:
                    act.wait_ge(tile_done, M_OUT)
                if k < 4:
                    act.wait_ge(y_gated, k + 1)
                elif k < 6:
                    act.wait_ge(*main_freed(M_OF[f"CB{k - 4}"]))
                src, shape = mix_block(k)
                act.activation(shape(mix_parts(k)[0]), src, ACT.Copy).then_inc(mix_hi, 1)

            def residual_squares(m0, acc_made, sq_made, nth):
                def square(i, b):
                    act.wait_ge(main_free[1 - b], i + ((m0 + b) // 2 + 1))
                    act.wait_ge(acc_made, i * 2 + (b + 1))
                    xk = X[:, bass.ds(i * 2 + b, 1), :]
                    act.activation(sq2[:, :].unsqueeze(1), xk, ACT.Square).then_inc(sq_made, 1)
                    if nth == 0:
                        act.activation(xg[:, bass.ds(i * 2 + b, 1), :], xk, ACT.Copy,
                                       scale=gain2[:, bass.ds(i * 2 + b, 1)]).then_inc(xg_made, 1)

                with act.Fori(0, KT // 2 - 1) as i:
                    for b in range(2):
                        square(i, b)
                square(KT // 2 - 1, 0)
                act.wait_ge(acc_made, KT)
                act.wait_ge(res_half, nth + 1)
                act.activation(sq2[:, 0:HALF], X[:, KT - 1, 0:HALF], ACT.Square).then_inc(sq_last, 1)
                act.wait_ge(main_free[0], (m0 + KT - 1) // 2 + 1)
                act.activation(sq2[:, HALF:N], X[:, KT - 1, HALF:N], ACT.Square).then_inc(sq_last, 1)

            residual_squares(M_OUT, acc2_made, sq2_made, 0)
            for half in range(2):
                cols = slice(half * HALF, (half + 1) * HALF)
                act.wait_ge(sums2_done, half + 1)
                rsqrt(rs2[:, cols], sm[:, half, :], D, rs2_made)
                act.activation(xg[:, KT - 1, cols], X[:, KT - 1, cols], ACT.Copy,
                               scale=gain2[:, KT - 1:KT]).then_inc(xg_made, 1)
            act.wait_ge(tile_done, M_OUT + KT)
            for half in range(2):
                cols = slice(half * HALF, (half + 1) * HALF)
                for k in range(KT):
                    if k in H2_POOL:
                        act.wait_ge(h2_scaled_pool, half * len(H2_POOL) + H2_POOL.index(k) + 1)
                    else:
                        act.wait_ge(h2_scaled, half * len(H2_DVE) + H2_DVE.index(k) + 1)
                    act.activation(h_hi[:, k, cols], xg[:, k, cols], ACT.Identity, bias=mods[:, 1, k:k + 1]).then_inc(hid_hi, 1)

            def hidden(c):
                with act.Fori(0, KT // 2) as j:
                    for b in range(2):
                        act.wait_ge(tile_done, j * 2 + (c * (2 * KT) + (M_MLP + b + 1)))
                        act.wait_ge(lo_made, j * 2 + (c * KT + (LO_HID + b - 1)))
                        act.activation(relu[:, b:b + 1, :], main[:, 1 - b:2 - b, :], ACT.Relu).then_inc(main_free[1 - b], 1)
                        act.wait_ge(main_free[1 - b], j + (c * KT + ((M_MLP + b) // 2 + 1)))
                        act.activation(a_hi[:, bass.ds(j * 2 + b, 1), :], relu[:, b:b + 1, :], ACT.Square).then_inc(hid_hi, 1)

            with act.Fori(0, NFC - 1) as c:
                hidden(c)
            hidden(NFC - 1)

            act.wait_ge(lo_made, LO_HID + NFC * KT)
            residual_squares(M_MLP + (2 * NFC - 1) * KT, acc3_made, sq3_made, 1)
            for half in range(2):
                act.wait_ge(sums3_done, half + 1)
                rsqrt(rs2[:, half * HALF:(half + 1) * HALF], sm[:, half, :], D, rs3_made)
            for half in range(2):
                cols = slice(half * HALF, (half + 1) * HALF)
                for k in range(OUT_DVE, KT):
                    act.wait_ge(out_scaled, half * (KT - OUT_DVE) + k - OUT_DVE + 1)
                    act.activation(X[:, k, cols], X[:, k, cols], ACT.Copy, scale=one_col("fw", k)).then_inc(out_made_act, 1)

        @block.vector
        def _(dve):
            link = chain(dve, dve_chain)
            tt, ts, stt = dve.tensor_tensor, dve.tensor_scalar, dve.scalar_tensor_tensor

            dve.wait_ge(c_exp, 1)
            link(ts(csig[:, :], csig[:, :], 1.0, None, ALU.add))
            link(dve.reciprocal(csig[:, :], csig[:, :]))
            tt(silu_c[:, :], csig[:, :], col("cc"), ALU.mult).then_inc(c_ready, 1)

            def modulation(j):
                s = S_OF[("turn", j)]
                dve.wait_ge(small_done, s + 1)
                for q in range(2):
                    i = 2 * j + q
                    ts(ab1[:, i, 0:2], sm[:, s % 2, 4 * q:4 * q + 2], one_col("bmod", i), None, ALU.add)
                    ins = ts(ab1[:, i, 2:4], sm[:, s % 2, 4 * q + 2:4 * q + 4], one_col("bmod", KT + i), 1.0, ALU.add, ALU.add)
                ins.then_inc(small_free[s % 2], 1)
                dve.wait_ge(*small_freed(s))
                ts(ab1[:, 2 * j, 2:4], ab1[:, 2 * j, 2:4], one_col("n1", 2 * j), None, ALU.mult)
                link(ts(ab1[:, 2 * j + 1, 2:4], ab1[:, 2 * j + 1, 2:4], one_col("n1", 2 * j + 1), None, ALU.mult))

            for k in range(KT - 1):
                dve.wait_ge(sq1_made, k + 1)
                if k == 0:
                    ins = dve.tensor_copy(acc1[:, :], sq1[:, 0, :])
                else:
                    ins = tt(acc1[:, :], acc1[:, :], sq1[:, k % 2, :], ALU.add)
                ins.then_inc(acc1_made, 1)
                dve.wait_ge(acc1_made, k + 1)
                if k == 3:
                    modulation(0)
            modulation(1)
            def low1(k):
                dve.wait_ge(h1_hi, k + 1)
                dve.wait_ge(small_done, S_OF[("rows", 2 + k // 4)] + 1)
                tt(a_lo[:, k, :], xs[:, k, 0:N], a_hi[:, k, :].bitcast(F32), ALU.subtract)
                tt(c_lo[:, k, :], xs[:, k, N:NA], c_hi[:, k, :].bitcast(F32), ALU.subtract).then_inc(h1_lo, 1)

            dve.wait_ge(rs1_made, 1)
            last = tt(xs[:, 0, :], xs[:, 0, :], rs1[:, :], ALU.mult)
            for j in range(KT):
                link(last)
                if j in (4, 6):
                    modulation(j // 2)
                ts(xs[:, j, N:NA], xs[:, j, N:NA], ab1[:, j, 3:4], ab1[:, j, 1:2], ALU.mult, ALU.add)
                ts(xs[:, j, 0:N], xs[:, j, 0:N], ab1[:, j, 2:3], ab1[:, j, 0:1], ALU.mult, ALU.add).then_inc(h1_made, 1)
                if j < KT - 1:
                    last = tt(xs[:, j + 1, :], xs[:, j + 1, :], rs1[:, :], ALU.mult)
                low1(j)

            def context_state(p):
                s = S_OF[("cs", p)]
                dve.wait_ge(small_done, s + 1)
                dve.tensor_copy(state[:, p:p + 3:2, :], sm[:, s % 2, 0:2 * DV].rearrange("p (d e) -> p d e", d=2)).then_inc(small_free[s % 2], 1)
                dve.wait_ge(*small_freed(s))

            def updates(p, g, side):
                if side == 0:
                    return
                s = S_OF[("u", p, g, 1)]
                assert S_OF[("u", p, g, 0)] == s - 1
                dve.wait_ge(small_done, s + 1)
                order = [[4 * g + q for q in range(5)], [NCH - 1 - 4 * g - q for q in range(5)]]
                if g == 0:
                    if p == 1:
                        dve.wait_ge(o_done, 8)
                    for d in range(2):
                        made = link.mark(dve.tensor_copy(tst[:, d, order[d][0], :], state[:, 2 * d + p, :]))
                    dve.wait_ge(dve_chain, made)
                made = [0, 0]
                for q in range(4):
                    for d in range(2):
                        dp, n = 2 * d + p, order[d][q]
                        bank = (s - 1 + n % 2) % 2
                        if made[d]:
                            dve.wait_ge(dve_chain, made[d])
                        if 4 * g + q == NCH - 1:
                            continue
                        ins = stt(out=tst[:, d, order[d][q + 1], :], in0=tst[:, d, n, :], scalar=decay[:, dp, n:n + 1],
                                  in1=sm[:, bank, (2 * d + q // 2) * DV:(2 * d + q // 2 + 1) * DV], op0=ALU.mult, op1=ALU.add)
                        if q == 3 or (4 * g + q == NCH - 2):
                            ins.then_inc(small_free[bank], 1)
                        else:
                            made[d] = link.mark(ins)
                for bank in range(2):
                    dve.wait_ge(*small_freed(s - 1 + bank))
                for d in range(2):
                    dp, n = 2 * d + p, min(order[d][0], order[d][3])
                    block = tst[:, d, n:n + 4, :]
                    tt(block, block, decay[:, dp, n:n + 4].unsqueeze(2).broadcast_to([P, 4, DV]),
                       ALU.mult).then_inc(states_made, 1)

            def scores(h, j):
                s = S_OF[("A", h, j)]
                dve.wait_ge(small_done, s + 1)
                for dst, mask, d in ((a_f, "maskf", 0), (a_b, "maskb", 1)):
                    ins = dve.copy_predicated(dst[:, :, :], col(mask).bitcast(U32).unsqueeze(1).broadcast_to([P, 2, P]),
                                              sm[:, s % 2, 2 * d * P:2 * (d + 1) * P].rearrange("p (t q) -> p t q", t=2))
                ins.then_inc(small_free[s % 2], 1)
                dve.wait_ge(*small_freed(s))
                if 4 * h + j >= 2:
                    dve.wait_ge(o_done, 4 * h + j - 1)
                tt(a_sum[:, j % 2, :, :], a_f[:, :, :], a_b[:, :, :], ALU.add).then_inc(a_ready, 1)
                dve.wait_ge(a_ready, 4 * h + j + 1)

            def head_sums(h, i):
                if i == 1:
                    dve.wait_ge(rso_made, 2 * (h + 1))
                    tt(y_gla(h), by_tile(ob[:, :]), by_tile(rso[:, :]), ALU.mult).then_inc(y_normed, 1)
                    dve.wait_ge(y_normed, h + 1)

            def mod_product(g):
                s = S_OF[("md", g)]
                dve.wait_ge(small_done, s + 1)
                a = COLS["bmod"][0] + (2 + g) * KT
                tt(mods[:, g, :], sm[:, s % 2, 0:KT], small[:, a:a + KT], ALU.add).then_inc(small_free[s % 2], 1)
                dve.wait_ge(*small_freed(s))
                if g == 2:
                    link(stt(out=gain2[:, :], in0=mods[:, 2, :], scalar=1.0, in1=col("n2"), op0=ALU.add, op1=ALU.mult))

            jobs = {"cs": context_state, "u": updates, "A": scores, "ns": head_sums, "md": mod_product}

            def gates(j):
                d, dp, m = j % 2, 2 * (j % 2) + j // 2, M_OF[f"g{j}"]
                dve.wait_ge(tile_done, m + 1)
                if j >= 1:
                    dve.wait_ge(gate_exp, j)
                ts(t1[:, 0:N], main[:, m % 2, :], one_col("gb", dp), 0.0, ALU.add, ALU.min)
                ts(t1[:, N:NA], ob[:, (m % 2) * HALF:(m % 2) * HALF + NC], one_col("gb", dp), 0.0, ALU.add,
                   ALU.min).then_inc(gate_min, 1)
                for n in IN_GATES[j]:
                    add_modulation(n)
                dve.wait_ge(gate_min, j + 1)
                dve.wait_ge(gate_log, j + 1)
                link(tt(t1[:, :], t1[:, :], t2[:, :], ALU.subtract))
                dve.wait_ge(masks_made, 1)
                link(dve.tensor_tensor_scan(out=t2[:, :], data0=gmask[:, :], data1=t1[:, :], initial=0.0,
                                            op0=ALU.mult, op1=ALU.add))
                if d == 0:
                    chunks = t2[:, 0:N].rearrange("p (n t) -> p n t", t=CH)
                    tt(t1[:, 0:N].rearrange("p (n t) -> p n t", t=CH), chunks,
                       chunks[:, :, CH - 1:CH].broadcast_to([P, NCH, CH]), ALU.subtract)
                    ts(t1[:, N:NA], t2[:, N:NA], t2[:, NA - 1:NA], None, ALU.subtract).then_inc(gate_dif, 1)
                else:
                    tt(t1[:, :], t2[:, :], t1[:, :], ALU.subtract).then_inc(gate_dif, 1)
                dve.wait_ge(gate_dif, j + 1)

            def add_modulation(n):
                g, k = n // KT, n % KT
                dve.wait_ge(mbuf_loaded[n % 2], 16 * (n // 2 + 1))
                if k == 0:
                    if g >= 1:
                        dve.wait_ge(small_done, S_OF[("md", g - 1)] + 1)
                    ins = ts(macc[:, :], mbuf[:, n % 2, :], silu_c[:, 2 * k:2 * k + 1], None, ALU.mult)
                else:
                    dve.wait_ge(mod_taken, n)
                    ins = stt(out=macc[:, :], in0=mbuf[:, n % 2, :], scalar=silu_c[:, 2 * k:2 * k + 1],
                              in1=macc[:, :], op0=ALU.mult, op1=ALU.add)
                ins.then_inc(mod_taken, 1)

            def after_k(p, m):
                dve.wait_ge(gate_exp, 2 * p + 2)
                for d in range(2):
                    ins = tt(ku[:, 2 * d + p, :], main[:, m % 2, :], ku[:, 2 * d + p, :], ALU.mult)
                ins.then_inc(main_free[m % 2], 1)
                for d in range(2):
                    ins = tt(kuc[:, 2 * d + p, :], ob[:, (m % 2) * HALF:(m % 2) * HALF + NC], kuc[:, 2 * d + p, :], ALU.mult)
                ins.then_inc(ctx_free[m % 2], 1)

            def after_q(p, m):
                for d in range(2):
                    ins = stt(out=qe[:, 2 * d + p, :], in0=main[:, m % 2, :], scalar=float(DK) ** -0.5,
                              in1=qe[:, 2 * d + p, :], op0=ALU.mult, op1=ALU.mult)
                ins.then_inc(main_free[m % 2], 1)

            def after_p(i, m):
                dve.wait_ge(*main_freed(m))
                dve.wait_ge(masks_made, 2)
                if i == 1:
                    dve.wait_ge(summed, 1)
                link(dve.tensor_tensor_scan(out=cpad[:, :, :].rearrange("p s t -> p (s t)"),
                                            data0=pmask[:, :, :].rearrange("p s t -> p (s t)"),
                                            data1=upad[:, :, :].rearrange("p s t -> p (s t)"), initial=0.0,
                                            op0=ALU.mult, op1=ALU.add))
                y = ypool[:, i, :].rearrange("p (s t) -> p s t", t=SEG)
                for r in range(2):
                    rows, w = slice(64 * r, 64 * r + 64), WINDOWS[2 * i + r]
                    last = tt(y[rows], cpad[rows, :, 8 + w // 2:8 + w // 2 + SEG], cpad[rows, :, 8 - w // 2:8 - w // 2 + SEG],
                              ALU.subtract)
                last.then_inc(summed, 1)

            def after_ch(i, m):
                dve.wait_ge(*main_freed(M_OF[f"CC{i}"]))
                z = zpad[:, :, 1:1 + SEG]
                tt(z, z, main[:, m % 2, :].rearrange("p (s t) -> p s t", t=SEG), ALU.mult).then_inc(main_free[m % 2], 1)
                dve.wait_ge(*main_freed(m))
                y = yconv[:, i, :].rearrange("p (s t) -> p s t", t=SEG)
                link(ts(y, zpad[:, :, 0:SEG], one_col("cw", 3 * i), None, ALU.mult))
                for j in (1, 2):
                    link(stt(out=y, in0=zpad[:, :, j:j + SEG], scalar=one_col("cw", 3 * i + j), in1=y,
                             op0=ALU.mult, op1=ALU.add))

            def after_cb(i, m):
                tt(yconv[:, i, :], main[:, m % 2, :], yconv[:, i, :], ALU.mult).then_inc(main_free[m % 2], 1)

            def after_r(h, m):
                dve.wait_ge(r_log, h + 1)
                stt(out=rsig[:, :], in0=main[:, m % 2, :], scalar=0.0, in1=rsig[:, :], op0=ALU.min,
                    op1=ALU.subtract).then_inc(r_min, 1)
                dve.wait_ge(r_sig, h + 1)
                tt(rsig[:, :], main[:, m % 2, :], rsig[:, :], ALU.mult).then_inc(main_free[m % 2], 1)
                dve.wait_ge(*main_freed(m))
                stt(out=y_gla(h), in0=y_gla(h), scalar=col("gnw"), in1=by_tile(rsig[:, :]), op0=ALU.mult,
                    op1=ALU.mult).then_inc(y_gated, 1)

            after = {"K": after_k, "Q": after_q, "P": after_p, "CH": after_ch, "CB": after_cb, "R": after_r}
            for t, name in enumerate(PROJ):
                for k in range(KT):
                    for job in PLAN.get((t, k), ()):
                        if job[0] in jobs:
                            jobs[job[0]](*job[1:])
                    if KT * t + k in MOD_SLOT:
                        add_modulation(MOD_SLOT[KT * t + k])
                m, i = M_OF[name], int(name[-1])
                if name == "P0":
                    dve.wait_ge(pads_made, 1)
                if name[:-1] in after:
                    dve.wait_ge(tile_done, m + 1)
                    after[name[:-1]](i, m)
                if name[:-1] == "V":
                    gates(i)

            for n, k in enumerate(MIX_ORDER):
                dve.wait_ge(mix_hi, n + 1)
                src, shape = mix_block(k)
                hi, lo = mix_parts(k)
                tt(shape(lo), src, shape(hi.bitcast(F32)), ALU.subtract).then_inc(lo_made, 1)

            def residual(m0, g, acc_made, sq_made):
                dve.memset(acc2[:, :], 0.0).then_inc(acc_made, 1)
                dve.wait_ge(acc_made, 1)

                def add(i, b):
                    dve.wait_ge(tile_done, i * 2 + (m0 + b + 1))
                    xk = X[:, bass.ds(i * 2 + b, 1), :]
                    stt(out=xk, in0=main[:, 1 - b:2 - b, :], scalar=mods[:, g, bass.ds(i * 2 + b, 1)], in1=xk,
                        op0=ALU.mult, op1=ALU.add).then_inc(main_free[1 - b], 1)
                    dve.wait_ge(sq_made, i * 2 + (b + 1))
                    tt(acc2[:, :], acc2[:, :], sq2[:, :], ALU.add).then_inc(acc_made, 1)
                    dve.wait_ge(acc_made, i * 2 + (b + 2))

                with dve.Fori(0, KT // 2 - 1) as i:
                    for b in range(2):
                        add(i, b)
                add(KT // 2 - 1, 0)
                k = KT - 1
                for half, (done, n, s_out) in enumerate(((half_done, 1 if m0 == M_OUT else 2, res_half),
                                                         (tile_done, m0 + KT, main_free[0]))):
                    cols = slice(half * HALF, (half + 1) * HALF)
                    dve.wait_ge(done, n)
                    stt(out=X[:, k, cols], in0=main[:, 0, cols], scalar=mods[:, g, k:k + 1], in1=X[:, k, cols],
                        op0=ALU.mult, op1=ALU.add).then_inc(s_out, 1)

            dve.wait_ge(x2_loaded[0], 16)
            dve.wait_ge(x2_loaded[1], 16)
            residual(M_OUT, 0, acc2_made, sq2_made)

            dve.wait_ge(main_free[0], (M_OUT + KT - 1) // 2 + 1)
            dve.wait_ge(res_half, 1)
            for half in range(2):
                cols = slice(half * HALF, (half + 1) * HALF)
                dve.wait_ge(rs2_made, half + 1)

                def low(k):
                    dve.wait_ge(hid_hi, half * KT + k + 1)
                    stt(out=h_lo[:, k, cols], in0=xg[:, k, cols], scalar=mods[:, 1, k:k + 1],
                        in1=h_hi[:, k, cols].bitcast(F32), op0=ALU.add, op1=ALU.subtract).then_inc(lo_made, 1)

                lows = 0
                for n, k in enumerate(H2_DVE):
                    dve.wait_ge(xg_made, k + 1)
                    tt(xg[:, k, cols], xg[:, k, cols], rs2[:, cols], ALU.mult).then_inc(h2_scaled, 1)
                    if n >= 1:
                        low(lows)
                        lows += 1
                for k in range(lows, KT):
                    low(k)

            def hidden(c):
                with dve.Fori(0, KT // 2) as j:
                    for b in range(2):
                        dve.wait_ge(hid_hi, j * 2 + (c * KT + (2 * KT + b + 1)))
                        r = relu[:, b:b + 1, :]
                        tt(r, r, r, ALU.mult).then_inc(hid_sq, 1)
                        dve.wait_ge(hid_sq, j * 2 + (c * KT + (b + 1)))
                        tt(a_lo[:, bass.ds(j * 2 + b, 1), :], r, a_hi[:, bass.ds(j * 2 + b, 1), :].bitcast(F32),
                           ALU.subtract).then_inc(lo_made, 1)

            with dve.Fori(0, NFC - 1) as c:
                hidden(c)
                with dve.Fori(0, KT // 2) as j:
                    for b in range(2):
                        dve.wait_ge(tile_done, j * 2 + c * (2 * KT) + (M_MLP + KT + b + 1))
                        xk = X[:, bass.ds(j * 2 + b, 1), :]
                        stt(out=xk, in0=main[:, 1 - b:2 - b, :], scalar=mods[:, 3, bass.ds(j * 2 + b, 1)], in1=xk,
                            op0=ALU.mult, op1=ALU.add).then_inc(main_free[1 - b], 1)
            hidden(NFC - 1)
            dve.wait_ge(lo_made, LO_HID + NFC * KT)
            residual(M_MLP + (2 * NFC - 1) * KT, 3, acc3_made, sq3_made)

            dve.wait_ge(main_free[0], (M_MLP + 2 * NFC * KT - 1) // 2 + 1)
            for half in range(2):
                cols = slice(half * HALF, (half + 1) * HALF)
                dve.wait_ge(rs3_made, half + 1)
                for k in range(OUT_DVE):
                    stt(out=X[:, k, cols], in0=X[:, k, cols], scalar=one_col("fw", k), in1=rs2[:, cols], op0=ALU.mult,
                        op1=ALU.mult).then_inc(out_made, 1)


def kernel(**inputs):
    import numpy as np
    from concourse import bacc
    from concourse.bass_utils import run_bass_kernel_spmd

    a = {k: np.asarray(v) for k, v in inputs.items()}

    def tiles(w):
        return w.reshape(KT, P, -1, P).transpose(2, 1, 0, 3).reshape(-1, P, KT * P)

    def by_feature(v):
        return v.reshape(-1, P).T

    w_in = a["w_in"][0]
    at = {}
    g_off = 2 * HEADS * DK + HEADS * DV
    rest = g_off + 2 * RANK
    for name, start in (("Q", 0), ("K", HEADS * DK), ("V", 2 * HEADS * DK), ("R", rest), ("CB", rest + HEADS * DV),
                        ("CC", rest + HEADS * DV + 256), ("CH", rest + HEADS * DV + 512), ("P", rest + HEADS * DV + 768)):
        at[name] = start
    stream = [tiles(w_in[:, at[n[:-1]] + P * int(n[-1]):at[n[:-1]] + P * int(n[-1]) + P]) for n in PROJ]
    stream.append(tiles(a["w_out"][0]))
    for c in range(NFC):
        cols = slice(c * CK, (c + 1) * CK)
        stream.append(tiles(a["w_mlp1"][0][:, cols]))
        stream.append(tiles(a["w_mlp2"][0][cols, :]))

    w_mod = a["w_mod"][0]
    wm1 = w_mod[:, :2 * D].reshape(KT, P, 2, KT // 2, 2, P).transpose(3, 1, 0, 4, 2, 5).reshape(KT // 2, P, 4 * KT * P)
    wm2 = w_mod[:, 2 * D:].reshape(KT, P, 4, D).transpose(2, 0, 1, 3)

    token = np.arange(P)
    same = (token[:, None] // CH) == (token[None, :] // CH)
    t = np.arange(SEG)
    inv = np.zeros((P, 2, SEG), np.float32)
    for g, w in enumerate(WINDOWS):
        count = np.clip(t + w // 2, 0, SEG) - np.clip(t - w // 2, 0, SEG)
        inv[64 * (g % 2):64 * (g % 2) + 64, g // 2] = np.float32(1) / count.astype(np.float32)
    pw = np.zeros((P, 2, P), np.float32)
    for g in range(4):
        r = slice(64 * (g % 2), 64 * (g % 2) + 64)
        pw[r, g // 2, r] = a["pool_w"][0, g]
    parts = {
        "cc": np.stack([by_feature(a["c"][0]), by_feature(a["c_ctx"])], axis=2),
        "bmod": by_feature(a["b_mod"][0]), "n1": by_feature(a["norm1_w"][0]), "n2": by_feature(a["norm2_w"][0]),
        "fw": by_feature(a["final_norm_w"]), "gb": by_feature(a["gla_gate_b"][0].reshape(-1)),
        "gnw": by_feature(a["gla_norm_w"][0]),
        "cw": a["conv_w"][0].reshape(3, 2, P).transpose(2, 1, 0),
        "ps": by_feature(a["pool_scale"][0]),
        "eps": np.full((P, 1), EPS), "one": np.ones((P, 1)), "inv": inv,
        "ident": np.eye(P), "ones": np.ones((P, P)),
        "maskf": same & (token[:, None] <= token[None, :]), "maskb": same & (token[:, None] >= token[None, :]),
        "pw": pw,
    }
    small = np.zeros((P, NSMALL), np.float32)
    for name, (lo, hi) in COLS.items():
        small[:, lo:hi] = np.asarray(parts[name], np.float32).reshape(P, hi - lo)
    gw = np.zeros((2 * RANK, 2, 2 * P), np.float32)
    for d in range(2):
        gw[d * RANK:(d + 1) * RANK, d] = a["gla_gate_w"][0, d]

    arrays = {
        "wstream": np.concatenate(stream), "wg_in": w_in[:, g_off:rest].reshape(KT, P, 32).transpose(1, 0, 2).reshape(P, -1),
        "wm1": wm1, "wm2": wm2, "xt": a["x"][0].T.reshape(KT, P, N),
        "ct": a["ctx"][0].T.reshape(KT, P, NC).transpose(1, 0, 2), "small_in": small, "gw_in": gw.reshape(2 * RANK, -1),
    }
    arrays = {k: np.ascontiguousarray(v) for k, v in arrays.items()}
    nc = bacc.Bacc("TRN2", target_bir_lowering=False, num_devices=1)
    args = [nc.dram_tensor(k, v.shape, mybir.dt.from_np(v.dtype), kind="ExternalInput").ap() for k, v in arrays.items()]
    out = nc.dram_tensor("out", (KT, P, N), F32, kind="ExternalOutput").ap()
    hybrid_trunk(nc, *args, out)
    r = run_bass_kernel_spmd(nc, [arrays], core_ids=[0])
    return r.results[0]["out"].reshape(D, N).T.reshape(1, N, D)
```

```python
from contextlib import ExitStack

import concourse.bass as bass
from concourse import mybir

F32 = mybir.dt.float32
F32R = mybir.dt.float32r
U8 = mybir.dt.uint8
U32 = mybir.dt.uint32
ALU = mybir.AluOpType
ACT = mybir.ActivationFunctionType

P = 128
D = 1024
KT = D // P
N = 1024
NC = 256
NA = N + NC
HALF = 512
HEADS, DK, DV = 4, 64, 128
CH = 64
NCH = N // CH
TT = N // P
SEG = 64
NSEG = N // SEG
PADW = SEG + 16
WINDOWS = (2, 4, 8, 16)
RANK = 16
TAU = 16.0
EPS = 1e-6
NFC = 4
CK = D
KIB = 1024

PROJ = ["V0", "V1", "V2", "V3", "K0", "K1", "Q0", "Q1", "P0", "P1", "CC0", "CH0", "CB0",
        "R0", "R1", "CC1", "CH1", "R2", "R3", "CB1"]
NPROJ = len(PROJ)
MAIN = ["G", "V0", "g0", "V1", "g1", "V2", "g2", "V3", "g3"] + PROJ[4:]
M_OF = {name: m for m, name in enumerate(MAIN)}
M_OUT = len(MAIN)
M_MLP = M_OUT + KT
T_OUT = NPROJ
T_MLP = T_OUT + KT
NSTREAM = T_MLP + 2 * NFC * KT
LO_H2 = KT
LO_HID = LO_H2 + 2 * KT

PLAN = {}


def put(tile, slot, *job):
    PLAN.setdefault((tile, slot), []).append(job)


def put_all(first, step, *jobs):
    for n, job in enumerate(jobs):
        put((first + step * n) // KT, (first + step * n) % KT, *job)


for _h in range(HEADS):
    for _i, _s in enumerate((2, 5, 7)):
        put(_h + 1, _s, "vt", _h, _i)
put_all(5 * 8 + 4, 1, ("kt", 0, 0), ("kt", 0, 1), ("kt", 1, 0), ("kt", 1, 1), ("kc", 0), ("cs", 0))
put_all(6 * 8 + 2, 1, ("u", 0, 0), ("u", 0, 1), ("kc", 1), ("cs", 1), ("u", 0, 2), ("u", 0, 3))
put_all(7 * 8, 2, ("u", 1, 0), ("u", 1, 1), ("u", 1, 2), ("u", 1, 3))
put_all(8 * 8 + 1, 2, ("kt", 2, 0), ("kt", 2, 1), ("kt", 3, 0), ("kt", 3, 1))
HEAD_AT = (9 * 8 + 5, 11 * 8, 13 * 8 + 1, 14 * 8 + 6)
UPD_AT = (0, 0, 11 * 8 + 2, 12 * 8)
CHAIN_AT = (7 * 8 + 1, 9 * 8 - 2, 11 * 8 + 7, 12 * 8 + 7)
for _h in range(HEADS):
    put_all(CHAIN_AT[_h], 2, ("ch", _h, 0), ("ch", _h, 1), ("ch", _h, 2))
    put_all(CHAIN_AT[_h] + 5, 1, ("mx", _h, 0), ("mx", _h, 1))
    put_all(HEAD_AT[_h], 1, ("A", _h, 0, 0), ("A", _h, 0, 1))
    put_all(HEAD_AT[_h] + 3, 1, ("A", _h, 1, 0), ("A", _h, 1, 1))
    put_all(HEAD_AT[_h] + 4, 3, ("O", _h, 0), ("O", _h, 1))
    put_all(HEAD_AT[_h] + 10, 1, ("ns", _h, 0), ("ns", _h, 1))
    _r = PROJ.index(f"R{_h}") + 1
    put(_r, 3, "rl", _h)
    put(_r, 5, "rg", _h)
    if _h >= 2:
        put_all(UPD_AT[_h], 1, *[("u", _h, _n) for _n in range(4)])
for _i in range(2):
    put(10, 5 + _i, "pl", 0, _i)
    put(11, 5 + 2 * _i, "pl", 1, _i)
IN_GATES = ((0, 1), (2, 3, 4), (5, 6, 7), (8, 9, 10))
MOD_SLOT = {41 + 5 * _i // 2: 11 + _i for _i in range(21)}
for _g, _q in enumerate((27, 53, 73, 93)):
    put(_q // 8, _q % 8, "md", _g)
for _jobs in PLAN.values():
    _jobs.sort(key=lambda job: (job[0] != "O"))

MIX_ORDER = [0, 1, 6, 7, 4, 2, 3, 5]
NORM1_DVE = 5
H_ORDER = (4, 5, 6, 7, 0, 1, 2, 3)
H2_POOL = ((6,), (6, 0, 3))
H2_DVE = tuple(tuple(k for k in H_ORDER if k not in H2_POOL[half]) for half in range(2))
OUT_DVE = 5
OUT_ORDER = (0, 1, 5, 2, 3, 6, 4, 7)
BANKED = ("vt", "kt", "kc", "cs", "u", "A", "ns", "pl", "md")
SMALL = [(_name, _j) for _j in range(KT // 2) for _name in ("rows", "turn")]
for _t in range(NPROJ):
    for _s in range(KT):
        SMALL += [job for job in PLAN.get((_t, _s), ()) if job[0] in BANKED]
S_OF = {job: s for s, job in enumerate(SMALL)}

COLS = {}
_at = 0
for _name, _w in (("cc", 2 * KT), ("bmod", 6 * KT), ("n1", KT), ("n2", KT), ("fw", KT), ("gb", 4),
                  ("gnw", 1), ("cw", 6), ("ps", 2), ("eps", 1), ("one", 1),
                  ("ident", P), ("ones", P), ("inv", 2 * SEG), ("maskf", P), ("maskb", P), ("pw", 2 * P)):
    COLS[_name] = (_at, _at + _w)
    _at += _w
NSMALL = _at
NFIRST = COLS["inv"][0]


def hybrid_trunk(nc, wstream, wg_in, wm1, wm2, xt, ct, small_in, gw_in, out):
    ctx = ExitStack()
    with ctx:
        cursor = [(nc.sbuf_base + 63) // 64 * 64]

        def at(name, shape, dt, offset):
            return nc.alloc_sbuf_tensor_at(name, shape, dt, offset=offset)

        def area(nbytes):
            start = cursor[0]
            cursor[0] += (nbytes + 31) // 32 * 32
            assert cursor[0] <= nc.sbuf_usable_end, cursor
            return start

        raw = at("raw", [P, 2, KT, P], F32, area(8 * KIB))
        w_hi = at("w_hi", [P, 2, KT, P], F32R, area(8 * KIB))
        w_lo = at("w_lo", [P, 2, KT, P], F32R, area(8 * KIB))
        HA = area(64 * KIB)
        a_hi = at("a_hi", [P, KT, N], F32R, HA)
        a_lo = at("a_lo", [P, KT, N], F32R, HA + 32 * KIB)
        wmod = at("wmod", [P, KT // 2, KT, HALF], F32, HA)
        small = at("small", [P, NSMALL], F32, area(NSMALL * 4))

        def col(name, rows=P):
            a, b = COLS[name]
            return small[0:rows, a:b]

        def one_col(name, i, rows=slice(0, P)):
            return small[rows, COLS[name][0] + i:COLS[name][0] + i + 1]

        ident, ones = col("ident"), col("ones")
        silu_c = at("silu_c", [P, 2 * KT], F32, area(64))
        csig = at("csig", [P, 2 * KT], F32, area(64))
        ab1 = at("ab1", [P, KT, 4], F32, area(KT * 16))
        mods = at("mods", [P, 4, KT], F32, area(KT * 16))
        gain2 = at("gain2", [P, KT], F32, area(KT * 4))
        decay = at("decay", [P, HEADS, NCH], F32, area(4 * NCH * 4))
        STATE = area(4 * P * 4)
        state = at("state", [P, HEADS, DV], F32, STATE)
        wg_parts = at("wg_parts", [P, KT, 4 * RANK], F32R, STATE)
        PM = area(NSEG * PADW)
        pmask = at("pmask", [P, NSEG, PADW], U8, PM)
        wg = at("wg", [P, KT, 32], F32, PM)
        EARLY = area(4 * KIB)
        gw = at("gw", [P, HEADS, P], F32, EARLY)
        gw_parts = at("gw_parts", [P, HEADS, P], F32R, EARLY)
        gmask = at("gmask", [P, NA], U8, EARLY + 2 * KIB)
        a_f = at("a_f", [P, 4, P], F32, EARLY)
        a_b = at("a_b", [P, 4, P], F32, EARLY + 2 * KIB)
        VCT1 = area(2 * KIB)
        vct1 = at("vct1", [P, HEADS * DV], F32, VCT1)
        a_sum = at("a_sum", [P, 4, P], F32, VCT1)

        ZB = area(16 * KIB)
        ZC = area(16 * KIB)
        ZA = area(16 * KIB)
        ZD = area(8 * KIB)
        ZE = area(16 * KIB)
        ZT = area(16 * KIB)
        ZF = cursor[0]
        assert nc.sbuf_usable_end - ZF >= 18 * KIB, nc.sbuf_usable_end - ZF
        xs = at("xs", [P, KT, NA], F32, ZB)
        sq1 = at("sq1", [P, 2, NA], F32, ZA + 8 * KIB)
        acc1 = at("acc1", [P, NA], F32, ZA + 28 * KIB)
        rs1 = at("rs1", [P, NA], F32, ZF)
        mrow = at("mrow", [2, 2, HALF], F32, ZF + 5 * KIB)
        c_hi = at("c_hi", [P, KT, NC], F32R, ZT)
        c_lo = at("c_lo", [P, KT, NC], F32R, ZT + 8 * KIB)
        qe = at("qe", [P, HEADS, N], F32, ZB)
        vtok = at("vtok", [P, TT, HEADS * DV], F32, ZC)
        ku = at("ku", [P, HEADS, N], F32, ZA)
        t1 = at("t1", [P, NA], F32, ZD)
        ktok = at("ktok", [P, 2, TT, P], F32, ZD)
        vtmp = at("vtmp", [P, NA], F32, ZE)
        mbuf = at("mbuf", [P, 2, N], F32, ZE + 8 * KIB)
        vct0 = at("vct0", [P, HEADS * DV], F32, ZE + 5 * KIB)
        ypool = at("ypool", [P, 2, N], F32, ZE)
        yconv = at("yconv", [P, 2, N], F32, ZE + 8 * KIB)
        tst = at("tst", [P, 2, NCH, DV], F32, ZT)
        zsb = at("zsb", [P, NA], F32R, ZF)
        kctok = at("kctok", [P, HEADS, 2, P], F32, ZF)
        kuc = at("kuc", [P, HEADS, NC], F32, ZF + 9 * KIB)
        macc = at("macc", [P, N], F32, ZF + 5 * KIB)
        t2 = at("t2", [P, NA], F32, ZF + 13 * KIB)
        gw_hi = at("gw_hi", [P, HEADS, P], F32R, ZF + 13 * KIB)
        upad = at("upad", [P, NSEG, PADW], F32, ZF)
        cpad = at("cpad", [P, NSEG, PADW], F32, ZF + 13 * KIB)
        zpad = at("zpad", [P, NSEG, SEG + 2], F32, ZF)
        rsig = at("rsig", [P, N], F32, ZF + 5 * KIB)
        sqo = at("sqo", [P, N], F32, ZF + 10 * KIB)
        rso = at("rso", [P, N], F32, ZF + 14 * KIB)
        early_hi = at("early_hi", [P, 2, N], F32R, ZA)
        early_lo = at("early_lo", [P, 2, N], F32R, ZA + 8 * KIB)
        X = at("X", [P, KT, N], F32, ZB)
        h_hi = at("h_hi", [P, KT, N], F32R, ZA)
        h_lo = at("h_lo", [P, KT, N], F32R, ZA + 32 * KIB)
        ZG = ZA + 64 * KIB
        assert nc.sbuf_usable_end - ZG >= 10 * KIB
        sq2 = at("sq2", [P, N], F32, ZG)
        acc2 = at("acc2", [P, N], F32, ZG + 4 * KIB)
        rs2 = at("rs2", [P, N], F32, ZG)
        xg = at("xg", [P, KT, N], F32, ZA + 32 * KIB)
        relu = at("relu", [P, 2, N], F32, ZG)

        main = ctx.enter_context(nc.psum_tensor("main", [P, 2, N], F32))
        ob = ctx.enter_context(nc.psum_tensor("ob", [P, N], F32))
        sm = ctx.enter_context(nc.psum_tensor("sm", [P, 2, HALF], F32))

        def sem(name):
            return ctx.enter_context(nc.semaphore(name))

        small_in_done = sem("small_loaded")
        masks_loaded = sem("masks_loaded")
        gw_loaded = sem("gw_loaded")
        gw_rounded = sem("gw_rounded")
        gw_split = sem("gw_split")
        z_copied = sem("z_copied")
        wg_loaded = sem("wg_loaded")
        wmod_loaded = [sem(f"wmod_loaded{j}") for j in range(KT // 2)]
        x_loaded = [sem(f"x_loaded{k}") for k in range(KT)]
        ctx_loaded = sem("ctx_loaded")
        raw_loaded = [sem("raw_loaded0"), sem("raw_loaded1")]
        mbuf_loaded = [sem("mbuf_loaded0"), sem("mbuf_loaded1")]
        x2_loaded = [sem("x2_loaded0"), sem("x2_loaded1")]
        out_stored = sem("out_stored")
        masks_made = sem("masks_made")
        pads_made = sem("pads_made")
        wg_split = sem("wg_split")
        hi_made = sem("hi_made")
        split_done = sem("split_done")
        tile_done = sem("tile_done")
        main_free = [sem("main_free0"), sem("main_free1")]
        ctx_free = [sem("ctx_free0"), sem("ctx_free1")]
        small_done = sem("small_done")
        small_free = [sem("small_free0"), sem("small_free1")]
        c_exp = sem("c_exp")
        c_ready = sem("c_ready")
        sq1_made = sem("sq1_made")
        acc1_made = sem("acc1_made")
        sums1_done = sem("sums1_done")
        rs1_made = sem("rs1_made")
        x_scaled_pool = sem("x_scaled_pool")
        h1_made = sem("h1_made")
        h1_hi = sem("h1_hi")
        h1_lo = sem("h1_lo")
        gate_min = sem("gate_min")
        gate_log = sem("gate_log")
        gate_dif = sem("gate_dif")
        gate_exp = sem("gate_exp")
        summed = sem("summed")
        pooled = sem("pooled")
        mod_taken = sem("mod_taken")
        a_ready = sem("a_ready")
        o_done = sem("o_done")
        sqo_made = sem("sqo_made")
        rso_made = sem("rso_made")
        y_normed = sem("y_normed")
        r_log = sem("r_log")
        r_min = sem("r_min")
        r_sig = sem("r_sig")
        y_gated = sem("y_gated")
        mix_hi = sem("mix_hi")
        half_done = sem("half_done")
        res_half = sem("res_half")
        sq_last = sem("sq_last")
        states_made = sem("states_made")
        states_decayed = sem("states_decayed")
        sq2_made = sem("sq2_made")
        acc2_made = sem("acc2_made")
        sums2_done = sem("sums2_done")
        rs2_made = sem("rs2_made")
        h2_scaled = sem("h2_scaled")
        h2_scaled_pool = sem("h2_scaled_pool")
        xg_made = sem("xg_made")
        hid_hi = sem("hid_hi")
        lo_made = sem("lo_made")
        hid_sq = sem("hid_sq")
        sq3_made = sem("sq3_made")
        acc3_made = sem("acc3_made")
        sums3_done = sem("sums3_done")
        rs3_made = sem("rs3_made")
        out_made = sem("out_made")
        out_scaled = sem("out_scaled")
        out_made_act = sem("out_made_act")
        dve_chain = sem("dve_chain")
        act_chain = sem("act_chain")
        pool_chain = sem("pool_chain")

        def chain(eng, s):
            count = [0]

            def link(ins):
                count[0] += 1
                ins.then_inc(s, 1)
                eng.wait_ge(s, count[0])
            return link

        def main_freed(m):
            return main_free[m % 2], m // 2 + 1

        def ctx_freed(m):
            return ctx_free[m % 2], m // 2 + 1

        def small_freed(s):
            return small_free[s % 2], s // 2 + 1

        def stream_free(t):
            return M_OF[PROJ[t]] + 1 if t < NPROJ else M_OUT + t - NPROJ + 1

        def chunks_of(n):
            return range(8 * (n // 2) + n % 2, 8 * (n // 2) + 8, 2)

        def xg_count(k, half):
            return k + 1 if k < KT - 2 else KT - 1 + 2 * half + k - (KT - 2)

        def by_tile(ap):
            return ap.rearrange("p (t e) -> p t e", e=DV)

        def y_gla(h):
            return vtok[:, :, h * DV:(h + 1) * DV]

        def mix_block(k):
            if k < 4:
                return y_gla(k), by_tile
            return (yconv[:, k - 4, :] if k < 6 else ypool[:, k - 6, :]), (lambda ap: ap)

        def mix_parts(k):
            n = MIX_ORDER.index(k)
            return (early_hi[:, n, :], early_lo[:, n, :]) if n < 2 else (a_hi[:, k, :], a_lo[:, k, :])

        block = ctx.enter_context(nc.Block())

        @block.sync
        def _(sp):
            sp.dma_start(small[:, 0:NFIRST], small_in[:, 0:NFIRST]).then_inc(small_in_done, 16)
            def load_wmod(j):
                sp.dma_start(wmod[:, j, :, :].rearrange("p k c -> p (k c)"), wm1[j]).then_inc(wmod_loaded[j], 16)

            def load_tile(t):
                if t >= 2:
                    sp.wait_ge(split_done, t - 1)
                sp.dma_start(raw[:, t % 2, :, :].rearrange("p k c -> p (k c)"), wstream[t]).then_inc(raw_loaded[t % 2], 16)

            def load_mod(n):
                if n >= 2:
                    sp.wait_ge(mod_taken, n - 1)
                sp.dma_start(mbuf[:, n % 2, :], wm2[n // KT, n % KT]).then_inc(mbuf_loaded[n % 2], 16)

            load_wmod(0)
            sp.dma_start(xs[:, :, N:NA], ct).then_inc(ctx_loaded, 16)
            for k in range(KT):
                sp.dma_start(xs[:, k, 0:N], xt[k]).then_inc(x_loaded[k], 16)
                if k == 2:
                    load_wmod(1)
            load_wmod(2)
            sp.dma_start(wg[:, :, :].rearrange("p k c -> p (k c)"), wg_in).then_inc(wg_loaded, 16)
            load_tile(0)
            load_wmod(3)
            sp.dma_start(gw[:, :, :].rearrange("r h c -> r (h c)"), gw_in).then_inc(gw_loaded, 16)
            sp.dma_start(small[:, NFIRST:NSMALL], small_in[:, NFIRST:NSMALL]).then_inc(masks_loaded, 16)
            for t in range(1, 4):
                load_tile(t)
            sp.wait_ge(h1_lo, KT)
            slot = {n: KT * (j + 1) + 1 for j, part in enumerate(IN_GATES) for n in part}
            slot.update({n: q for q, n in MOD_SLOT.items()})
            loads = [(slot[max(n - 2, 0)], 0, load_mod, n) for n in range(4 * KT)]
            loads += [(KT * (t - 3) + 3, 1, load_tile, t) for t in range(4, T_OUT + 2)]
            for _, _, load, n in sorted(loads, key=lambda x: (x[0], x[1], x[3])):
                load(n)
            sp.wait_ge(o_done, 2 * HEADS)
            sp.dma_start(X[:, 0:4, :], xt[0:4].rearrange("k p n -> p k n")).then_inc(x2_loaded[0], 16)
            load_tile(T_OUT + 2)
            sp.wait_ge(lo_made, KT)
            sp.dma_start(X[:, 4:8, :], xt[4:8].rearrange("k p n -> p k n")).then_inc(x2_loaded[1], 16)
            load_tile(T_OUT + 3)
            with sp.Fori(T_OUT // 2 + 2, NSTREAM // 2) as i:
                for b in range(2):
                    sp.wait_ge(split_done, i * 2 + (b - 1))
                    sp.dma_start(raw[:, b, :, :].rearrange("p k c -> p (k c)"),
                                 wstream[bass.ds(i * 2 + b, 1)].rearrange("a p c -> p (a c)")).then_inc(raw_loaded[b], 16)
            for half in range(2):
                cols = slice(half * HALF, (half + 1) * HALF)
                for k in OUT_ORDER:
                    if k < OUT_DVE:
                        sp.wait_ge(out_made, half * OUT_DVE + k + 1)
                    else:
                        sp.wait_ge(out_made_act, half * (KT - OUT_DVE) + k - OUT_DVE + 1)
                    sp.dma_start(out[k][:, cols], X[:, k, cols]).then_inc(out_stored, 16)
            sp.wait_ge(out_stored, 16 * 2 * KT)

        @block.gpsimd
        def _(pool):
            link = chain(pool, pool_chain)
            pool.wait_ge(small_in_done, 16)
            link(pool.memset(gmask[:, :], 1))
            pool.memset(gmask[:, 0:N + 1:CH], 0).then_inc(masks_made, 1)
            pool.wait_ge(wg_loaded, 16)
            hi, lo = wg_parts[:, :, 0:2 * RANK], wg_parts[:, :, 2 * RANK:4 * RANK]
            link(pool.tensor_scalar(hi, wg[:, :, :], 1.0, None, ALU.mult))
            pool.tensor_tensor(lo, wg[:, :, :], hi.bitcast(F32), ALU.subtract).then_inc(wg_split, 1)

            def split(b, n, linked):
                pool.tensor_tensor(w_hi[:, b, :, :], raw[:, b, :, :], ones.unsqueeze(1).broadcast_to([P, KT, P]),
                                   ALU.mult).then_inc(linked, 1)
                pool.wait_ge(linked, n)
                pool.tensor_tensor(w_lo[:, b, :, :], raw[:, b, :, :], w_hi[:, b, :, :].bitcast(F32),
                                   ALU.subtract).then_inc(split_done, 1)

            for t in range(NPROJ):
                pool.wait_ge(raw_loaded[t % 2], 16 * (t // 2 + 1))
                if t >= 2:
                    pool.wait_ge(tile_done, stream_free(t - 2))
                split(t % 2, t + 1, hi_made)
                if PROJ[t] == "P0":
                    pool.wait_ge(small_done, S_OF[("cs", 1)] + 1)
                    pool.wait_ge(gate_exp, HEADS)
                    pool.memset(a_f[:, :, :], 0.0)
                    pool.memset(a_b[:, :, :], 0.0)
                    pool.memset(upad[:, :, :], 0.0).then_inc(pads_made, 1)
                if t >= 2 and PROJ[t - 2] in ("P0", "P1"):
                    i = int(PROJ[t - 2][1])
                    pool.wait_ge(summed, i + 1)
                    pool.wait_ge(masks_loaded, 16)
                    y = ypool[:, i, :].rearrange("p (s t) -> p s t", t=SEG)
                    a = COLS["inv"][0] + i * SEG
                    link(pool.tensor_tensor(y, y, small[:, a:a + SEG].unsqueeze(1).broadcast_to([P, NSEG, SEG]), ALU.mult))
                    pool.tensor_tensor(y, y, upad[:, :, 9:9 + SEG], ALU.subtract).then_inc(pooled, 1)
                    if i == 1:
                        pool.wait_ge(pooled, 2)
                        pool.memset(zpad[:, :, :], 0.0).then_inc(pads_made, 1)
                if t == 0:
                    pool.wait_ge(rs1_made, 1)
                    for k in range(NORM1_DVE, KT):
                        pool.tensor_tensor(xs[:, k, :], xs[:, k, :], rs1[:, :], ALU.mult).then_inc(x_scaled_pool, 1)
                    pool.wait_ge(wg_split, 1)
                    link(pool.memset(pmask[:, :, :], 1))
                    pool.memset(pmask[:, :, 0], 0).then_inc(masks_made, 1)
            for t in (T_OUT, T_OUT + 1):
                pool.wait_ge(raw_loaded[t % 2], 16 * (t // 2 + 1))
                pool.wait_ge(tile_done, stream_free(t - 2))
                split(t % 2, t + 1, hi_made)
            def split_pairs(first, last):
                with pool.Fori(first, last) as i:
                    for b in range(2):
                        pool.wait_ge(raw_loaded[b], i * 16 + 16)
                        pool.wait_ge(tile_done, i * 2 + (b - 2 + M_OUT - T_OUT + 1))
                        split(b, i * 2 + (b + 1), hi_made)

            split_pairs(T_OUT // 2 + 1, T_MLP // 2)
            def scale_blocks(half):
                cols = slice(half * HALF, (half + 1) * HALF)
                pool.wait_ge(rs2_made, half + 1)
                for k in H2_POOL[half]:
                    pool.wait_ge(xg_made, xg_count(k, half))
                    pool.tensor_tensor(xg[:, k, cols], xg[:, k, cols], rs2[:, cols], ALU.mult).then_inc(h2_scaled_pool, 1)

            scale_blocks(0)
            for b in range(2):
                pool.wait_ge(raw_loaded[b], 16 * (T_MLP // 2 + 1))
                pool.wait_ge(tile_done, stream_free(T_MLP + b - 2))
                split(b, T_MLP + b + 1, hi_made)
            scale_blocks(1)
            split_pairs(T_MLP // 2 + 1, NSTREAM // 2)
            for half in range(2):
                cols = slice(half * HALF, (half + 1) * HALF)
                pool.wait_ge(rs3_made, half + 1)
                for k in range(OUT_DVE, KT):
                    pool.tensor_tensor(X[:, k, cols], X[:, k, cols], rs2[:, cols], ALU.mult).then_inc(out_scaled, 1)

        @block.tensor
        def _(pe):
            def of_a(k):
                return a_hi[:, k, :], a_lo[:, k, :]

            def of_h(k):
                return h_hi[:, k, :], h_lo[:, k, :]

            def product(bank, slot, parts, order=range(KT), ready=None, after=None):
                for n, k in enumerate(order):
                    if ready is not None:
                        ready(n, k)
                    first, last = n == 0, n == KT - 1
                    h, l = parts(k)
                    for w, x, begin, end in ((w_hi, h, first, False), (w_hi, l, False, False), (w_lo, h, False, last)):
                        for half in range(2):
                            ins = pe.matmul(main[:, bank, half * HALF:(half + 1) * HALF], w[:, slot, k, :],
                                            x[:, half * HALF:(half + 1) * HALF], start=begin, stop=end)
                    if after is not None and not last:
                        after(k)
                ins.then_inc(tile_done, 1)

            def half_product(bank, slot, parts, half, order=range(KT), ready=None, within=None):
                for n, k in enumerate(order):
                    if ready is not None:
                        ready(half, n)
                    if within is not None and n == 3:
                        within()
                    h, l = parts(k)
                    for w, x, begin, end in ((w_hi, h, n == 0, False), (w_hi, l, False, False),
                                             (w_lo, h, False, n == KT - 1)):
                        ins = pe.matmul(main[:, bank, half * HALF:(half + 1) * HALF], w[:, slot, k, :],
                                        x[:, half * HALF:(half + 1) * HALF], start=begin, stop=end)
                return ins

            def squares_summed(acc_made, nth, s_out, half):
                pe.wait_ge(acc_made, KT + half)
                cols = slice(half * HALF, (half + 1) * HALF)
                pe.matmul(sm[:, half, :], ones, acc2[:, cols], start=True, stop=False)
                pe.wait_ge(sq_last, 2 * nth + half + 1)
                pe.matmul(sm[:, half, :], ones, sq2[:, cols], start=False, stop=True).then_inc(s_out, 1)

            def context_product(m, w_h, w_l, rows):
                for k in range(KT):
                    for w, x, begin, end in ((w_h, c_hi, k == 0, False), (w_h, c_lo, False, False),
                                             (w_l, c_hi, False, k == KT - 1)):
                        ins = pe.matmul(ob[0:rows, (m % 2) * HALF:(m % 2) * HALF + NC], w(k), x[:, k, :],
                                        start=begin, stop=end)
                return ins

            def modulation_rows(j):
                s = S_OF[("rows", j)]
                if s >= 2:
                    pe.wait_ge(*small_freed(s - 2))
                pe.wait_ge(wmod_loaded[j], 16)
                for k in range(KT):
                    ins = pe.matmul(sm[0:2, s % 2, :], silu_c[:, 2 * k:2 * k + 2], wmod[:, j, k, :],
                                    start=(k == 0), stop=(k == KT - 1))
                ins.then_inc(small_done, 1)

            def modulation_turned(j):
                s = S_OF[("turn", j)]
                if s >= 2:
                    pe.wait_ge(*small_freed(s - 2))
                pe.wait_ge(*small_freed(S_OF[("rows", j)]))
                for q in range(4):
                    ins = pe.transpose(sm[:, s % 2, 2 * q:2 * q + 2], mrow[:, j % 2, q * P:(q + 1) * P], ident[0:2, 0:2])
                ins.then_inc(small_done, 1)

            pe.wait_ge(c_ready, 1)
            pe.wait_ge(small_in_done, 16)
            modulation_rows(0)
            modulation_turned(0)
            modulation_rows(1)
            for squares, ready, n in ((acc1, acc1_made, KT - 1), (sq1[:, (KT - 1) % 2, :], sq1_made, KT)):
                pe.wait_ge(ready, n)
                for half in range(2):
                    pe.matmul(main[:, 1, half * HALF:(half + 1) * HALF], ones, squares[:, half * HALF:(half + 1) * HALF],
                              start=(n < KT), stop=(n == KT))
                ins = pe.matmul(ob[:, HALF:HALF + NC], ones, squares[:, N:NA], start=(n < KT), stop=(n == KT))
            ins.then_inc(sums1_done, 1)
            modulation_turned(1)

            def begin_small(job):
                s = S_OF[job]
                pe.wait_ge(*small_freed(s - 2))
                return s % 2

            def v_to_tokens(h, i):
                b = begin_small(("vt", h, i))
                m = M_OF[f"V{h}"]
                pe.wait_ge(*main_freed(m))
                pe.wait_ge(*ctx_freed(m))
                for q in range(4 if i < 2 else 2):
                    ins = pe.transpose(sm[:, b, q * P:(q + 1) * P], vtmp[:, (4 * i + q) * P:(4 * i + q + 1) * P], ident)
                ins.then_inc(small_done, 1)

            def k_to_tokens(h, i):
                b = begin_small(("kt", h, i))
                pe.wait_ge(*main_freed(M_OF[f"K{h // 2}"]))
                for q in range(4):
                    ins = pe.transpose(sm[:, b, q * P:(q + 1) * P], ku[:, h, (4 * i + q) * P:(4 * i + q + 1) * P], ident)
                ins.then_inc(small_done, 1)

            def kc_to_tokens(p):
                b = begin_small(("kc", p))
                pe.wait_ge(*ctx_freed(M_OF[f"K{p}"]))
                for hh in range(2):
                    for q in range(2):
                        ins = pe.transpose(sm[:, b, (2 * hh + q) * P:(2 * hh + q + 1) * P],
                                           kuc[:, 2 * p + hh, q * P:(q + 1) * P], ident)
                ins.then_inc(small_done, 1)

            def context_state(p):
                b = begin_small(("cs", p))
                pe.wait_ge(*small_freed(S_OF[("kc", p)]))
                pe.wait_ge(*small_freed(S_OF[("vt", 3, 2)]))
                for hh in range(2):
                    h = 2 * p + hh
                    for q, v in enumerate((vct0, vct1)):
                        ins = pe.matmul(sm[:, b, hh * DV:(hh + 1) * DV], kctok[:, h, q, :], v[:, h * DV:(h + 1) * DV],
                                        start=(q == 0), stop=(q == 1))
                ins.then_inc(small_done, 1)

            def updates(h, n):
                b = begin_small(("u", h, n))
                for i in range(2):
                    pe.wait_ge(*small_freed(S_OF[("kt", h, i)]))
                    pe.wait_ge(*small_freed(S_OF[("vt", 3, i)]))
                rows = slice((n % 2) * CH, (n % 2 + 1) * CH)
                for q, c in enumerate(chunks_of(n)):
                    ins = pe.matmul(sm[:, b, q * DV:(q + 1) * DV], ktok[rows, h % 2, c // 2, :],
                                    vtok[rows, c // 2, h * DV:(h + 1) * DV], start=True, stop=True)
                ins.then_inc(small_done, 1)

            def scores(h, i, d):
                b = begin_small(("A", h, i, d))
                rows = slice(d * DK, (d + 1) * DK)
                pe.wait_ge(*main_freed(M_OF[f"Q{h // 2}"]))
                for q in range(4):
                    t = slice((4 * i + q) * P, (4 * i + q + 1) * P)
                    ins = pe.matmul(sm[:, b, q * P:(q + 1) * P], ku[rows, h, t], qe[rows, h, t], start=True, stop=True)
                ins.then_inc(small_done, 1)

            def outputs(h, i):
                pe.wait_ge(states_decayed, 2 * h + i + 1)
                pe.wait_ge(a_ready, 2 * h + i + 1)
                if i == 0:
                    if h == 0:
                        pe.wait_ge(*ctx_freed(M_OF["K1"]))
                        pe.wait_ge(*ctx_freed(M_OF["K0"]))
                    else:
                        pe.wait_ge(y_normed, h)
                for q in range(4):
                    t = 4 * i + q
                    pe.matmul(ob[:, t * P:(t + 1) * P], vtok[:, t, h * DV:(h + 1) * DV], a_sum[:, q, :],
                              start=(q == 0), stop=False, skip_group_check=True)
                    for n in (2 * t, 2 * t + 1):
                        ins = pe.matmul(ob[:, n * CH:(n + 1) * CH], tst[:, h % 2, n, :], qe[:, h, n * CH:(n + 1) * CH],
                                        start=False, stop=(q == 3 and n % 2 == 1), skip_group_check=True)
                ins.then_inc(o_done, 1)

            def head_sums(h, i):
                b = begin_small(("ns", h, i))
                pe.wait_ge(sqo_made, h + 1)
                pe.matmul(sm[:, b, :], ones, sqo[:, i * HALF:(i + 1) * HALF], start=True, stop=True).then_inc(small_done, 1)

            def pool_product(i, half):
                b = begin_small(("pl", i, half))
                pe.wait_ge(pooled, i + 1)
                pe.wait_ge(masks_loaded, 16)
                a = COLS["pw"][0] + i * P
                pe.matmul(sm[:, b, :], small[:, a:a + P], ypool[:, i, half * HALF:(half + 1) * HALF],
                          start=True, stop=True).then_inc(small_done, 1)

            def mod_product(g):
                b = begin_small(("md", g))
                pe.wait_ge(mod_taken, KT * (g + 1))
                for j in range(KT):
                    ins = pe.matmul(sm[:, b, j:j + 1], macc[:, j * P:(j + 1) * P], ones[:, 0:1], start=True, stop=True)
                ins.then_inc(small_done, 1)

            jobs = {"vt": v_to_tokens, "kt": k_to_tokens, "kc": kc_to_tokens, "cs": context_state, "u": updates,
                    "A": scores, "O": outputs, "ns": head_sums, "pl": pool_product, "md": mod_product}

            def gate_products(j):
                m = M_OF[f"g{j}"]
                pe.wait_ge(*main_freed(m - 2))
                pe.wait_ge(*ctx_freed(m - 2))
                if j == 0:
                    pe.wait_ge(*main_freed(M_OF["G"]))
                    pe.wait_ge(*ctx_freed(M_OF["G"]))
                    pe.wait_ge(z_copied, 2)
                    pe.wait_ge(gw_split, 1)
                pe.matmul(ob[:, (m % 2) * HALF:(m % 2) * HALF + NC], gw_parts[:, j, :], zsb[:, N:NA], start=True, stop=True)
                for half in range(2):
                    ins = pe.matmul(main[:, m % 2, half * HALF:(half + 1) * HALF], gw_parts[:, j, :],
                                    zsb[:, half * HALF:(half + 1) * HALF], start=True, stop=True)
                ins.then_inc(tile_done, 1)

            def first_products(k):
                pe.wait_ge(h1_lo, k + 1)
                begin, end = k == 0, k == KT - 1

                def both(m, rows, w, x, c, b, e):
                    for half in range(2):
                        pe.matmul(main[rows, m, half * HALF:(half + 1) * HALF], w,
                                  x[:, k, half * HALF:(half + 1) * HALF], start=b, stop=e)
                    return pe.matmul(ob[rows, m * HALF:m * HALF + NC], w, c[:, k, :], start=b, stop=e)

                steps = [lambda: both(0, slice(0, 4 * RANK), wg_parts[:, k, :], a_hi, c_hi, begin, end),
                         lambda: both(0, slice(0, 2 * RANK), wg_parts[:, k, 0:2 * RANK], a_lo, c_lo, False, False)]
                for step in reversed(steps) if end else steps:
                    ins = step()
                if end:
                    ins.then_inc(tile_done, 1)
                for w, x, c, b, e in ((w_hi, a_hi, c_hi, begin, False), (w_hi, a_lo, c_lo, False, False),
                                      (w_lo, a_hi, c_hi, False, end)):
                    ins = both(1, slice(0, P), w[:, 0, k, :], x, c, b, e)
                if end:
                    ins.then_inc(tile_done, 1)

            modulation_rows(2)
            pe.wait_ge(wg_split, 1)
            pe.wait_ge(split_done, 1)
            first_products(0)
            modulation_turned(2)
            modulation_rows(3)
            first_products(1)
            first_products(2)
            modulation_turned(3)
            for k in range(3, KT):
                first_products(k)
            gate_products(0)

            for t, name in enumerate(PROJ[1:], 1):
                m = M_OF[name]
                pe.wait_ge(split_done, t + 1)
                if m <= M_OF["K1"]:
                    pe.wait_ge(*ctx_freed(m - 2))
                    context_product(m, lambda k: w_hi[:, t % 2, k, :], lambda k: w_lo[:, t % 2, k, :], P)
                pe.wait_ge(*main_freed(m - 2))

                def small_jobs(k, t=t):
                    for job in PLAN.get((t, k), ()):
                        if job[0] in jobs:
                            jobs[job[0]](*job[1:])

                product(m % 2, t % 2, of_a, after=small_jobs)
                small_jobs(KT - 1)
                if name in ("V1", "V2", "V3"):
                    gate_products(int(name[1]))

            def out_pair(m_free, t_ready, first):
                for b in range(2):
                    pe.wait_ge(split_done, t_ready + b)
                    pe.wait_ge(main_free[1 - b], m_free + b)

                    def mixed(n, k):
                        pe.wait_ge(lo_made, n + 1)

                    product(1 - b, b, mix_parts, order=MIX_ORDER, ready=mixed if first and b == 0 else None)

            out_pair((M_OUT - 2) // 2 + 1, T_OUT + 1, True)
            with pe.Fori(1, KT // 2 - 1) as i:
                out_pair(i + ((M_OUT - 2) // 2 + 1), i * 2 + (T_OUT + 1), False)

            def last_pair(m_free, t_ready, acc_made, nth, s_out, parts, order=range(KT)):
                for b in range(2):
                    pe.wait_ge(split_done, t_ready + b)
                    pe.wait_ge(main_free[1 - b], m_free + b)
                    half_product(1 - b, b, parts, 0, order).then_inc(half_done, 1)
                half_product(1, 0, parts, 1, order,
                             within=lambda: squares_summed(acc_made, nth, s_out, 0)).then_inc(tile_done, 1)
                half_product(0, 1, parts, 1, order).then_inc(tile_done, 1)

            last_pair(KT // 2 - 1 + (M_OUT - 2) // 2 + 1, T_OUT + KT - 1, acc2_made, 0, sums2_done, mix_parts, MIX_ORDER)

            def mlp_pair(parts, m_free, t_ready, ready=None):
                for b in range(2):
                    pe.wait_ge(split_done, t_ready + b)
                    pe.wait_ge(main_free[1 - b], m_free + b)
                    product(1 - b, b, parts, ready=ready if b == 0 else None)

            free0, ready0 = (M_MLP - 2) // 2 + 1, T_MLP + 1

            def normed(half, n):
                pe.wait_ge(lo_made, LO_H2 + half * KT + n + 1)

            for b in range(2):
                pe.wait_ge(split_done, ready0 + b)
                pe.wait_ge(main_free[1 - b], free0 + b)
                half_product(1 - b, b, of_h, 0, H_ORDER, normed, None if b else
                             lambda: squares_summed(acc2_made, 0, sums2_done, 1))
            for b in range(2):
                half_product(1 - b, b, of_h, 1, H_ORDER, normed).then_inc(tile_done, 1)
            with pe.Fori(1, KT // 2) as i:
                mlp_pair(of_h, i + free0, i * 2 + ready0)

            def second(base, pairs=KT // 2):
                def squared(n, k):
                    pe.wait_ge(lo_made, base + (LO_HID + n + 1 - KT // 2))

                mlp_pair(of_a, base + free0, base * 2 + ready0, squared)
                with pe.Fori(1, pairs) as i:
                    mlp_pair(of_a, i + base + free0, i * 2 + (base * 2 + ready0))

            second(KT // 2)
            with pe.Fori(1, NFC - 1) as c:
                with pe.Fori(0, KT // 2) as i:
                    mlp_pair(of_h, i + c * KT + free0, i * 2 + (c * (2 * KT) + ready0))
                second(c * KT + KT // 2)
            base = (NFC - 1) * KT
            with pe.Fori(0, KT // 2) as i:
                mlp_pair(of_h, i + (base + free0), i * 2 + (2 * base + ready0))
            second(base + KT // 2, KT // 2 - 1)
            last_pair(base + KT - 1 + free0, 2 * (base + KT - 1) + ready0, acc3_made, 1, sums3_done, of_a)
            squares_summed(acc3_made, 1, sums3_done, 1)

        @block.scalar
        def _(act):
            act.preload_act_table_set("natural_log_exp_and_others")
            link = chain(act, act_chain)

            def rsqrt(dst, src, width, s_out, free=None):
                ins = act.activation(dst, src, ACT.Ln, bias=col("eps"), scale=1.0 / width)
                if free is None:
                    link(ins)
                else:
                    ins.then_inc(free[0], 1)
                    act.wait_ge(*free)
                ins = act.activation(dst, dst, ACT.Exp, scale=-0.5)
                return ins if s_out is None else ins.then_inc(s_out, 1)

            act.wait_ge(small_in_done, 16)
            act.activation(csig[:, :], col("cc"), ACT.Exp, scale=-1.0).then_inc(c_exp, 1)
            act.wait_ge(ctx_loaded, 16)
            def copy_rows(j):
                s = S_OF[("rows", j)]
                act.wait_ge(small_done, s + 1)
                if j >= 2:
                    act.wait_ge(small_done, S_OF[("turn", j - 2)] + 1)
                act.activation(mrow[:, j % 2, :], sm[0:2, s % 2, :], ACT.Copy).then_inc(small_free[s % 2], 1)

            for k in range(KT):
                act.wait_ge(x_loaded[k], 16)
                if k >= 2:
                    act.wait_ge(acc1_made, k - 1)
                act.activation(sq1[:, k % 2, :], xs[:, k, :], ACT.Square).then_inc(sq1_made, 1)
                if k == 2:
                    copy_rows(0)
            copy_rows(1)
            act.wait_ge(sums1_done, 1)
            rsqrt(rs1[:, 0:N], main[:, 1, :], D, None)
            rsqrt(rs1[:, N:NA], ob[:, HALF:HALF + NC], D, rs1_made)
            for k in range(KT):
                act.wait_ge(h1_made, k + 1)
                act.activation(a_hi[:, k, :], xs[:, k, 0:N], ACT.Copy)
                act.activation(c_hi[:, k, :], xs[:, k, N:NA], ACT.Copy).then_inc(h1_hi, 1)
                if k in (0, 2):
                    copy_rows(2 + k // 2)
                if k == 4:
                    act.wait_ge(gw_loaded, 16)
                    act.activation(gw_parts[0:64, :, :], gw[0:64, :, :], ACT.Copy)
                    act.activation(gw_parts[96:128, :, :], gw[96:128, :, :], ACT.Copy)
                    act.activation(gw_hi[64:96, :, :], gw[64:96, :, :], ACT.Copy).then_inc(gw_rounded, 1)

            def v_to_tokens(h, i):
                s = S_OF[("vt", h, i)]
                act.wait_ge(small_done, s + 1)
                if i < 2:
                    act.activation(vtok[:, 4 * i:4 * i + 4, h * DV:(h + 1) * DV],
                                   sm[:, s % 2, :].rearrange("p (t e) -> p t e", t=4), ACT.Copy).then_inc(small_free[s % 2], 1)
                else:
                    act.activation(vct0[:, h * DV:(h + 1) * DV], sm[:, s % 2, 0:DV], ACT.Copy)
                    act.activation(vct1[:, h * DV:(h + 1) * DV], sm[:, s % 2, DV:2 * DV], ACT.Copy).then_inc(small_free[s % 2], 1)

            def k_to_tokens(h, i):
                s = S_OF[("kt", h, i)]
                act.wait_ge(small_done, s + 1)
                act.activation(ktok[:, h % 2, 4 * i:4 * i + 4, :], sm[:, s % 2, :].rearrange("p (t e) -> p t e", t=4),
                               ACT.Copy).then_inc(small_free[s % 2], 1)

            def kc_to_tokens(p):
                s = S_OF[("kc", p)]
                act.wait_ge(small_done, s + 1)
                act.activation(kctok[:, 2 * p:2 * p + 2, :, :], sm[:, s % 2, :].rearrange("p (h q e) -> p h q e", h=2, q=2),
                               ACT.Copy).then_inc(small_free[s % 2], 1)

            def updates(h, n):
                s = S_OF[("u", h, n)]
                if n == 0:
                    act.wait_ge(*small_freed(S_OF[("cs", h // 2)]))
                    if h >= 2:
                        act.wait_ge(o_done, 2 * (h - 1))
                    act.activation(tst[0:DK, h % 2, 0, :], state[0:DK, h, :], ACT.Copy)
                    act.activation(tst[DK:P, h % 2, NCH - 1, :], state[DK:P, h, :], ACT.Copy)
                act.wait_ge(small_done, s + 1)
                src = sm[:, s % 2, :].rearrange("p (q e) -> p q e", q=4)
                c = chunks_of(n)
                a, b = (0, 3) if c[-1] == NCH - 1 else (0, 4)
                act.activation(tst[0:DK, h % 2, c[a] + 1:c[b - 1] + 2:2, :], src[0:DK, a:b], ACT.Copy)
                a, b = (1, 4) if c[0] == 0 else (0, 4)
                act.activation(tst[DK:P, h % 2, c[a] - 1:c[b - 1]:2, :], src[DK:P, a:b], ACT.Copy).then_inc(small_free[s % 2], 1)

            def decay_states(h, i):
                act.wait_ge(states_made, 2 * (NCH - 1) * (h + 1))
                for n in range(8 * i, 8 * i + 8):
                    ins = act.activation(tst[:, h % 2, n, :], tst[:, h % 2, n, :], ACT.Copy, scale=decay[:, h, n:n + 1])
                ins.then_inc(states_decayed, 1)

            def outputs(h, i):
                if i == 1:
                    act.wait_ge(o_done, 2 * (h + 1))
                    act.wait_ge(summed, 2)
                    if h >= 1:
                        act.wait_ge(y_normed, h)
                    act.activation(sqo[:, :], ob[:, :], ACT.Square).then_inc(sqo_made, 1)

            def head_sums(h, i):
                s = S_OF[("ns", h, i)]
                act.wait_ge(small_done, s + 1)
                half = slice(i * HALF, (i + 1) * HALF)
                rsqrt(rso[:, half], sm[:, s % 2, :], DV, rso_made, small_freed(s))

            def pool_product(i, half):
                s = S_OF[("pl", i, half)]
                act.wait_ge(small_done, s + 1)
                act.activation(ypool[:, i, half * HALF:(half + 1) * HALF], sm[:, s % 2, :], ACT.Copy,
                               scale=one_col("ps", i)).then_inc(small_free[s % 2], 1)

            jobs = {"vt": v_to_tokens, "kt": k_to_tokens, "kc": kc_to_tokens, "u": updates, "mx": decay_states, "O": outputs,
                    "ns": head_sums, "pl": pool_product}

            def after_g():
                act.wait_ge(tile_done, 1)
                act.wait_ge(h1_made, KT)
                act.activation(zsb[0:32, 0:N], main[0:32, 0, :], ACT.Copy)
                act.activation(zsb[0:32, N:NA], ob[0:32, 0:NC], ACT.Copy).then_inc(z_copied, 1)

            def after_v(h, m):
                if h >= 1:
                    act.wait_ge(small_done, S_OF[("vt", h - 1, 2)] + 1)
                act.activation(vtmp[:, N:NA], ob[:, (m % 2) * HALF:(m % 2) * HALF + NC], ACT.Copy).then_inc(ctx_free[m % 2], 1)
                if h == 0:
                    act.wait_ge(z_copied, 1)
                    act.activation(zsb[64:96, :], zsb[0:32, :].bitcast(F32), ACT.Copy).then_inc(z_copied, 1)
                act.activation(vtmp[:, 0:N], main[:, m % 2, :], ACT.Copy).then_inc(main_free[m % 2], 1)

            def gates(j):
                m = M_OF[f"g{j}"]
                act.wait_ge(gate_min, j + 1)
                act.activation(t2[:, 0:N], main[:, m % 2, :], ACT.Abs, bias=one_col("gb", j)).then_inc(main_free[m % 2], 1)
                act.activation(t2[:, N:NA], ob[:, (m % 2) * HALF:(m % 2) * HALF + NC], ACT.Abs,
                               bias=one_col("gb", j)).then_inc(ctx_free[m % 2], 1)
                act.wait_ge(*main_freed(m))
                act.wait_ge(*ctx_freed(m))
                link(act.activation(t2[:, :], t2[:, :], ACT.Exp, scale=-1.0))
                act.activation(t2[:, :], t2[:, :], ACT.Ln, bias=col("one")).then_inc(gate_log, 1)

            def decays(j):
                act.wait_ge(gate_dif, j + 1)
                act.activation(decay[:, j, :], t2[:, CH - 1:N:CH], ACT.Exp, scale=1.0 / TAU)
                link(act.activation(qe[:, j, :], ku[:, j, :], ACT.Exp, scale=-1.0 / TAU))
                act.activation(ku[:, j, :], ku[:, j, :], ACT.Exp, scale=1.0 / TAU)
                act.activation(kuc[:, j, :], kuc[:, j, :], ACT.Exp, scale=1.0 / TAU).then_inc(gate_exp, 1)

            def after_p(i, m):
                act.wait_ge(pads_made, 1)
                if i == 1:
                    act.wait_ge(pooled, 1)
                act.activation(upad[:, :, 9:9 + SEG], main[:, m % 2, :].rearrange("p (s t) -> p s t", t=SEG),
                               ACT.Copy).then_inc(main_free[m % 2], 1)

            def after_cc(i, m):
                act.wait_ge(pads_made, 2)
                if i == 1:
                    act.wait_ge(*main_freed(M_OF["CB0"]))
                act.activation(zpad[:, :, 1:1 + SEG], main[:, m % 2, :].rearrange("p (s t) -> p s t", t=SEG),
                               ACT.Copy).then_inc(main_free[m % 2], 1)

            def after_r(h, m):
                act.wait_ge(pads_made, 2)
                if h >= 1:
                    act.wait_ge(y_gated, h)
                link(act.activation(rsig[:, :], main[:, m % 2, :], ACT.Abs))
                link(act.activation(rsig[:, :], rsig[:, :], ACT.Exp, scale=-1.0))
                act.activation(rsig[:, :], rsig[:, :], ACT.Ln, bias=col("one")).then_inc(r_log, 1)

            def sigmoid(h):
                act.wait_ge(r_min, h + 1)
                act.activation(rsig[:, :], rsig[:, :], ACT.Exp).then_inc(r_sig, 1)

            jobs["rl"] = sigmoid
            after_g()
            for t, name in enumerate(PROJ):
                for k in range(KT):
                    for job in PLAN.get((t, k), ()):
                        if job[0] in jobs:
                            jobs[job[0]](*job[1:])
                        if job == ("vt", HEADS - 1, 0):
                            decays(HEADS - 1)
                m, i = M_OF[name], int(name[-1])
                if name[:-1] in ("V", "P", "CC", "R"):
                    act.wait_ge(tile_done, m + 1)
                    {"V": after_v, "P": after_p, "CC": after_cc, "R": after_r}[name[:-1]](i, m)
                if name[:-1] == "V":
                    if i >= 1:
                        decays(i - 1)
                    gates(i)

            for n, k in enumerate(MIX_ORDER):
                if n == 0:
                    act.wait_ge(o_done, 2 * HEADS)
                if n == 2:
                    act.wait_ge(tile_done, M_OUT)
                if k < 4:
                    act.wait_ge(y_gated, k + 1)
                elif k < 6:
                    act.wait_ge(*main_freed(M_OF[f"CB{k - 4}"]))
                src, shape = mix_block(k)
                act.activation(shape(mix_parts(k)[0]), src, ACT.Copy).then_inc(mix_hi, 1)

            def residual_squares(m0, acc_made, sq_made, nth, sums_done, rs_made, between, after):
                def square(i, b):
                    act.wait_ge(main_free[1 - b], i + ((m0 + b) // 2 + 1))
                    act.wait_ge(acc_made, i * 2 + (b + 1))
                    xk = X[:, bass.ds(i * 2 + b, 1), :]
                    act.activation(sq2[:, :].unsqueeze(1), xk, ACT.Square).then_inc(sq_made, 1)
                    if nth == 0:
                        act.activation(xg[:, bass.ds(i * 2 + b, 1), :], xk, ACT.Copy,
                                       scale=gain2[:, bass.ds(i * 2 + b, 1)]).then_inc(xg_made, 1)

                with act.Fori(0, KT // 2 - 1) as i:
                    for b in range(2):
                        square(i, b)
                def square_half(k, half, s_out):
                    cols = slice(half * HALF, (half + 1) * HALF)
                    act.activation(sq2[:, cols], X[:, k, cols], ACT.Square).then_inc(s_out, 1)

                def scale_half(k, half):
                    if nth == 0:
                        cols = slice(half * HALF, (half + 1) * HALF)
                        act.activation(xg[:, k, cols], X[:, k, cols], ACT.Copy, scale=gain2[:, k:k + 1]).then_inc(xg_made, 1)

                act.wait_ge(acc_made, KT - 1)
                act.wait_ge(res_half, 2 * nth + 1)
                square_half(KT - 2, 0, sq_made)
                scale_half(KT - 2, 0)
                act.wait_ge(acc_made, KT)
                act.wait_ge(res_half, 2 * nth + 2)
                square_half(KT - 1, 0, sq_last)
                scale_half(KT - 1, 0)
                act.wait_ge(sums_done, 1)
                rsqrt(rs2[:, 0:HALF], sm[:, 0, :], D, rs_made)
                act.wait_ge(main_free[1], (m0 + KT - 2) // 2 + 1)
                square_half(KT - 2, 1, sq_made)
                scale_half(KT - 2, 1)
                between()
                act.wait_ge(acc_made, KT + 1)
                act.wait_ge(main_free[0], (m0 + KT - 1) // 2 + 1)
                square_half(KT - 1, 1, sq_last)
                after()
                scale_half(KT - 1, 1)
                act.wait_ge(sums_done, 2)
                rsqrt(rs2[:, HALF:N], sm[:, 1, :], D, rs_made)

            def high(half, k):
                if k in H2_POOL[half]:
                    act.wait_ge(h2_scaled_pool, half * len(H2_POOL[0]) + H2_POOL[half].index(k) + 1)
                else:
                    act.wait_ge(h2_scaled, half * len(H2_DVE[0]) + H2_DVE[half].index(k) + 1)
                cols = slice(half * HALF, (half + 1) * HALF)
                act.activation(h_hi[:, k, cols], xg[:, k, cols], ACT.Identity, bias=mods[:, 1, k:k + 1]).then_inc(hid_hi, 1)

            def early_highs():
                for k in H_ORDER[:4]:
                    high(0, k)
                act.wait_ge(tile_done, M_OUT + KT)
                high(0, H_ORDER[4])

            def late_highs():
                for k in H_ORDER[5:]:
                    high(0, k)

            residual_squares(M_OUT, acc2_made, sq2_made, 0, sums2_done, rs2_made, early_highs, late_highs)
            for k in H_ORDER:
                high(1, k)

            def hidden(c):
                with act.Fori(0, KT // 2) as j:
                    for b in range(2):
                        act.wait_ge(tile_done, j * 2 + (c * (2 * KT) + (M_MLP + b + 1)))
                        act.wait_ge(lo_made, j * 2 + (c * KT + (LO_HID + b - 1)))
                        act.activation(relu[:, b:b + 1, :], main[:, 1 - b:2 - b, :], ACT.Relu).then_inc(main_free[1 - b], 1)
                        act.wait_ge(main_free[1 - b], j + (c * KT + ((M_MLP + b) // 2 + 1)))
                        act.activation(a_hi[:, bass.ds(j * 2 + b, 1), :], relu[:, b:b + 1, :], ACT.Square).then_inc(hid_hi, 1)

            with act.Fori(0, NFC - 1) as c:
                hidden(c)
            hidden(NFC - 1)

            act.wait_ge(lo_made, LO_HID + NFC * KT)
            def scale_out(half):
                cols = slice(half * HALF, (half + 1) * HALF)
                for k in range(OUT_DVE, KT):
                    act.wait_ge(out_scaled, half * (KT - OUT_DVE) + k - OUT_DVE + 1)
                    act.activation(X[:, k, cols], X[:, k, cols], ACT.Copy, scale=one_col("fw", k)).then_inc(out_made_act, 1)

            residual_squares(M_MLP + (2 * NFC - 1) * KT, acc3_made, sq3_made, 1, sums3_done, rs3_made,
                             lambda: scale_out(0), lambda: None)
            scale_out(1)

        @block.vector
        def _(dve):
            link = chain(dve, dve_chain)
            tt, ts, stt = dve.tensor_tensor, dve.tensor_scalar, dve.scalar_tensor_tensor

            dve.wait_ge(c_exp, 1)
            link(ts(csig[:, :], csig[:, :], 1.0, None, ALU.add))
            link(dve.reciprocal(csig[:, :], csig[:, :]))
            tt(silu_c[:, :], csig[:, :], col("cc"), ALU.mult).then_inc(c_ready, 1)

            def modulation(j):
                s = S_OF[("turn", j)]
                dve.wait_ge(small_done, s + 1)
                for q in range(2):
                    i = 2 * j + q
                    ts(ab1[:, i, 0:2], sm[:, s % 2, 4 * q:4 * q + 2], one_col("bmod", i), None, ALU.add)
                    ins = ts(ab1[:, i, 2:4], sm[:, s % 2, 4 * q + 2:4 * q + 4], one_col("bmod", KT + i), 1.0, ALU.add, ALU.add)
                ins.then_inc(small_free[s % 2], 1)
                dve.wait_ge(*small_freed(s))
                ts(ab1[:, 2 * j, 2:4], ab1[:, 2 * j, 2:4], one_col("n1", 2 * j), None, ALU.mult)
                link(ts(ab1[:, 2 * j + 1, 2:4], ab1[:, 2 * j + 1, 2:4], one_col("n1", 2 * j + 1), None, ALU.mult))

            for k in range(KT - 1):
                dve.wait_ge(sq1_made, k + 1)
                if k == 0:
                    ins = dve.tensor_copy(acc1[:, :], sq1[:, 0, :])
                else:
                    ins = tt(acc1[:, :], acc1[:, :], sq1[:, k % 2, :], ALU.add)
                ins.then_inc(acc1_made, 1)
                dve.wait_ge(acc1_made, k + 1)
                if k == 3:
                    modulation(0)
            def low1(k):
                dve.wait_ge(h1_hi, k + 1)
                dve.wait_ge(small_done, S_OF[("rows", 2 + k // 4)] + 1)
                tt(a_lo[:, k, :], xs[:, k, 0:N], a_hi[:, k, :].bitcast(F32), ALU.subtract)
                tt(c_lo[:, k, :], xs[:, k, N:NA], c_hi[:, k, :].bitcast(F32), ALU.subtract).then_inc(h1_lo, 1)

            modulation(1)
            dve.wait_ge(rs1_made, 1)
            last = tt(xs[:, 0, :], xs[:, 0, :], rs1[:, :], ALU.mult)
            for j in range(KT):
                if j < NORM1_DVE:
                    link(last)
                else:
                    dve.wait_ge(x_scaled_pool, j - NORM1_DVE + 1)
                if j in (2, 5):
                    modulation(2 + j // 4)
                ts(xs[:, j, N:NA], xs[:, j, N:NA], ab1[:, j, 3:4], ab1[:, j, 1:2], ALU.mult, ALU.add)
                ts(xs[:, j, 0:N], xs[:, j, 0:N], ab1[:, j, 2:3], ab1[:, j, 0:1], ALU.mult, ALU.add).then_inc(h1_made, 1)
                if j >= 2:
                    low1(j - 1)
                if j < NORM1_DVE - 1:
                    last = tt(xs[:, j + 1, :], xs[:, j + 1, :], rs1[:, :], ALU.mult)
                if j == 0:
                    low1(0)
            dve.wait_ge(gw_rounded, 1)
            tt(gw_parts[64:96, :, :], gw[64:96, :, :], gw_hi[64:96, :, :].bitcast(F32), ALU.subtract).then_inc(gw_split, 1)
            low1(KT - 1)

            dve.wait_ge(tile_done, 1)
            dve.tensor_copy(zsb[96:128, 0:N], main[32:64, 0, :])
            dve.tensor_copy(zsb[96:128, N:NA], ob[32:64, 0:NC])
            dve.wait_ge(z_copied, 1)
            tt(zsb[32:64, 0:N], main[0:32, 0, :], zsb[0:32, 0:N].bitcast(F32), ALU.subtract).then_inc(main_free[0], 1)
            tt(zsb[32:64, N:NA], ob[0:32, 0:NC], zsb[0:32, N:NA].bitcast(F32), ALU.subtract).then_inc(ctx_free[0], 1)

            def context_state(p):
                s = S_OF[("cs", p)]
                dve.wait_ge(small_done, s + 1)
                dve.tensor_copy(state[:, 2 * p:2 * p + 2, :], sm[:, s % 2, 0:2 * DV].rearrange("p (h e) -> p h e", h=2)).then_inc(small_free[s % 2], 1)
                dve.wait_ge(*small_freed(s))

            def chain_states(h, part):
                if part == 0:
                    for i in (2, 3):
                        dve.wait_ge(*small_freed(S_OF[("u", h, i)]))
                steps = (NCH - 1) // 3
                for q in range(steps * part, steps * (part + 1)):
                    for d, (c, step) in enumerate(((q, 1), (NCH - 1 - q, -1))):
                        rows = slice(d * DK, (d + 1) * DK)
                        n = 2 * ((NCH - 1) * h + q) + d + 1
                        if q >= 1:
                            dve.wait_ge(states_made, n - 2)
                        stt(out=tst[rows, h % 2, c + step, :], in0=tst[rows, h % 2, c, :], scalar=decay[rows, h, c:c + 1],
                            in1=tst[rows, h % 2, c + step, :], op0=ALU.mult, op1=ALU.add).then_inc(states_made, 1)

            def scores(h, i, d):
                s = S_OF[("A", h, i, d)]
                dve.wait_ge(small_done, s + 1)
                dve.wait_ge(masks_loaded, 16)
                dst, mask = ((a_f, "maskf"), (a_b, "maskb"))[d]
                dve.copy_predicated(dst[:, :, :], col(mask).bitcast(U32).unsqueeze(1).broadcast_to([P, 4, P]),
                                    sm[:, s % 2, :].rearrange("p (t q) -> p t q", t=4)).then_inc(small_free[s % 2], 1)
                dve.wait_ge(*small_freed(s))
                if d == 1:
                    if 2 * h + i >= 1:
                        dve.wait_ge(o_done, 2 * h + i)
                    tt(a_sum[:, :, :], a_f[:, :, :], a_b[:, :, :], ALU.add).then_inc(a_ready, 1)
                    dve.wait_ge(a_ready, 2 * h + i + 1)

            def head_sums(h, i):
                if i == 1:
                    dve.wait_ge(rso_made, 2 * (h + 1))
                    tt(y_gla(h), by_tile(ob[:, :]), by_tile(rso[:, :]), ALU.mult).then_inc(y_normed, 1)
                    dve.wait_ge(y_normed, h + 1)

            def mod_product(g):
                s = S_OF[("md", g)]
                dve.wait_ge(small_done, s + 1)
                a = COLS["bmod"][0] + (2 + g) * KT
                tt(mods[:, g, :], sm[:, s % 2, 0:KT], small[:, a:a + KT], ALU.add).then_inc(small_free[s % 2], 1)
                dve.wait_ge(*small_freed(s))
                if g == 2:
                    link(stt(out=gain2[:, :], in0=mods[:, 2, :], scalar=1.0, in1=col("n2"), op0=ALU.add, op1=ALU.mult))

            jobs = {"cs": context_state, "ch": chain_states, "A": scores, "ns": head_sums, "md": mod_product}

            def gates(j):
                m = M_OF[f"g{j}"]
                dve.wait_ge(tile_done, m + 1)
                ts(t1[:, 0:N], main[:, m % 2, :], one_col("gb", j), 0.0, ALU.add, ALU.min)
                ts(t1[:, N:NA], ob[:, (m % 2) * HALF:(m % 2) * HALF + NC], one_col("gb", j), 0.0, ALU.add,
                   ALU.min).then_inc(gate_min, 1)
                for n in IN_GATES[j]:
                    add_modulation(n)
                dve.wait_ge(gate_min, j + 1)
                dve.wait_ge(gate_log, j + 1)
                link(tt(t1[:, :], t1[:, :], t2[:, :], ALU.subtract))
                dve.wait_ge(masks_made, 1)
                link(dve.tensor_tensor_scan(out=t2[:, :], data0=gmask[:, :], data1=t1[:, :], initial=0.0,
                                            op0=ALU.mult, op1=ALU.add))
                f, b = slice(0, DK), slice(DK, P)
                chunks = t2[f, 0:N].rearrange("p (n t) -> p n t", t=CH)
                tt(ku[f, j, :].rearrange("p (n t) -> p n t", t=CH), chunks[:, :, CH - 1:CH].broadcast_to([DK, NCH, CH]),
                   chunks, ALU.subtract)
                ts(kuc[f, j, :], t2[f, N:NA], -1.0, t2[f, NA - 1:NA], ALU.mult, ALU.add)
                tt(ku[b, j, :], t2[b, 0:N], t1[b, 0:N], ALU.subtract)
                tt(kuc[b, j, :], t2[b, N:NA], t1[b, N:NA], ALU.subtract).then_inc(gate_dif, 1)
                dve.wait_ge(gate_dif, j + 1)

            def add_modulation(n):
                g, k = n // KT, n % KT
                dve.wait_ge(mbuf_loaded[n % 2], 16 * (n // 2 + 1))
                if k == 0:
                    if g >= 1:
                        dve.wait_ge(small_done, S_OF[("md", g - 1)] + 1)
                    ins = ts(macc[:, :], mbuf[:, n % 2, :], silu_c[:, 2 * k:2 * k + 1], None, ALU.mult)
                else:
                    dve.wait_ge(mod_taken, n)
                    ins = stt(out=macc[:, :], in0=mbuf[:, n % 2, :], scalar=silu_c[:, 2 * k:2 * k + 1],
                              in1=macc[:, :], op0=ALU.mult, op1=ALU.add)
                ins.then_inc(mod_taken, 1)

            def halves(p):
                return [(2 * p + hh, slice(hh * DK, (hh + 1) * DK), slice(d * DK, (d + 1) * DK))
                        for hh in range(2) for d in range(2)]

            def after_k(p, m):
                dve.wait_ge(gate_exp, 2 * p + 2)
                for h, rows, place in halves(p):
                    ins = tt(ku[place, h, :], main[rows, m % 2, :], ku[place, h, :], ALU.mult)
                ins.then_inc(main_free[m % 2], 1)
                for h, rows, place in halves(p):
                    ins = tt(kuc[place, h, :], ob[rows, (m % 2) * HALF:(m % 2) * HALF + NC], kuc[place, h, :], ALU.mult)
                ins.then_inc(ctx_free[m % 2], 1)

            def after_q(p, m):
                for h, rows, place in halves(p):
                    ins = stt(out=qe[place, h, :], in0=main[rows, m % 2, :], scalar=float(DK) ** -0.5,
                              in1=qe[place, h, :], op0=ALU.mult, op1=ALU.mult)
                ins.then_inc(main_free[m % 2], 1)

            def after_p(i, m):
                dve.wait_ge(*main_freed(m))
                dve.wait_ge(masks_made, 2)
                if i == 1:
                    dve.wait_ge(summed, 1)
                link(dve.tensor_tensor_scan(out=cpad[:, :, :].rearrange("p s t -> p (s t)"),
                                            data0=pmask[:, :, :].rearrange("p s t -> p (s t)"),
                                            data1=upad[:, :, :].rearrange("p s t -> p (s t)"), initial=0.0,
                                            op0=ALU.mult, op1=ALU.add))
                y = ypool[:, i, :].rearrange("p (s t) -> p s t", t=SEG)
                for r in range(2):
                    rows, w = slice(64 * r, 64 * r + 64), WINDOWS[2 * i + r]
                    last = tt(y[rows], cpad[rows, :, 8 + w // 2:8 + w // 2 + SEG], cpad[rows, :, 8 - w // 2:8 - w // 2 + SEG],
                              ALU.subtract)
                last.then_inc(summed, 1)

            def after_ch(i, m):
                dve.wait_ge(*main_freed(M_OF[f"CC{i}"]))
                z = zpad[:, :, 1:1 + SEG]
                tt(z, z, main[:, m % 2, :].rearrange("p (s t) -> p s t", t=SEG), ALU.mult).then_inc(main_free[m % 2], 1)
                dve.wait_ge(*main_freed(m))
                y = yconv[:, i, :].rearrange("p (s t) -> p s t", t=SEG)
                link(ts(y, zpad[:, :, 0:SEG], one_col("cw", 3 * i), None, ALU.mult))
                for j in (1, 2):
                    link(stt(out=y, in0=zpad[:, :, j:j + SEG], scalar=one_col("cw", 3 * i + j), in1=y,
                             op0=ALU.mult, op1=ALU.add))

            def after_cb(i, m):
                tt(yconv[:, i, :], main[:, m % 2, :], yconv[:, i, :], ALU.mult).then_inc(main_free[m % 2], 1)

            def log_sigmoid(h):
                m = M_OF[f"R{h}"]
                dve.wait_ge(tile_done, m + 1)
                dve.wait_ge(r_log, h + 1)
                stt(out=rsig[:, :], in0=main[:, m % 2, :], scalar=0.0, in1=rsig[:, :], op0=ALU.min,
                    op1=ALU.subtract).then_inc(r_min, 1)

            def gated(h):
                m = M_OF[f"R{h}"]
                dve.wait_ge(r_sig, h + 1)
                tt(rsig[:, :], main[:, m % 2, :], rsig[:, :], ALU.mult).then_inc(main_free[m % 2], 1)
                dve.wait_ge(*main_freed(m))
                stt(out=y_gla(h), in0=y_gla(h), scalar=col("gnw"), in1=by_tile(rsig[:, :]), op0=ALU.mult,
                    op1=ALU.mult).then_inc(y_gated, 1)

            def low_mix(n):
                dve.wait_ge(mix_hi, n + 1)
                src, shape = mix_block(MIX_ORDER[n])
                hi, lo = mix_parts(MIX_ORDER[n])
                tt(shape(lo), src, shape(hi.bitcast(F32)), ALU.subtract).then_inc(lo_made, 1)

            jobs.update({"rl": log_sigmoid, "rg": gated})
            after = {"K": after_k, "Q": after_q, "P": after_p, "CH": after_ch, "CB": after_cb}
            for t, name in enumerate(PROJ):
                for k in range(KT):
                    for job in PLAN.get((t, k), ()):
                        if job[0] in jobs:
                            jobs[job[0]](*job[1:])
                    if KT * t + k in MOD_SLOT:
                        add_modulation(MOD_SLOT[KT * t + k])
                m, i = M_OF[name], int(name[-1])
                if name == "P0":
                    dve.wait_ge(pads_made, 1)
                if name == "CB1":
                    low_mix(0)
                    low_mix(1)
                if name[:-1] in after:
                    dve.wait_ge(tile_done, m + 1)
                    after[name[:-1]](i, m)
                if name[:-1] == "V":
                    gates(i)

            for n in range(2, KT):
                low_mix(n)

            def residual(m0, g, acc_made, sq_made, nth, between, after):
                dve.memset(acc2[:, :], 0.0).then_inc(acc_made, 1)
                dve.wait_ge(acc_made, 1)

                def add(i, b):
                    dve.wait_ge(tile_done, i * 2 + (m0 + b + 1))
                    xk = X[:, bass.ds(i * 2 + b, 1), :]
                    stt(out=xk, in0=main[:, 1 - b:2 - b, :], scalar=mods[:, g, bass.ds(i * 2 + b, 1)], in1=xk,
                        op0=ALU.mult, op1=ALU.add).then_inc(main_free[1 - b], 1)
                    dve.wait_ge(sq_made, i * 2 + (b + 1))
                    tt(acc2[:, :], acc2[:, :], sq2[:, :], ALU.add).then_inc(acc_made, 1)
                    dve.wait_ge(acc_made, i * 2 + (b + 2))

                with dve.Fori(0, KT // 2 - 1) as i:
                    for b in range(2):
                        add(i, b)
                def add_half(k, half, s_out):
                    cols = slice(half * HALF, (half + 1) * HALF)
                    stt(out=X[:, k, cols], in0=main[:, (k + 1) % 2, cols], scalar=mods[:, g, k:k + 1], in1=X[:, k, cols],
                        op0=ALU.mult, op1=ALU.add).then_inc(s_out, 1)

                def sum_half(half):
                    cols = slice(half * HALF, (half + 1) * HALF)
                    dve.wait_ge(sq_made, KT - 1 + half)
                    tt(acc2[:, cols], acc2[:, cols], sq2[:, cols], ALU.add).then_inc(acc_made, 1)

                dve.wait_ge(half_done, 2 * nth + 1)
                add_half(KT - 2, 0, res_half)
                sum_half(0)
                dve.wait_ge(half_done, 2 * nth + 2)
                add_half(KT - 1, 0, res_half)
                between()
                dve.wait_ge(tile_done, m0 + KT - 1)
                add_half(KT - 2, 1, main_free[1])
                sum_half(1)
                after()
                dve.wait_ge(tile_done, m0 + KT)
                add_half(KT - 1, 1, main_free[0])

            dve.wait_ge(x2_loaded[0], 16)
            dve.wait_ge(x2_loaded[1], 16)

            def scale(half, k):
                cols = slice(half * HALF, (half + 1) * HALF)
                dve.wait_ge(xg_made, xg_count(k, half))
                tt(xg[:, k, cols], xg[:, k, cols], rs2[:, cols], ALU.mult).then_inc(h2_scaled, 1)

            def low(half, n):
                k = H_ORDER[n]
                cols = slice(half * HALF, (half + 1) * HALF)
                dve.wait_ge(hid_hi, half * KT + n + 1)
                stt(out=h_lo[:, k, cols], in0=xg[:, k, cols], scalar=mods[:, 1, k:k + 1],
                    in1=h_hi[:, k, cols].bitcast(F32), op0=ALU.add, op1=ALU.subtract).then_inc(lo_made, 1)

            def first_blocks():
                dve.wait_ge(rs2_made, 1)
                for k in H2_DVE[0][:2]:
                    scale(0, k)

            def next_blocks():
                for n, k in enumerate(H2_DVE[0][2:5]):
                    scale(0, k)
                    low(0, n)
                low(0, 3)

            residual(M_OUT, 0, acc2_made, sq2_made, 0, first_blocks, next_blocks)
            for k in H2_DVE[0][5:]:
                scale(0, k)
            for n in range(4, KT):
                low(0, n)
            dve.wait_ge(rs2_made, 2)
            lows = 0
            for n, k in enumerate(H2_DVE[1]):
                scale(1, k)
                if n >= 1:
                    low(1, lows)
                    lows += 1
            for n in range(lows, KT):
                low(1, n)

            def hidden(c):
                with dve.Fori(0, KT // 2) as j:
                    for b in range(2):
                        dve.wait_ge(hid_hi, j * 2 + (c * KT + (2 * KT + b + 1)))
                        r = relu[:, b:b + 1, :]
                        tt(r, r, r, ALU.mult).then_inc(hid_sq, 1)
                        dve.wait_ge(hid_sq, j * 2 + (c * KT + (b + 1)))
                        tt(a_lo[:, bass.ds(j * 2 + b, 1), :], r, a_hi[:, bass.ds(j * 2 + b, 1), :].bitcast(F32),
                           ALU.subtract).then_inc(lo_made, 1)

            with dve.Fori(0, NFC - 1) as c:
                hidden(c)
                with dve.Fori(0, KT // 2) as j:
                    for b in range(2):
                        dve.wait_ge(tile_done, j * 2 + c * (2 * KT) + (M_MLP + KT + b + 1))
                        xk = X[:, bass.ds(j * 2 + b, 1), :]
                        stt(out=xk, in0=main[:, 1 - b:2 - b, :], scalar=mods[:, 3, bass.ds(j * 2 + b, 1)], in1=xk,
                            op0=ALU.mult, op1=ALU.add).then_inc(main_free[1 - b], 1)
            hidden(NFC - 1)
            dve.wait_ge(lo_made, LO_HID + NFC * KT)
            def scale_out(half):
                cols = slice(half * HALF, (half + 1) * HALF)
                dve.wait_ge(rs3_made, half + 1)
                for k in range(OUT_DVE):
                    stt(out=X[:, k, cols], in0=X[:, k, cols], scalar=one_col("fw", k), in1=rs2[:, cols], op0=ALU.mult,
                        op1=ALU.mult).then_inc(out_made, 1)

            residual(M_MLP + (2 * NFC - 1) * KT, 3, acc3_made, sq3_made, 1, lambda: None, lambda: scale_out(0))
            scale_out(1)


def kernel(**inputs):
    import numpy as np
    from concourse import bacc
    from concourse.bass_utils import run_bass_kernel_spmd

    a = {k: np.asarray(v) for k, v in inputs.items()}

    def tiles(w):
        return w.reshape(KT, P, -1, P).transpose(2, 1, 0, 3).reshape(-1, P, KT * P)

    def by_feature(v):
        return v.reshape(-1, P).T

    w_in = a["w_in"][0]
    at = {}
    g_off = 2 * HEADS * DK + HEADS * DV
    rest = g_off + 2 * RANK
    for name, start in (("Q", 0), ("K", HEADS * DK), ("V", 2 * HEADS * DK), ("R", rest), ("CB", rest + HEADS * DV),
                        ("CC", rest + HEADS * DV + 256), ("CH", rest + HEADS * DV + 512), ("P", rest + HEADS * DV + 768)):
        at[name] = start
    stream = [tiles(w_in[:, at[n[:-1]] + P * int(n[-1]):at[n[:-1]] + P * int(n[-1]) + P]) for n in PROJ]
    stream.append(tiles(a["w_out"][0]))
    for c in range(NFC):
        cols = slice(c * CK, (c + 1) * CK)
        stream.append(tiles(a["w_mlp1"][0][:, cols]))
        stream.append(tiles(a["w_mlp2"][0][cols, :]))

    w_mod = a["w_mod"][0]
    wm1 = w_mod[:, :2 * D].reshape(KT, P, 2, KT // 2, 2, P).transpose(3, 1, 0, 4, 2, 5).reshape(KT // 2, P, 4 * KT * P)
    wm2 = w_mod[:, 2 * D:].reshape(KT, P, 4, D).transpose(2, 0, 1, 3)

    token = np.arange(P)
    same = (token[:, None] // CH) == (token[None, :] // CH)
    t = np.arange(SEG)
    inv = np.zeros((P, 2, SEG), np.float32)
    for g, w in enumerate(WINDOWS):
        count = np.clip(t + w // 2, 0, SEG) - np.clip(t - w // 2, 0, SEG)
        inv[64 * (g % 2):64 * (g % 2) + 64, g // 2] = np.float32(1) / count.astype(np.float32)
    pw = np.zeros((P, 2, P), np.float32)
    for g in range(4):
        r = slice(64 * (g % 2), 64 * (g % 2) + 64)
        pw[r, g // 2, r] = a["pool_w"][0, g]
    parts = {
        "cc": np.stack([by_feature(a["c"][0]), by_feature(a["c_ctx"])], axis=2),
        "bmod": by_feature(a["b_mod"][0]), "n1": by_feature(a["norm1_w"][0]), "n2": by_feature(a["norm2_w"][0]),
        "fw": by_feature(a["final_norm_w"]), "gb": a["gla_gate_b"][0].reshape(2, HEADS, DK).transpose(0, 2, 1).reshape(P, HEADS),
        "gnw": by_feature(a["gla_norm_w"][0]),
        "cw": a["conv_w"][0].reshape(3, 2, P).transpose(2, 1, 0),
        "ps": by_feature(a["pool_scale"][0]),
        "eps": np.full((P, 1), EPS), "one": np.ones((P, 1)), "inv": inv,
        "ident": np.eye(P), "ones": np.ones((P, P)),
        "maskf": same & (token[:, None] <= token[None, :]), "maskb": same & (token[:, None] >= token[None, :]),
        "pw": pw,
    }
    small = np.zeros((P, NSMALL), np.float32)
    for name, (lo, hi) in COLS.items():
        small[:, lo:hi] = np.asarray(parts[name], np.float32).reshape(P, hi - lo)
    gw = np.zeros((2, RANK, HEADS, 2, DK), np.float32)
    for d in range(2):
        gw[d, :, :, d] = a["gla_gate_w"][0, d].reshape(RANK, HEADS, DK)

    arrays = {
        "wstream": np.concatenate(stream), "wg_in": w_in[:, g_off:rest].reshape(KT, P, 32).transpose(1, 0, 2).reshape(P, -1),
        "wm1": wm1, "wm2": wm2, "xt": a["x"][0].T.reshape(KT, P, N),
        "ct": a["ctx"][0].T.reshape(KT, P, NC).transpose(1, 0, 2), "small_in": small, "gw_in": np.concatenate([gw.reshape(2 * RANK, -1)] * 4),
    }
    arrays = {k: np.ascontiguousarray(v) for k, v in arrays.items()}
    nc = bacc.Bacc("TRN2", target_bir_lowering=False, num_devices=1)
    args = [nc.dram_tensor(k, v.shape, mybir.dt.from_np(v.dtype), kind="ExternalInput").ap() for k, v in arrays.items()]
    out = nc.dram_tensor("out", (KT, P, N), F32, kind="ExternalOutput").ap()
    hybrid_trunk(nc, *args, out)
    r = run_bass_kernel_spmd(nc, [arrays], core_ids=[0])
    return r.results[0]["out"].reshape(D, N).T.reshape(1, N, D)
```
